# Optimizing a Trainium2 kernel written in Bass

```python
import jax, jax.numpy as jnp
from jax import lax
import numpy as np
import math

D_MODEL = 1024
BATCH = 1
SEQ = 512
DEPTH = 1

HGRN_EXPAND = 128
HGRN_WIDTH = D_MODEL
HGRN_HEADS = HGRN_WIDTH // HGRN_EXPAND
HGRN_HEAD_V = HGRN_WIDTH // HGRN_HEADS
HGRN_CHUNK = 16
POOL_WINDOWS = (2, 4, 8, 16)
POOL_GROUPS = len(POOL_WINDOWS)
POOL_WIDTH = D_MODEL
POOL_GROUP_DIM = POOL_WIDTH // POOL_GROUPS
D_FF = 4 * D_MODEL
IN_COLS = 4 * HGRN_WIDTH + POOL_WIDTH + 2 * D_MODEL
DEEPNORM_ALPHA = (2.0 * DEPTH) ** 0.25
DEEPNORM_BETA = (8.0 * DEPTH) ** -0.25
LN_EPS = 1e-5
RMS_EPS = 1e-6


def layer_norm(x, g, b):
    xf = x.astype(jnp.float32)
    mu = jnp.mean(xf, axis=-1, keepdims=True)
    var = jnp.mean(jnp.square(xf - mu), axis=-1, keepdims=True)
    y = (xf - mu) * lax.rsqrt(var + LN_EPS)
    return (y * g.astype(jnp.float32) + b.astype(jnp.float32)).astype(x.dtype)

def hgrn2_chunked(q, k, v, log_f):
    B, S, H, dk = q.shape
    dv = v.shape[-1]
    n = S // HGRN_CHUNK

    def to_chunks(t):
        return t.reshape(B, n, HGRN_CHUNK, H, t.shape[-1]).transpose(1, 0, 3, 2, 4)

    q, k, v, log_f = to_chunks(q), to_chunks(k), to_chunks(v), to_chunks(log_f)
    G = jnp.cumsum(log_f, axis=3)
    G_last = G[:, :, :, -1:, :]
    q_dec = q * jnp.exp(G)
    k_inv = k * jnp.exp(-G)
    k_to_end = k * jnp.exp(G_last - G)
    causal = jnp.tril(jnp.ones((HGRN_CHUNK, HGRN_CHUNK), dtype=bool))
    scores = jnp.einsum('nbhtd,nbhsd->nbhts', q_dec, k_inv)
    scores = jnp.where(causal, scores, 0.0)
    o_intra = jnp.einsum('nbhts,nbhsv->nbhtv', scores, v)

    def step(state, xs):
        q_c, k_c, v_c, decay_c = xs
        o_inter = jnp.einsum('bhtd,bhdv->bhtv', q_c, state)
        new_state = jnp.swapaxes(decay_c, -1, -2) * state + jnp.einsum('bhsd,bhsv->bhdv', k_c, v_c)
        return new_state, o_inter

    state0 = jnp.zeros((B, H, dk, dv), jnp.float32)
    _, o_inter = lax.scan(step, state0, (q_dec, k_to_end, v, jnp.exp(G_last)))
    o = o_intra + o_inter
    return o.transpose(1, 0, 3, 2, 4).reshape(B, S, H, dv)

def causal_multiscale_pool(v):
    B, S, _ = v.shape
    vg = v.reshape(B, S, POOL_GROUPS, POOL_GROUP_DIM).astype(jnp.float32)
    csum = jnp.cumsum(vg, axis=1)
    pos = jnp.arange(S)
    outs = []
    for g, w in enumerate(POOL_WINDOWS):
        c = csum[:, :, g]
        lagged = jnp.pad(c, ((0, 0), (w, 0), (0, 0)))[:, :S]
        count = jnp.minimum(pos + 1, w).astype(jnp.float32)[:, None]
        outs.append((c - lagged) / count - vg[:, :, g])
    return jnp.stack(outs, axis=2).astype(v.dtype)

def hybrid_mixer(x, w_in, lower_bound, hgrn_norm_g, w_a, w_pool, pool_scale, w_out):
    B, S, _ = x.shape
    proj = x @ w_in
    hw = HGRN_WIDTH
    splits = [hw, 2 * hw, 3 * hw, 4 * hw, 4 * hw + POOL_WIDTH, 4 * hw + POOL_WIDTH + D_MODEL]
    q, f_pre, i_val, o_gate, pool_v, gate_a, gate_b = jnp.split(proj, splits, axis=-1)

    qf = jax.nn.silu(q.astype(jnp.float32)) * (HGRN_EXPAND ** -0.5)
    lb = lower_bound.astype(jnp.float32)
    f = lb + (1.0 - lb) * jax.nn.sigmoid(f_pre.astype(jnp.float32))
    k = 1.0 - f
    log_f = jnp.log(f)
    shp = (B, S, HGRN_HEADS, HGRN_EXPAND)
    o = hgrn2_chunked(qf.reshape(shp), k.reshape(shp),
                      i_val.astype(jnp.float32).reshape(B, S, HGRN_HEADS, HGRN_HEAD_V), log_f.reshape(shp))
    o = o * lax.rsqrt(jnp.mean(jnp.square(o), axis=-1, keepdims=True) + RMS_EPS)
    o = o.reshape(B, S, hw) * hgrn_norm_g.astype(jnp.float32) * jax.nn.sigmoid(o_gate.astype(jnp.float32))
    a = o.astype(x.dtype) @ w_a

    pooled = causal_multiscale_pool(pool_v)
    b = jnp.einsum('bsgc,gcd->bsgd', pooled, w_pool).reshape(B, S, POOL_WIDTH) * pool_scale

    merged = jax.nn.sigmoid(gate_a) * a + jax.nn.sigmoid(gate_b) * b
    return merged @ w_out

def sq_relu_mlp(x, w_up, w_down):
    return jnp.square(jax.nn.relu(x @ w_up)) @ w_down

def first_inputs(seed: int = 0) -> dict:
    key = jax.random.key(seed)
    ks = jax.random.split(key, 15)
    f32 = jnp.float32
    nrm = lambda k, s: jax.random.normal(k, s, f32)
    return {
        "x": nrm(ks[0], (BATCH, SEQ, D_MODEL)),
        "w_in": nrm(ks[1], (DEPTH, D_MODEL, IN_COLS)) * D_MODEL ** -0.5,
        "lb_logits": nrm(ks[2], (DEPTH + 1, HGRN_WIDTH)) * 0.5,
        "hgrn_norm_g": 1.0 + 0.05 * nrm(ks[3], (DEPTH, HGRN_WIDTH)),
        "w_a": nrm(ks[4], (DEPTH, HGRN_WIDTH, D_MODEL)) * HGRN_WIDTH ** -0.5,
        "w_pool": nrm(ks[5], (DEPTH, POOL_GROUPS, POOL_GROUP_DIM, POOL_GROUP_DIM)) * POOL_GROUP_DIM ** -0.5,
        "pool_scale": 1.0 + 0.05 * nrm(ks[6], (DEPTH, POOL_WIDTH)),
        "w_out": nrm(ks[7], (DEPTH, D_MODEL, D_MODEL)) * (D_MODEL ** -0.5) * DEEPNORM_BETA,
        "ln1_g": 1.0 + 0.05 * nrm(ks[8], (DEPTH, D_MODEL)),
        "ln1_b": 0.02 * nrm(ks[9], (DEPTH, D_MODEL)),
        "w_up": nrm(ks[10], (DEPTH, D_MODEL, D_FF)) * D_MODEL ** -0.5,
        "w_down": nrm(ks[11], (DEPTH, D_FF, D_MODEL)) * (D_FF ** -0.5) * DEEPNORM_BETA,
        "ln2_g": 1.0 + 0.05 * nrm(ks[12], (DEPTH, D_MODEL)),
        "ln2_b": 0.02 * nrm(ks[13], (DEPTH, D_MODEL)),
    }

def first_block(x, w_in, lb_logits, hgrn_norm_g, w_a, w_pool, pool_scale, w_out,
              ln1_g, ln1_b, w_up, w_down, ln2_g, ln2_b):
    lower_bounds = jnp.cumsum(jax.nn.softmax(lb_logits.astype(jnp.float32), axis=0), axis=0)
    for l in range(DEPTH):
        mix = hybrid_mixer(x, w_in[l], lower_bounds[l], hgrn_norm_g[l], w_a[l], w_pool[l],
                           pool_scale[l], w_out[l])
        x = layer_norm(DEEPNORM_ALPHA * x + mix, ln1_g[l], ln1_b[l])
        x = layer_norm(DEEPNORM_ALPHA * x + sq_relu_mlp(x, w_up[l], w_down[l]), ln2_g[l], ln2_b[l])
    return x


DEPTH_2 = 2

HEAD_DIM = 64
FOX_HEADS = 8
RET_HEADS = 8
FOX_WIDTH = FOX_HEADS * HEAD_DIM
RET_WIDTH = RET_HEADS * HEAD_DIM
EVEN_MIX_WIDTH = FOX_WIDTH + RET_WIDTH
FOX_Q_BLOCK = 128
RET_CHUNK = 128
EVEN_SIZES = (FOX_WIDTH, FOX_WIDTH, FOX_WIDTH, FOX_HEADS, RET_WIDTH, RET_WIDTH, RET_WIDTH, EVEN_MIX_WIDTH)
EVEN_IN = sum(EVEN_SIZES)
EVEN_SPLITS = tuple(int(v) for v in np.cumsum(EVEN_SIZES)[:-1])
NSA_HEADS = 16
NSA_KV_GROUPS = 4
NSA_HEADS_PER_GROUP = NSA_HEADS // NSA_KV_GROUPS
NSA_WIDTH = NSA_HEADS * HEAD_DIM
NSA_KV_WIDTH = NSA_KV_GROUPS * HEAD_DIM
N_BRANCH = 3
CMP_BLOCK = 32
CMP_STRIDE = 16
CMP_HIDDEN = 256
SLC_BLOCK = 64
SLC_TOPK = 16
WINDOW = 512
NSA_Q_BLOCK = 64
ODD_SIZES = (NSA_WIDTH,) + (NSA_KV_WIDTH,) * 6 + (NSA_HEADS * N_BRANCH, NSA_WIDTH)
ODD_IN = sum(ODD_SIZES)
ODD_SPLITS = tuple(int(v) for v in np.cumsum(ODD_SIZES)[:-1])

GN_EPS = 1e-5
NEG = -1e30
FORCE_BONUS = 1e6


def rms_norm(x, g):
    xf = x.astype(jnp.float32)
    y = xf * lax.rsqrt(jnp.mean(xf * xf, axis=-1, keepdims=True) + RMS_EPS)
    return (y * g.astype(jnp.float32)).astype(x.dtype)

def masked_softmax(s, mask):
    s = jnp.where(mask, s, NEG)
    p = jax.nn.softmax(s, axis=-1)
    return jnp.where(mask, p, 0.0)

def alibi_slopes(n):
    return jnp.asarray(2.0 ** (-8.0 * (np.arange(n) + 1) / n), jnp.float32)

def fox_attention(q, k, v, f_logit):
    B, S, H, d = q.shape
    nb = S // FOX_Q_BLOCK
    scale = d ** -0.5
    c = jnp.cumsum(jax.nn.log_sigmoid(f_logit.astype(jnp.float32)), axis=1)
    c_h = c.transpose(0, 2, 1)
    kh = k.transpose(0, 2, 1, 3)
    vh = v.transpose(0, 2, 1, 3)
    qb = q.reshape(B, nb, FOX_Q_BLOCK, H, d).transpose(1, 0, 3, 2, 4)
    cb = c.reshape(B, nb, FOX_Q_BLOCK, H).transpose(1, 0, 3, 2)
    key_pos = jnp.arange(S)

    def block(args):
        qi, ci, bi = args
        t = bi * FOX_Q_BLOCK + jnp.arange(FOX_Q_BLOCK)
        s = jnp.einsum('bhqd,bhkd->bhqk', qi, kh).astype(jnp.float32) * scale
        s = s + ci[..., None] - c_h[:, :, None, :]
        p = masked_softmax(s, key_pos[None, :] <= t[:, None])
        return jnp.einsum('bhqk,bhkd->bhqd', p.astype(vh.dtype), vh)

    o = lax.map(block, (qb, cb, jnp.arange(nb)))
    return o.transpose(1, 0, 3, 2, 4).reshape(B, S, H, d)

def retention_decays(n_heads, chunk):
    lg = np.log(1.0 - 2.0 ** (-5.0 - np.arange(n_heads)))
    i = np.arange(chunk)
    diff = i[:, None] - i[None, :]
    inner = np.where(diff[None] >= 0, np.exp(lg[:, None, None] * np.maximum(diff, 0)[None]), 0.0)
    cross = np.exp(lg[:, None] * (i[None, :] + 1))
    kdec = np.exp(lg[:, None] * (chunk - 1 - i)[None, :])
    cdec = np.exp(lg * chunk)
    return (jnp.asarray(inner, jnp.float32), jnp.asarray(cross, jnp.float32),
            jnp.asarray(kdec, jnp.float32), jnp.asarray(cdec, jnp.float32))

def retention(q, k, v):
    B, S, H, d = q.shape
    n = S // RET_CHUNK
    inner, cross, kdec, cdec = retention_decays(H, RET_CHUNK)

    def chunks(a):
        return a.astype(jnp.float32).reshape(B, n, RET_CHUNK, H, d).transpose(1, 0, 3, 2, 4)

    qc, kc, vc = chunks(q), chunks(k) * (d ** -0.5), chunks(v)

    def step(state, xs):
        qi, ki, vi = xs
        a = jnp.einsum('bhid,bhjd->bhij', qi, ki) * inner
        o = jnp.einsum('bhij,bhje->bhie', a, vi) + jnp.einsum('bhid,bhde->bhie', qi, state) * cross[None, :, :, None]
        state = state * cdec[None, :, None, None] + jnp.einsum('bhjd,bhje->bhde', ki * kdec[None, :, :, None], vi)
        return state, o

    _, o = lax.scan(step, jnp.zeros((B, H, d, d), jnp.float32), (qc, kc, vc))
    o = o.transpose(1, 0, 3, 2, 4).reshape(B, S, H, d)
    mu = jnp.mean(o, axis=-1, keepdims=True)
    var = jnp.mean(jnp.square(o - mu), axis=-1, keepdims=True)
    return ((o - mu) * lax.rsqrt(var + GN_EPS)).reshape(B, S, H * d)

def even_layer(x, norm_g, w_in, b_f, gn_g, w_out):
    B, S, _ = x.shape
    h = rms_norm(x, norm_g)
    u = h @ w_in
    q_f, k_f, v_f, f_l, q_r, k_r, v_r, z = jnp.split(u, EVEN_SPLITS, axis=-1)
    hd = lambda a, n: a.reshape(B, S, n, HEAD_DIM)
    o_f = fox_attention(hd(q_f, FOX_HEADS), hd(k_f, FOX_HEADS), hd(v_f, FOX_HEADS), f_l + b_f)
    o_f = o_f.reshape(B, S, FOX_WIDTH)
    o_r = (retention(hd(q_r, RET_HEADS), hd(k_r, RET_HEADS), hd(v_r, RET_HEADS)) * gn_g).astype(x.dtype)
    y = jnp.concatenate([o_f, o_r], axis=-1) * jax.nn.silu(z)
    return x + y @ w_out

def compress_blocks(a, idx, pe, w1, w2):
    B = a.shape[0]
    nc, l = idx.shape
    ab = a[:, idx] + pe[None, None, :, None, :]
    ab = ab.transpose(0, 1, 3, 2, 4).reshape(B, nc, NSA_KV_GROUPS, l * HEAD_DIM)
    return jax.nn.silu(ab @ w1) @ w2

def nsa_attention(q, kc, vc, ks, vs, kw, vw, gate_logit, pe_k, pe_v, wk1, wk2, wv1, wv2):
    B, S, H, d = q.shape
    G, Hg, QB = NSA_KV_GROUPS, NSA_HEADS_PER_GROUP, NSA_Q_BLOCK
    scale = d ** -0.5
    dtype = q.dtype
    nc = (S - CMP_BLOCK) // CMP_STRIDE + 1
    idx = np.arange(nc)[:, None] * CMP_STRIDE + np.arange(CMP_BLOCK)[None, :]
    cmp_end = jnp.asarray(idx[:, -1], jnp.int32)
    k_cmp = compress_blocks(kc, idx, pe_k, wk1, wk2)
    v_cmp = compress_blocks(vc, idx, pe_v, wv1, wv2)
    ns = S // SLC_BLOCK
    topk = min(SLC_TOPK, ns)
    c0 = np.arange(nc)[:, None] * CMP_STRIDE
    s0 = np.arange(ns)[None, :] * SLC_BLOCK
    overlap = np.clip(np.minimum(c0 + CMP_BLOCK, s0 + SLC_BLOCK) - np.maximum(c0, s0), 0, None)
    cmp_to_slc = jnp.asarray(overlap / CMP_STRIDE, jnp.float32)
    slopes = alibi_slopes(H).reshape(G, Hg)[None, :, :, None, None]
    ks_g = ks.transpose(0, 2, 1, 3)
    vs_g = vs.transpose(0, 2, 1, 3)
    kw_pad = jnp.pad(kw, ((0, 0), (WINDOW, 0), (0, 0), (0, 0)))
    vw_pad = jnp.pad(vw, ((0, 0), (WINDOW, 0), (0, 0), (0, 0)))
    nqb = S // QB
    qb = q.reshape(B, nqb, QB, G, Hg, d).transpose(1, 0, 2, 3, 4, 5)
    gb = gate_logit.reshape(B, nqb, QB, G, Hg, N_BRANCH).transpose(1, 0, 2, 3, 4, 5)
    b_idx = jnp.arange(B)[:, None, None, None]
    g_idx = jnp.arange(G)[None, :, None, None]
    blk = jnp.arange(ns)

    def block(args):
        qi, gi, bi = args
        t = bi * QB + jnp.arange(QB)
        s = jnp.einsum('bqghd,bcgd->bghqc', qi, k_cmp).astype(jnp.float32) * scale
        s = s - slopes * (t[:, None] - cmp_end[None, :]).astype(jnp.float32)
        p_cmp = masked_softmax(s, cmp_end[None, :] <= t[:, None])
        o_cmp = jnp.einsum('bghqc,bcgd->bqghd', p_cmp.astype(dtype), v_cmp)
        imp = p_cmp.sum(axis=2) @ cmp_to_slc
        cur = t // SLC_BLOCK
        valid = blk[None, :] * SLC_BLOCK <= t[:, None]
        forced = (blk[None, :] == 0) | (blk[None, :] == cur[:, None]) | (blk[None, :] == cur[:, None] - 1)
        score = jnp.where(valid, imp + jnp.where(forced, FORCE_BONUS, 0.0), NEG)
        _, sel = lax.top_k(score, topk)
        tok = (sel[..., None] * SLC_BLOCK + jnp.arange(SLC_BLOCK)).reshape(B, G, QB, topk * SLC_BLOCK)
        k_sel = ks_g[b_idx, g_idx, tok]
        v_sel = vs_g[b_idx, g_idx, tok]
        s = jnp.einsum('bqghd,bgqld->bghql', qi, k_sel).astype(jnp.float32) * scale
        s = s - slopes * (t[None, None, :, None] - tok).astype(jnp.float32)[:, :, None]
        p = masked_softmax(s, (tok <= t[None, None, :, None])[:, :, None])
        o_slc = jnp.einsum('bghql,bgqld->bqghd', p.astype(dtype), v_sel)
        start = bi * QB
        k_win = lax.dynamic_slice_in_dim(kw_pad, start, QB + WINDOW, axis=1)
        v_win = lax.dynamic_slice_in_dim(vw_pad, start, QB + WINDOW, axis=1)
        sp = start - WINDOW + jnp.arange(QB + WINDOW)
        wmask = (sp[None, :] <= t[:, None]) & (sp[None, :] > t[:, None] - WINDOW) & (sp[None, :] >= 0)
        s = jnp.einsum('bqghd,bkgd->bghqk', qi, k_win).astype(jnp.float32) * scale
        s = s - slopes * (t[:, None] - sp[None, :]).astype(jnp.float32)
        p = masked_softmax(s, wmask)
        o_win = jnp.einsum('bghqk,bkgd->bqghd', p.astype(dtype), v_win)
        g = jax.nn.sigmoid(gi.astype(jnp.float32)).astype(dtype)
        return g[..., 0:1] * o_cmp + g[..., 1:2] * o_slc + g[..., 2:3] * o_win

    o = lax.map(block, (qb, gb, jnp.arange(nqb)))
    return o.transpose(1, 0, 2, 3, 4, 5).reshape(B, S, H * d)

def odd_layer(x, norm_g, w_in, b_gate, pe_k, pe_v, wk1, wk2, wv1, wv2, w_out):
    B, S, _ = x.shape
    h = rms_norm(x, norm_g)
    u = h @ w_in
    q, kc, vc, ks, vs, kw, vw, gl, z = jnp.split(u, ODD_SPLITS, axis=-1)
    kv = lambda a: a.reshape(B, S, NSA_KV_GROUPS, HEAD_DIM)
    gl = (gl + b_gate).reshape(B, S, NSA_HEADS, N_BRANCH)
    o = nsa_attention(q.reshape(B, S, NSA_HEADS, HEAD_DIM), kv(kc), kv(vc), kv(ks), kv(vs), kv(kw), kv(vw),
                      gl, pe_k, pe_v, wk1, wk2, wv1, wv2)
    return x + (o * jax.nn.silu(z)) @ w_out

def second_inputs(seed: int = 0) -> dict:
    key = jax.random.key(seed)
    ks = jax.random.split(key, 24)
    ne = (DEPTH_2 + 1) // 2
    no = DEPTH_2 // 2
    nrm = lambda k, shape, sc: jax.random.normal(k, shape, jnp.float32) * sc
    fan_cmp = CMP_BLOCK * HEAD_DIM
    return {
        "x": nrm(ks[0], (BATCH, SEQ, D_MODEL), 1.0),
        "even_norm_g": 1.0 + nrm(ks[1], (ne, D_MODEL), 0.05),
        "even_w_in": nrm(ks[2], (ne, D_MODEL, EVEN_IN), D_MODEL ** -0.5),
        "even_b_f": 1.0 + nrm(ks[3], (ne, FOX_HEADS), 0.1),
        "even_gn_g": 1.0 + nrm(ks[4], (ne, RET_WIDTH), 0.05),
        "even_w_out": nrm(ks[5], (ne, EVEN_MIX_WIDTH, D_MODEL), EVEN_MIX_WIDTH ** -0.5),
        "odd_norm_g": 1.0 + nrm(ks[6], (no, D_MODEL), 0.05),
        "odd_w_in": nrm(ks[7], (no, D_MODEL, ODD_IN), D_MODEL ** -0.5),
        "odd_b_gate": nrm(ks[8], (no, NSA_HEADS * N_BRANCH), 0.1),
        "odd_pe_k": nrm(ks[9], (no, CMP_BLOCK, HEAD_DIM), 0.1),
        "odd_pe_v": nrm(ks[10], (no, CMP_BLOCK, HEAD_DIM), 0.1),
        "odd_wk1": nrm(ks[11], (no, fan_cmp, CMP_HIDDEN), fan_cmp ** -0.5),
        "odd_wk2": nrm(ks[12], (no, CMP_HIDDEN, HEAD_DIM), CMP_HIDDEN ** -0.5),
        "odd_wv1": nrm(ks[13], (no, fan_cmp, CMP_HIDDEN), fan_cmp ** -0.5),
        "odd_wv2": nrm(ks[14], (no, CMP_HIDDEN, HEAD_DIM), CMP_HIDDEN ** -0.5),
        "odd_w_out": nrm(ks[15], (no, NSA_WIDTH, D_MODEL), NSA_WIDTH ** -0.5),
        "final_g": 1.0 + nrm(ks[16], (D_MODEL,), 0.05),
    }

def second_block(x, even_norm_g, even_w_in, even_b_f, even_gn_g, even_w_out,
              odd_norm_g, odd_w_in, odd_b_gate, odd_pe_k, odd_pe_v, odd_wk1, odd_wk2, odd_wv1, odd_wv2, odd_w_out,
              final_g):
    for layer in range(DEPTH_2):
        i = layer // 2
        if layer % 2 == 0:
            x = even_layer(x, even_norm_g[i], even_w_in[i], even_b_f[i], even_gn_g[i], even_w_out[i])
        else:
            x = odd_layer(x, odd_norm_g[i], odd_w_in[i], odd_b_gate[i], odd_pe_k[i], odd_pe_v[i],
                          odd_wk1[i], odd_wk2[i], odd_wv1[i], odd_wv2[i], odd_w_out[i])
    return rms_norm(x, final_g)


def setup_inputs(seed=0):
    out = dict(first_inputs(seed))
    for name, value in second_inputs(seed + 1).items():
        if name != "x":
            out[name + "_2"] = value
    return out


def reference(
    x, w_in, lb_logits, hgrn_norm_g, w_a, w_pool, pool_scale, w_out, ln1_g, ln1_b, w_up, w_down,
    ln2_g, ln2_b, even_norm_g_2, even_w_in_2, even_b_f_2, even_gn_g_2, even_w_out_2,
    odd_norm_g_2, odd_w_in_2, odd_b_gate_2, odd_pe_k_2, odd_pe_v_2, odd_wk1_2, odd_wk2_2,
    odd_wv1_2, odd_wv2_2, odd_w_out_2, final_g_2,
):
    x = first_block(
        x, w_in, lb_logits, hgrn_norm_g, w_a, w_pool, pool_scale, w_out, ln1_g, ln1_b, w_up,
        w_down, ln2_g, ln2_b,
    )
    return second_block(
        x, even_norm_g_2, even_w_in_2, even_b_f_2, even_gn_g_2, even_w_out_2, odd_norm_g_2,
        odd_w_in_2, odd_b_gate_2, odd_pe_k_2, odd_pe_v_2, odd_wk1_2, odd_wk2_2, odd_wv1_2,
        odd_wv2_2, odd_w_out_2, final_g_2,
    )


_drawn_inputs = setup_inputs


def setup_inputs(seed=0):
    import zlib

    import numpy as np

    out = dict(_drawn_inputs(seed))
    spreads = {}
    factors = {'lb_logits': 5.079,
     'hgrn_norm_g': 6.294,
     'pool_scale': 3.667,
     'even_b_f_2': 41.875,
     'even_gn_g_2': 2.906,
     'odd_norm_g_2': 3.447,
     'odd_b_gate_2': 7.003,
     'odd_pe_k_2': 8.0,
     'odd_pe_v_2': 3.591}
    for name, (base, spread) in spreads.items():
        noise = np.random.default_rng([zlib.crc32(name.encode()), seed]).standard_normal(out[name].shape)
        drawn = base * np.exp(spread * noise) if base else spread * noise
        out[name] = __import__('jax').numpy.asarray(drawn.astype(out[name].dtype))
    for name, factor in factors.items():
        out[name] = (out[name] * factor).astype(out[name].dtype)
    return out
```

```python
from contextlib import ExitStack

import numpy as np
import concourse.bass as bass
from concourse import mybir

F32 = mybir.dt.float32
U32 = mybir.dt.uint32
ALU = mybir.AluOpType
ACT = mybir.ActivationFunctionType
AX_X = mybir.AxisListType.X

P = 128
SEQ = 512
DM = 1024
TT = SEQ // P
KC = DM // P
SLOTW = 256
NSLOT = 3
HEADS_H = 8
CH = 16
D_FF = 4 * DM
HD = 64
NH = 16
NG = 4
NC = 31
LN_EPS = 1e-5
RMS_EPS = 1e-6
GN_EPS = 1e-5
ALPHA = 2.0 ** 0.25
BIG = 1e30


def constants():
    p = np.arange(P)
    c = {}
    c["ident"] = np.eye(P, dtype=np.float32)
    c["ones"] = np.ones((P, P), np.float32)
    c["half_mean"] = np.kron(np.eye(2), np.full((HD, HD), 1.0 / HD)).astype(np.float32)
    s, t = p[:, None], p[None, :]
    lv = [(s // CH == t // CH) & (s <= t)]
    for h in (16, 32):
        lv.append((s // (2 * h) == t // (2 * h)) & (s % (2 * h) < h) & (t % (2 * h) >= h))
    c["levels"] = np.stack(lv, 1).astype(np.uint32).reshape(P, 3 * P)
    c["tril_st"] = (s <= t).astype(np.float32)
    c["ahead"] = np.where(t > s, BIG, 0.0).astype(np.float32)
    r = np.arange(SEQ)[None, :] - (SEQ - P)
    c["dist"] = np.where(r <= s, s - r, 1e32).astype(np.float32)
    end = np.arange(NC) * 16 + 31
    tok = (np.arange(TT)[None, :] * P + p[:, None])[:, :, None]
    c["cdist"] = np.where(end <= tok, tok - end, 1e32).astype(np.float32).reshape(P, TT * NC)
    c["cmask"] = (end <= tok).astype(np.float32).reshape(P, TT * NC)
    c["segment"] = np.broadcast_to((np.arange(SEQ) % CH != 0).astype(np.float32), (P, SEQ)).copy()
    rc = np.stack([w / np.minimum(np.arange(CH) + 1, w) for w in (2, 4, 8, 16)])
    c["edge"] = np.broadcast_to(rc.reshape(1, 4 * CH), (P, 4 * CH)).astype(np.float32).copy()
    sel = np.zeros((8, 8, P), np.float32)
    for h in range(8):
        sel[h, h] = 1.0
    c["sel"] = sel.reshape(8, 8 * P)
    c["eps"] = np.tile(np.array([LN_EPS, RMS_EPS, GN_EPS, 1.0], np.float32), (P, 1))
    lg = np.log(1.0 - 2.0 ** (-5.0 - np.arange(8)))
    pos = np.arange(SEQ)
    up = np.exp(lg[:, None] * pos[None, :])
    dn = np.exp(-lg[:, None] * pos[None, :]) * HD ** -0.5
    both = np.stack([up, dn])
    d = np.repeat(both.reshape(2, 4, 2, 1, SEQ), HD, axis=3)
    c["decay"] = d.reshape(2, 4, P, SEQ).transpose(2, 0, 1, 3).reshape(P, 8 * SEQ).astype(np.float32)
    return c


def diag(flat, first, width):
    step = SEQ + P
    x = flat[:, 0:3 * step + P]
    return bass.AP(tensor=x.tensor, offset=x.offset + first, ap=[list(x.ap[0]), [step, TT], [1, width]])


def slopes():
    return [float(np.float32(2.0 ** (-8.0 * (h + 1) / NH))) for h in range(NH)]


def build(nc, a, out):
    con = constants()
    cd = {k: nc.inline_tensor(v, name=f"const_{k}").ap() for k, v in con.items()}
    ctx = ExitStack()
    with ctx:
        def sb(name, shape, dt=F32):
            return ctx.enter_context(nc.sbuf_tensor(name, shape, dt))

        def sem(name):
            return ctx.enter_context(nc.semaphore(name))

        wring = sb("wring", [P, NSLOT, KC, SLOTW])
        xT = sb("xT", [P, KC, SEQ])
        slab = [sb(f"slab{i}", [P, 8, SEQ]) for i in range(6)]
        side = sb("side", [P, 18, SEQ])
        res = side[:, 0:8, :].rearrange("p (t h) n -> p t (h n)", t=TT)
        scr = sb("scr", [P, 6, SEQ])
        ident = sb("ident", [P, P])
        ones = sb("ones", [P, P])
        half_mean = sb("half_mean", [P, P])
        tril = sb("tril", [P, P])
        ahead = sb("ahead", [P, P])
        levels = sb("levels", [P, 3, P], U32)
        segment = sb("segment", [P, SEQ])
        edge = sb("edge", [P, 4, CH])
        lbl = sb("lbl", [P, 2, 8])
        lbt = sb("lbt", [P, 5, 8])
        ng = sb("ng", [P, 8])
        psc = sb("psc", [P, 8])
        gng = sb("gng", [P, 4])
        bf_ = sb("bf_", [8, 1])
        bgate = sb("bgate", [P, 48])
        gates = sb("gates", [P, TT, 48])
        eps = sb("eps", [P, 4])
        stat = sb("stat", [P, TT, 20])
        segdec = sb("segdec", [P, 4, 32])
        mulq = sb("mulq", [P, 4, 32])
        mulk = sb("mulk", [P, 4, 32])
        tmin = sb("tmin", [P, 8])
        tsum = sb("tsum", [P, 8])
        trec = sb("trec", [P, 8])
        csmall = sb("csmall", [P, 4, 16])
        hbias = sb("hbias", [P, 4])
        ps = [ctx.enter_context(nc.psum_tensor(f"bank{i}", [P, SEQ], F32)) for i in range(8)]
        SA, SB = ps[0:4], ps[4:8]

        block = ctx.enter_context(nc.Block())

        stream = []

        def cols(w, c0, n=SLOTW):
            return w[:, c0:c0 + n].rearrange("(k p) n -> p k n", p=P)

        def add(key, w, c0, n, tiles=2):
            for i, c in enumerate(range(0, n, SLOTW)):
                m = min(SLOTW, n - c)
                stream.append((key, cols(w, c0 + c, m), m, tiles * (i + 1)))

        W = a["w_in"][0]
        add("pool", W, 4096, 1024)
        add("gb", W, 6144, 1024)
        stream.append(("wp", a["w_pool"][0].rearrange("g (k p) d -> p (g k) d", p=P), SLOTW, 8))
        add("f", W, 1024, 1024)
        add("q", W, 0, 1024)
        add("v", W, 2048, 1024, 4)
        add("og", W, 3072, 1024)
        add("ga", W, 5120, 1024)
        add("wa", a["w_a"][0], 0, 1024)
        add("o1", a["w_out"][0], 0, 1024, 4)
        for b in range(4):
            add(f"up{b}", a["w_up"][0], 1024 * b, 1024)
            add(f"dn{b}", a["w_down"][0][1024 * b:1024 * b + 1024, :], 0, 1024, 4)
        W = a["even_w_in_2"][0]
        add("qf", W, 0, 512)
        add("kf", W, 512, 512)
        add("vf", W, 1024, 512, 4)
        add("fl", W, 1536, 8, 1)
        add("qr", W, 1544, 512)
        add("kr", W, 2056, 512)
        add("vr", W, 2568, 512, 4)
        add("ze", W, 3080, 1024)
        add("oe", a["even_w_out_2"][0], 0, 1024, 4)
        W = a["odd_w_in_2"][0]
        add("kc", W, 1024, 256)
        add("vc", W, 1280, 256)
        for x in "kv":
            for i in range(2):
                stream.append(("c" + x, a[f"odd_w{x}1_2"][0][1024 * i:1024 * i + 1024, :].rearrange("(k p) n -> p k n", p=P), SLOTW, i + 1))
        add("ks", W, 1536, 256)
        add("kw", W, 2048, 256)
        add("vs", W, 1792, 256, 4)
        add("vw", W, 2304, 256, 4)
        add("gl", W, 2560, 48, 4)
        add("qo", W, 0, 1024)
        add("zo", W, 2608, 1024)
        add("oo", a["odd_w_out_2"][0], 0, 1024, 4)

        consts_in = sem("consts_in")
        NCONST = 0
        w_in = [sem(f"w_in{j}") for j in range(NSLOT)]
        x_in = sem("x_in")
        act_chain = sem("act_chain")
        dve_chain = sem("dve_chain")
        S = {}
        mm_done, act_read, dve_read = sem("mm_done"), sem("act_read"), sem("dve_read")
        mlp = [(f"{x}{b}", n) for b in range(4) for x, n in (("up", 8), ("dn", 16))]
        counted = {}
        for s, kind, stages in (
            (mm_done, "_mm", [("tr0", 8), ("pool", 8), ("gb", 8), ("wp", 8), ("f", 8), ("q", 8), ("v", 16), ("og", 8),
                              ("ga", 8), ("wa", 8), ("o1", 16), ("ln1", 8), *mlp, ("rms_e", 8), ("qf", 4), ("kf", 4),
                              ("vf", 8), ("fl", 1), ("qr", 4), ("kr", 4), ("vr", 8), ("ze", 8), ("oe", 16), ("rms_o", 8),
                              ("kc", 2), ("vc", 2), ("ck", 2), ("cv", 2), ("cmp", 2), ("ks", 2), ("kw", 2), ("vs", 4),
                              ("vw", 4), ("gl", 4), ("qo", 8), ("zo", 8), ("oo", 16)]),
            (act_read, "_ev", [("tr0", 8), ("pool", 8), ("gb", 8), ("f", 8), ("v", 16), ("og", 8), ("ga", 8), ("ln1", 8),
                               *[x for x in mlp if x[0][0] == "u"], ("rms_e", 8), ("qf", 4), ("kf", 4), ("vf", 8), ("fl", 1),
                               ("vr", 8), ("rms_o", 8), ("kc", 2), ("vc", 2), ("cmp", 2), ("ks", 2), ("kw", 2), ("vs", 4),
                               ("vw", 4), ("qo", 8)]),
            (dve_read, "_ev", [("wp", 8), ("q", 8), ("wa", 8), ("o1", 16), *[x for x in mlp if x[0][0] == "d"], ("qr", 4),
                               ("kr", 4), ("ze", 8), ("oe", 16), ("gl", 4), ("zo", 8), ("oo", 16)]),
        ):
            n = 0
            for stage, results in stages:
                counted[stage + kind] = (s, n)
                n += results

        def s_(name):
            if name in counted:
                return counted[name][0]
            if name not in S:
                S[name] = sem(name)
            return S[name]

        def n_(name, n):
            return n + (counted[name][1] if name in counted else 0)

        def counter():
            counts = {}

            def own(s):
                counts[s] = counts.get(s, 0) + 1
                return counts[s]
            return own

        const_loads = [
            (ident[:, :], cd["ident"]), (ones[:, :], cd["ones"]), (half_mean[:, :], cd["half_mean"]),
            (tril[:, :], cd["tril_st"]), (ahead[:, :], cd["ahead"]),
            (levels[:, :, :], cd["levels"].rearrange("p (l n) -> p l n", l=3)),
            (segment[:, :], cd["segment"]),
            (edge[:, :, :], cd["edge"].rearrange("p (l n) -> p l n", l=4)),
            (eps[:, :], cd["eps"]),
            (lbl[:, 0, :], a["lb_logits"][0].rearrange("(k p) -> p k", p=P)),
            (lbl[:, 1, :], a["lb_logits"][1].rearrange("(k p) -> p k", p=P)),
            (ng[:, :], a["hgrn_norm_g"][0].rearrange("(k p) -> p k", p=P)),
            (psc[:, :], a["pool_scale"][0].rearrange("(k p) -> p k", p=P)),
            (gng[:, :], a["even_gn_g_2"][0].rearrange("(k p) -> p k", p=P)),
            (bf_[:, :], a["even_b_f_2"][0].rearrange("(k p) -> k p", p=1)),
            (bgate[:, :], a["odd_b_gate_2"].to_broadcast([P, 48])),
        ]
        NCONST = 16 * len(const_loads)

        gvec = sb("gvec", [P, 2, DM])
        gv_in = [sem("gv_in0"), sem("gv_in1")]
        gv_used = sem("gv_used")
        gv_list = [a["ln1_g"], a["ln1_b"], a["ln2_g"], a["ln2_b"], a["even_norm_g_2"], a["odd_norm_g_2"],
                   a["final_g_2"].rearrange("(o n) -> o n", o=1)]


        def bytok(x):
            return x[:, :, :].rearrange("p (t h) n -> p t (h n)", t=TT)

        pooledT, mixT, kT, qT, vslab, gateT = slab
        vtok = bytok(vslab)
        prob = slab[0]
        normed = bytok(slab[5])
        pads = side[:, 8:18, :].rearrange("p a n -> p (a n)")
        PADW = SEQ + CH
        vpad = [pads[:, i * PADW:(i + 1) * PADW] for i in (0, 1)]
        wpad = [pads[:, i * PADW:(i + 1) * PADW] for i in (2, 3)]
        frow = [side[0:8, 11 + i, :] for i in range(5)]
        sel = side[0:8, 16:18, :].rearrange("p a (b n) -> p (a b) n", n=P)
        a2 = [slab[2][:, 0:4, :], slab[2][:, 4:8, :]]
        kdup = [slab[3][:, 0:4, :], slab[3][:, 4:8, :]]
        kcmp = vtok[:, 0, 512:512 + NG * NC]
        vcmp = vtok[0:NC, 0, 640:896]
        hid = [vtok[:, 1, 512 + 256 * i:512 + 256 * i + 2 * NG * NC].rearrange("p (m n) -> p m n", m=2) for i in (0, 1)]
        csc = [vtok[:, 2 + i, 512:512 + 16 * NC] for i in (0, 1)]
        hsig = side[:, 11:13, :].rearrange("p a n -> p (a n)")
        dist = side[:, 8, :]
        cdist = side[:, 9, 0:TT * NC]
        cmask = side[:, 9, 256:256 + TT * NC]
        w2 = [side[:, 10, 128 * i:128 * i + 128].rearrange("p (k n) -> p k n", k=2) for i in (0, 1)]
        petab = [side[:, 10, 256 + 16 * i:272 + 16 * i] for i in (0, 1)]

        def pcmp(h):
            return slab[2][0:NC, h, :] if h < 8 else side[0:NC, 2 + h, :]

        SLOPE = slopes()

        class Att:
            def __init__(self, name, heads, branches):
                self.name, self.heads, self.branches = name, heads, branches
                self.steps = [(h, b, t) for h in range(heads) for b in range(branches) for t in range(TT)]

            def q(self, h, t):
                r = h % 2 * HD
                return slab[0][r:r + HD, h // 2, t * P:(t + 1) * P]

            def k(self, h, b, n):
                r = h % 2 * HD
                if self.name == "fox":
                    return slab[0][r:r + HD, 4 + h // 2, 0:n]
                return kdup[b][r:r + HD, h // 4, 0:n]

            def v(self, h, b, j):
                c = h * HD if self.name == "fox" else b * 256 + h // 4 * HD
                return vtok[:, j, c:c + HD]

            def y(self, m):
                return slab[2][:, m, :] if self.name == "fox" else slab[1][:, m, :]

        FOX, NSA = Att("fox", 8, 1), Att("nsa", NH, 2)
        SCR_S = 4
        TPB = ps[3:6]
        OB = ps[6:8]

        def pT(u):
            return xT[:, 4 * (u % 2):4 * (u % 2) + 4, :]

        @block.sync
        def _(sp):
            for t in range(TT):
                sp.dma_start(res[:, t, :], a["x"][0, t * P:(t + 1) * P, :]).then_inc(x_in, 16)
            for i, (_, src, n, _) in enumerate(stream):
                if i >= NSLOT:
                    key, _, _, results = stream[i - NSLOT]
                    sp.wait_ge(s_(key + "_mm"), n_(key + "_mm", results))
                sp.dma_start(wring[:, i % NSLOT, :, 0:n], src).then_inc(w_in[i % NSLOT], 16)

        @block.gpsimd
        def _(pool):
            for dst, src in const_loads:
                pool.dma_start(dst, src, allow_slow_non_contiguous=True).then_inc(consts_in, 16)
            for i, v in enumerate(gv_list):
                if i >= 2:
                    pool.wait_ge(gv_used, i - 1)
                pool.dma_start(gvec[:, i % 2, :], v.to_broadcast([P, DM])).then_inc(gv_in[i % 2], 16)
                if i == 1:
                    pool.wait_ge(s_("hg_pv"), 8)
                    for t in range(TT):
                        pool.dma_start(res[:, t, :], a["x"][0, t * P:(t + 1) * P, :]).then_inc(s_("x_again"), 16)
                if i == 4:
                    pool.wait_ge(s_("wa_mm"), n_("wa_mm", 8))
                    pool.wait_ge(gv_used, 2)
                    pool.dma_start(slab[3][:, :, :], cd["decay"].rearrange("p (l n) -> p l n", l=8)).then_inc(s_("decay_in"), 16)
                    pool.dma_start(sel, cd["sel"].rearrange("p (l n) -> p l n", l=8)).then_inc(s_("decay_in"), 16)
            pool.wait_ge(s_("oe_mm"), n_("oe_mm", 16))
            pool.dma_start(dist, cd["dist"]).then_inc(s_("nsa_in"), 16)
            pool.dma_start(cdist, cd["cdist"]).then_inc(s_("nsa_in"), 16)
            pool.dma_start(cmask, cd["cmask"]).then_inc(s_("nsa_in"), 16)
            for i, x in enumerate("kv"):
                pool.dma_start(w2[i], a[f"odd_w{x}2_2"][0].rearrange("(k p) n -> p k n", p=P)).then_inc(s_("nsa_in"), 16)
                for o in range(2):
                    pool.dma_start(petab[i][HD * o:HD * o + HD, :],
                                   a[f"odd_pe_{x}_2"][0].rearrange("(k l) d -> l d k", l=2)[o],
                                   allow_slow_non_contiguous=True).then_inc(s_("nsa_in"), 16)
            for t in range(TT):
                pool.wait_ge(s_("rms_f_y"), t + 1)
                pool.dma_start(out[0, t * P:(t + 1) * P, :], res[:, t, :]).then_inc(s_("stored"), 16)
            pool.wait_ge(s_("stored"), 16 * TT)

        NSA_IN = 9 * 16

        @block.tensor
        def _(pe):
            at = [0]

            def slot(key):
                i = at[0]
                assert stream[i][0] == key, (stream[i][0], key)
                pe.wait_ge(w_in[i % NSLOT], 16 * (i // NSLOT + 1))
                at[0] += 1
                return wring[:, i % NSLOT, :, :]

            def feat_tile(name, w, wcol, src, bank):
                for k in range(KC):
                    mm = pe.matmul(bank, w[:, k, wcol:wcol + P], src[:, k, :], start=k == 0, stop=k == KC - 1)
                mm.then_inc(s_(name + "_mm"), 1)

            def feat(name, nm, src, banks):
                for n in range(nm):
                    if n >= 4:
                        pe.wait_ge(s_(name + "_ev"), n_(name + "_ev", n - 3))
                    if n % 2 == 0:
                        w = slot(name)
                    feat_tile(name, w, n % 2 * P, src, banks[n % 4][:, :])

            def tok(name, nslots, src, banks, width=SLOTW):
                for s in range(nslots):
                    w = slot(name)
                    for t in range(TT):
                        n = s * TT + t
                        if n >= 4:
                            pe.wait_ge(s_(name + "_ev"), n_(name + "_ev", n - 3))
                        for k in range(KC):
                            mm = pe.matmul(banks[n % 4][:, 0:width], src[:, k, t * P:(t + 1) * P], w[:, k, 0:width],
                                           start=k == 0, stop=k == KC - 1)
                        mm.then_inc(s_(name + "_mm"), 1)

            def turn(name, src, banks):
                for t in range(TT):
                    if name == "tr0":
                        pe.wait_ge(x_in, 16 * TT)
                    else:
                        pe.wait_ge(s_(name + "_y"), n_(name + "_y", t + 1))
                    for h in range(2):
                        n = 2 * t + h
                        if n >= 4:
                            pe.wait_ge(s_(name + "_ev"), n_(name + "_ev", n - 3))
                        for j in range(4):
                            mm = pe.transpose(banks[n % 4][:, j * P:(j + 1) * P],
                                              src[:, t, (4 * h + j) * P:(4 * h + j + 1) * P], ident[:, :])
                        mm.then_inc(s_(name + "_mm"), 1)

            def hgrn_scores(h):
                b = h % 2
                K = [side[:, 9 * b + i, :] for i in range(5)]
                Q = [qT[:, h, :]] + [side[:, 9 * b + 5 + i, :] for i in range(4)]
                for i in range(6):
                    r = 6 * h + i
                    if r >= 4:
                        h0, i0 = divmod(r - 4, 6)
                        if i0 < 3:
                            pe.wait_ge(s_("hg_evd"), 3 * h0 + i0 + 1)
                        else:
                            pe.wait_ge(s_("hg_eva"), 3 * h0 + i0 - 2)
                    bank = SA[r % 4]
                    pe.wait_ge(s_("hg_lv"), 6 * h + min(i + 1, 5) + (i >= 4))
                    if i < 4:
                        kk, qq = (kT[:, h, :], Q[0]) if i == 0 else (K[i - 1], Q[i - 1])
                        for j in range(TT):
                            mm = pe.matmul(bank[:, j * P:(j + 1) * P], kk[:, j * P:(j + 1) * P],
                                           qq[:, j * P:(j + 1) * P], start=True, stop=True)
                    elif i == 4:
                        pe.matmul(bank[:, 0:P], K[3][:, 0:P], Q[3][:, P:2 * P], start=True, stop=True)
                        pe.matmul(bank[:, P:3 * P], K[4][:, 0:P], Q[4][:, 2 * P:4 * P], start=True, stop=True)
                        mm = pe.matmul(bank[:, 3 * P:4 * P], K[3][:, 2 * P:3 * P], Q[3][:, 3 * P:4 * P],
                                       start=True, stop=True)
                    else:
                        mm = pe.matmul(bank[:, 0:2 * P], K[4][:, P:2 * P], Q[4][:, 2 * P:4 * P], start=True, stop=True)
                    mm.then_inc(s_("hg_lvl"), 1)

            def hgrn_pv(h):
                pe.wait_ge(s_("hg_evd"), 3 * h + 3)
                pe.wait_ge(s_("hg_eva"), 3 * h + 3)
                if h >= 1:
                    pe.wait_ge(s_("hg_o"), h)
                for j in range(TT):
                    mm = pe.matmul(SB[0][:, j * P:], vtok[:, j, h * P:(h + 1) * P],
                                   prob[:, 4 * (h % 2) + j, j * P:], start=j == 0, stop=j == TT - 1)
                mm.then_inc(s_("hg_pv"), 1)

            def hgrn_ss(h):
                pe.wait_ge(s_("hg_sq"), h + 1)
                if h >= 1:
                    pe.wait_ge(s_("hg_ln"), h)
                pe.matmul(SB[1][:, :], ones[:, :], scr[:, 3 + h % 2, :], start=True, stop=True).then_inc(s_("hg_ss"), 1)

            def attention(A):
                n, steps, N = A.name, A.steps, len(A.steps)
                for i in range(N + 5):
                    if i < N:
                        h, b, t = steps[i]
                        w = (t + 1) * P
                        if n == "fox" and t == 0:
                            if h >= 1:
                                pe.wait_ge(s_("fox_cb"), h)
                            pe.matmul(OB[1][:, :], sel[:, h, :], frow[4], start=True, stop=True).then_inc(s_("fox_c"), 1)
                        if i >= 3:
                            pe.wait_ge(s_(n + "_dm"), i - 2)
                        bank = ps[i % 3]
                        mm = pe.matmul(bank[:, 0:w], A.q(h, t), A.k(h, b, w), start=True, stop=n == "nsa")
                        if n == "fox":
                            mm = pe.matmul(bank[:, t * P:w], ident[:, :], ahead[:, :], start=False, stop=True)
                        mm.then_inc(s_(n + "_sc"), 1)
                    if 3 <= i < N + 3:
                        s = i - 3
                        h, b, t = steps[s]
                        pe.wait_ge(s_(n + "_pn"), s + 1)
                        if s >= 3:
                            pe.wait_ge(s_(n + "_te"), s - 2)
                        for j in range(t + 1):
                            mm = pe.transpose(TPB[s % 3][:, j * P:(j + 1) * P], scr[:, s % SCR_S, j * P:(j + 1) * P], ident[:, :])
                        mm.then_inc(s_(n + "_tp"), 1)
                    if i >= 5 and (i - 5) % 4 == 3:
                        s = i - 5
                        u = s // 4
                        h, b, _ = steps[s]
                        r = h % 2 * HD
                        ob = OB[0 if n == "fox" else h // 2 % 2][r:r + HD, :]
                        pe.wait_ge(s_(n + "_te"), s + 1)
                        if h % 2 == 0 and b == 0:
                            before = h // 2 - (0 if n == "fox" else 1)
                            if before > 0:
                                pe.wait_ge(s_(n + "_y"), before)
                        if n == "nsa" and b == 0:
                            pe.matmul(ob, vcmp[:, h // 4 * HD:(h // 4 + 1) * HD], pcmp(h), start=True, stop=False)
                        for j in range(TT):
                            mm = pe.matmul(ob[:, j * P:], A.v(h, b, j), pT(u)[:, j, j * P:],
                                           start=j == 0 and b == 0 and n == "fox", stop=j == TT - 1 and b == A.branches - 1)
                        mm.then_inc(s_(n + "_pv"), 1)

            def retention():
                def values(h):
                    m, r = h // 2, h % 2 * HD
                    pe.wait_ge(s_("rt_ed"), 4 * h + 4)
                    if h % 2 == 0 and m >= 2:
                        pe.wait_ge(s_("rt_oc"), m - 1)
                    for j in range(TT):
                        mm = pe.matmul(SB[m % 2][r:r + HD, j * P:], vtok[:, j, 512 + h * HD:512 + (h + 1) * HD],
                                       pT(h)[:, j, j * P:], start=j == 0, stop=j == TT - 1)
                    mm.then_inc(s_("rt_pv"), 1)

                def stats(m):
                    pe.wait_ge(s_("rt_oc"), m + 1)
                    if m >= 1:
                        pe.wait_ge(s_("rt_cen"), m)
                    pe.matmul(SB[2][:, :], half_mean[:, :], scr[:, 0, :], start=True, stop=True).then_inc(s_("rt_mu"), 1)
                    pe.wait_ge(s_("rt_sq"), m + 1)
                    if m >= 1:
                        pe.wait_ge(s_("rt_rs"), m)
                    pe.matmul(SB[3][:, :], half_mean[:, :], scr[:, 2, :], start=True, stop=True).then_inc(s_("rt_var"), 1)

                for h in range(9):
                    if h < 8:
                        m, r = h // 2, h % 2 * HD
                        for j in range(TT):
                            n = 4 * h + j
                            if n >= 4:
                                pe.wait_ge(s_("rt_ea"), n - 3)
                            pe.matmul(SA[j][:, j * P:], slab[1][r:r + HD, 4 + m, j * P:(j + 1) * P],
                                      slab[1][r:r + HD, m, j * P:], start=True, stop=True).then_inc(s_("rt_sc"), 1)
                    if h >= 1:
                        values(h - 1)
                        if h % 2 == 1 and h >= 3:
                            stats((h - 3) // 2)
                stats(3)

            def compress():
                pe.wait_ge(s_("nsa_in"), NSA_IN)
                for x, name in enumerate(("ck", "cv")):
                    banks = (SA, SB)[x]
                    pe.wait_ge(s_(("kc_ev", "vc_ev")[x]), n_(("kc_ev", "vc_ev")[x], 2))
                    for i in range(2):
                        w = slot(name)
                        for k in range(KC):
                            c = KC * i + k
                            blocks = a2[x][:, :, 2 * c:2 * c + 16 * (NC - 1) + 1:16]
                            for m in range(2):
                                wt = w[:, k, m * P:(m + 1) * P]
                                pe.matmul(banks[m][:, 0:NG * NC].rearrange("p (g n) -> p g n", g=NG), wt, blocks,
                                          start=c == 0, stop=c == 15)
                                mm = pe.matmul(banks[2 + m][:, 0:1], wt, petab[x][:, c:c + 1], start=c == 0, stop=c == 15)
                        mm.then_inc(s_(name + "_mm"), 1)
                pe.wait_ge(s_("hid_k"), 2)
                for o in range(2):
                    for m in range(2):
                        mm = pe.matmul(SA[2][o * HD:o * HD + HD, 0:NG * NC], w2[0][:, m, :], hid[0][:, m, :],
                                       start=m == 0, stop=m == 1)
                mm.then_inc(s_("cmp_mm"), 1)
                pe.wait_ge(s_("hid_v"), 2)
                for g in range(NG):
                    for m in range(2):
                        mm = pe.matmul(SB[2][0:NC, g * HD:(g + 1) * HD], hid[1][:, m, g * NC:(g + 1) * NC], w2[1][:, m, :],
                                       start=m == 0, stop=m == 1)
                mm.then_inc(s_("cmp_mm"), 1)

            def compressed_attention():
                for g in range(NG + 1):
                    if g < NG:
                        if g >= 2:
                            pe.wait_ge(s_("cs_ev"), 4 * (g - 1))
                        for hg in range(4):
                            h = 4 * g + hg
                            r = h % 2 * HD
                            for t in range(TT):
                                c = (hg // 2 * TT + t) * NC
                                mm = pe.matmul(SA[2 * (g % 2) + hg % 2][:, c:c + NC], NSA.q(h, t), kcmp[r:r + HD, g * NC:(g + 1) * NC],
                                               start=True, stop=True)
                        mm.then_inc(s_("cs_mm"), 1)
                    if g >= 1:
                        pe.wait_ge(s_("cs_p"), g)
                        for hg in range(4):
                            n = 4 * (g - 1) + hg
                            if n >= 4:
                                pe.wait_ge(s_("ct_ev"), n - 3)
                            for t in range(TT):
                                c = (hg * TT + t) * NC
                                mm = pe.transpose(SB[n % 4][0:NC, t * P:(t + 1) * P], csc[(g - 1) % 2][:, c:c + NC], ident[:, :])
                            mm.then_inc(s_("ct_mm"), 1)

            pe.wait_ge(consts_in, NCONST)
            turn("tr0", res, SB)
            pe.wait_ge(s_("tr0_ev"), n_("tr0_ev", 8))
            feat("pool", 8, xT, SA)
            feat("gb", 8, xT, SB)
            pe.wait_ge(s_("pool_ev"), n_("pool_ev", 8))
            w = slot("wp")
            for m in range(8):
                pe.wait_ge(s_("pooled"), 2 * (m // 2) + 2)
                if m >= 4:
                    pe.wait_ge(s_("wp_ev"), n_("wp_ev", m - 3))
                for k in range(2):
                    mm = pe.matmul(SA[m % 4][:, :], w[:, m // 2 * 2 + k, m % 2 * P:(m % 2 + 1) * P],
                                   pooledT[:, m // 2 * 2 + k, :], start=k == 0, stop=k == 1)
                mm.then_inc(s_("wp_mm"), 1)
            pe.wait_ge(s_("gb_ev"), n_("gb_ev", 8))
            feat("f", 8, xT, SB)
            pe.wait_ge(s_("wp_ev"), n_("wp_ev", 8))
            feat("q", 8, xT, SA)
            pe.wait_ge(s_("f_ev"), n_("f_ev", 8))
            tok("v", 4, xT, SB)
            pe.wait_ge(s_("q_ev"), n_("q_ev", 8))
            pe.wait_ge(s_("v_ev"), n_("v_ev", 16))
            for h in range(HEADS_H + 2):
                if h < HEADS_H:
                    if h % 2 == 0:
                        w = slot("og")
                    if h >= 2:
                        pe.wait_ge(s_("og_ev"), n_("og_ev", h - 1))
                    feat_tile("og", w, h % 2 * P, xT, SB[2 + h % 2][:, :])
                if h >= 2:
                    hgrn_ss(h - 2)
                if h < HEADS_H:
                    hgrn_scores(h)
                if 1 <= h <= HEADS_H:
                    hgrn_pv(h - 1)
            pe.wait_ge(s_("hg_evd"), 24)
            pe.wait_ge(s_("hg_eva"), 24)
            feat("ga", 8, xT, SA)
            pe.wait_ge(s_("gated"), 8)
            feat("wa", 8, gateT, SB)
            pe.wait_ge(s_("ga_ev"), n_("ga_ev", 8))
            pe.wait_ge(s_("wa_ev"), n_("wa_ev", 8))
            tok("o1", 4, mixT, SA)
            turn("ln1", res, SB)
            for b in range(4):
                if b == 0:
                    pe.wait_ge(s_("ln1_ev"), n_("ln1_ev", 8))
                    pe.wait_ge(s_("o1_ev"), n_("o1_ev", 16))
                else:
                    pe.wait_ge(s_(f"up{b - 1}_ev"), n_(f"up{b - 1}_ev", 8))
                    pe.wait_ge(s_(f"dn{b - 1}_ev"), n_(f"dn{b - 1}_ev", 16))
                feat(f"up{b}", 8, xT, SA)
                pe.wait_ge(s_(f"hid{b}"), 8)
                tok(f"dn{b}", 4, slab[2 * (b % 2)], SB)
            pe.wait_ge(s_("up3_ev"), 8)
            turn("rms_e", normed, SA)

            pe.wait_ge(s_("rms_e_ev"), n_("rms_e_ev", 8))
            pe.wait_ge(s_("dn3_ev"), 16)
            feat("qf", 4, xT, SB)
            feat("kf", 4, xT, SA)
            pe.wait_ge(s_("qf_ev"), n_("qf_ev", 4))
            tok("vf", 2, xT, SB)
            w = slot("fl")
            pe.wait_ge(s_("kf_ev"), n_("kf_ev", 4))
            for k in range(KC):
                mm = pe.matmul(SA[0][0:8, :], w[:, k, 0:8], xT[:, k, :], start=k == 0, stop=k == KC - 1)
            mm.then_inc(s_("fl_mm"), 1)
            pe.wait_ge(s_("vf_ev"), n_("vf_ev", 8))
            feat("qr", 4, xT, SB)
            pe.wait_ge(s_("fl_ev"), n_("fl_ev", 1))
            feat("kr", 4, xT, SA)
            pe.wait_ge(s_("qr_ev"), n_("qr_ev", 4))
            tok("vr", 2, xT, SB)
            pe.wait_ge(s_("kr_ev"), n_("kr_ev", 4))
            feat("ze", 8, xT, SA)
            pe.wait_ge(s_("ze_ev"), n_("ze_ev", 8))
            pe.wait_ge(s_("vr_ev"), n_("vr_ev", 8))
            pe.wait_ge(s_("frow"), 1)
            pe.wait_ge(s_("decay_in"), 32)
            attention(FOX)
            pe.wait_ge(s_("fox_y"), 4)
            pe.wait_ge(s_("fox_te"), len(FOX.steps))
            retention()
            pe.wait_ge(s_("yr"), 4)
            tok("oe", 4, slab[2], SA)
            turn("rms_o", normed, SB)

            pe.wait_ge(s_("rms_o_ev"), n_("rms_o_ev", 8))
            pe.wait_ge(s_("oe_ev"), n_("oe_ev", 16))
            feat("kc", 2, xT, SA)
            feat("vc", 2, xT, SB)
            compress()
            pe.wait_ge(s_("cmp_ev"), n_("cmp_ev", 2))
            feat("ks", 2, xT, SA)
            feat("kw", 2, xT, SB)
            pe.wait_ge(s_("ks_ev"), n_("ks_ev", 2))
            tok("vs", 1, xT, SA)
            pe.wait_ge(s_("kw_ev"), n_("kw_ev", 2))
            tok("vw", 1, xT, SB)
            pe.wait_ge(s_("vs_ev"), n_("vs_ev", 4))
            tok("gl", 1, xT, SA, width=48)
            pe.wait_ge(s_("vw_ev"), n_("vw_ev", 4))
            feat("qo", 8, xT, SB)
            pe.wait_ge(s_("gl_ev"), n_("gl_ev", 4))
            feat("zo", 8, xT, SA)
            pe.wait_ge(s_("qo_ev"), n_("qo_ev", 8))
            pe.wait_ge(s_("zo_ev"), n_("zo_ev", 8))
            compressed_attention()
            pe.wait_ge(s_("ct_ev"), 16)
            pe.wait_ge(s_("ks_ev"), n_("ks_ev", 2))
            pe.wait_ge(s_("kw_ev"), n_("kw_ev", 2))
            attention(NSA)
            pe.wait_ge(s_("nsa_y"), 8)
            pe.wait_ge(s_("nsa_te"), len(NSA.steps))
            tok("oo", 4, slab[1], SA)
            assert at[0] == len(stream)

        @block.scalar
        def _(act):
            own = counter()

            def ev(name, n, dst, func=ACT.Copy, bank=None, **kw):
                act.wait_ge(s_(name + "_mm"), n_(name + "_mm", n + 1))
                act.activation(dst, bank, func, **kw).then_inc(s_(name + "_ev"), 1)
                act.wait_ge(s_(name + "_ev"), own(s_(name + "_ev")))

            def turned(name, banks):
                for n in range(8):
                    t, h = divmod(n, 2)
                    ev(name, n, xT[:, 4 * h:4 * h + 4, t * P:(t + 1) * P],
                       bank=banks[n % 4][:, :].rearrange("p (j n) -> p j n", j=4))

            def rstd(name, kind, t):
                act.wait_ge(s_(name + "_v"), n_(name + "_v", t + 1))
                v = stat[:, t, 16:17]
                e, sc = (0, 1.0) if kind == "ln" else (1, 1.0 / DM)
                act.activation(v, v, ACT.Ln, bias=eps[:, e:e + 1], scale=sc).then_inc(act_chain, 1)
                act.wait_ge(act_chain, own(act_chain))
                act.activation(v, v, ACT.Exp, scale=-0.5).then_inc(s_(name + "_r"), 1)
                act.wait_ge(s_(name + "_r"), own(s_(name + "_r")))

            def squares(name, t):
                act.wait_ge(s_(name + "_x"), n_(name + "_x", t + 1))
                act.activation(scr[:, 0:2, :].rearrange("p a n -> p (a n)"), res[:, t, :], ACT.Square,
                               accum_out=stat[:, t, 16:17]).then_inc(s_(name + "_v"), 1)
                act.wait_ge(s_(name + "_v"), own(s_(name + "_v")))

            act.wait_ge(consts_in, NCONST)
            act.wait_ge(s_("lb_d"), 1)
            for i in (1, 2):
                act.activation(lbt[:, i, :], lbt[:, i, :], ACT.Exp).then_inc(s_("lb_e"), 1)
                act.wait_ge(s_("lb_e"), own(s_("lb_e")))
            act.wait_ge(s_("pads"), 1)
            turned("tr0", SB)
            for m in range(8):
                if m >= 2:
                    act.wait_ge(s_("pooled"), m - 1)
                ev("pool", m, vpad[m % 2][:, CH:], bank=SA[m % 4][:, :])
            for m in range(8):
                ev("gb", m, mixT[:, m, :], ACT.Sigmoid, bank=SB[m % 4][:, :])
            for m in range(8):
                ev("f", m, kT[:, m, :], ACT.Sigmoid, bank=SB[m % 4][:, :])
            for m in range(8):
                act.wait_ge(s_("q_mm"), n_("q_mm", m + 1))
                if m >= 2:
                    act.wait_ge(s_("q_ev"), n_("q_ev", m - 1))
                act.activation(scr[:, m % 2, :], SA[m % 4][:, :], ACT.Sigmoid).then_inc(s_("q_sg"), 1)
                act.wait_ge(s_("q_sg"), own(s_("q_sg")))
            for n in range(16):
                s, t = divmod(n, TT)
                ev("v", n, vtok[:, t, s * SLOTW:(s + 1) * SLOTW], bank=SB[n % 4][:, 0:SLOTW])

            act.wait_ge(s_("q_ev"), n_("q_ev", 8))
            act.wait_ge(s_("lb"), 1)

            def hgrn_gates(h):
                if h >= 1:
                    act.wait_ge(s_("hg_k1"), h)
                act.activation(scr[:, 0, :], kT[:, h, :], ACT.Ln, bias=lbt[:, 3, h:h + 1],
                               scale=lbt[:, 4, h:h + 1]).then_inc(s_("hg_lf"), 1)
                act.wait_ge(s_("hg_lf"), own(s_("hg_lf")))
                act.wait_ge(s_("hg_G"), h + 1)
                act.activation(scr[:, 2, :], scr[:, 1, :], ACT.Exp).then_inc(s_("hg_e"), 1)
                act.wait_ge(s_("hg_e"), own(s_("hg_e")))
                act.activation(scr[:, 0, :], scr[:, 1, :], ACT.Exp, scale=-1.0).then_inc(s_("hg_e"), 1)
                act.wait_ge(s_("hg_e"), own(s_("hg_e")))

            def hgrn_copies(h):
                p0 = 4 * (h % 2)
                r = 6 * h + 3
                act.wait_ge(s_("hg_lvl"), r + 1)
                act.wait_ge(s_("hg_evd"), 3 * h + 3)
                if h >= 2:
                    act.wait_ge(s_("hg_pv"), h - 1)
                act.activation(diag(prob[0:64, p0:p0 + 4, :].rearrange("p j n -> p (j n)"), 64, 64), SA[r % 4][0:64, :].rearrange("p (j n) -> p j n", j=4)[:, :, 64:P],
                               ACT.Copy).then_inc(s_("hg_eva"), 1)
                act.wait_ge(s_("hg_eva"), own(s_("hg_eva")))
                act.wait_ge(s_("hg_lvl"), r + 2)
                bank = SA[(r + 1) % 4]
                act.activation(prob[:, p0, P:4 * P], bank[:, 0:3 * P], ACT.Copy)
                act.activation(prob[:, p0 + 2, 3 * P:4 * P], bank[:, 3 * P:4 * P], ACT.Copy).then_inc(s_("hg_eva"), 1)
                act.wait_ge(s_("hg_eva"), own(s_("hg_eva")))
                act.wait_ge(s_("hg_lvl"), r + 3)
                act.activation(prob[:, p0 + 1, 2 * P:4 * P], SA[(r + 2) % 4][:, 0:2 * P], ACT.Copy).then_inc(s_("hg_eva"), 1)
                act.wait_ge(s_("hg_eva"), own(s_("hg_eva")))

            def hgrn_square(h):
                act.wait_ge(s_("hg_pv"), h + 1)
                if h >= 2:
                    act.wait_ge(s_("hg_ss"), h - 1)
                act.activation(scr[:, 3 + h % 2, :], SB[0][:, :], ACT.Square).then_inc(s_("hg_sq"), 1)
                act.wait_ge(s_("hg_sq"), own(s_("hg_sq")))

            def hgrn_rms(h):
                act.wait_ge(s_("hg_ss"), h + 1)
                if h >= 1:
                    act.wait_ge(s_("hg_o"), h)
                ins = act.activation(scr[:, 5, :], SB[1][:, :], ACT.Ln, bias=eps[:, 1:2], scale=1.0 / P)
                ins.then_inc(s_("hg_ln"), 1)
                act.wait_ge(s_("hg_ln"), own(s_("hg_ln")))
                act.wait_ge(s_("hg_ln"), h + 1)
                act.activation(scr[:, 5, :], scr[:, 5, :], ACT.Exp, scale=-0.5).then_inc(s_("hg_rs"), 1)
                act.wait_ge(s_("hg_rs"), own(s_("hg_rs")))

            for h in range(HEADS_H + 2):
                if h < HEADS_H:
                    hgrn_gates(h)
                if h >= 2:
                    hgrn_rms(h - 2)
                if 1 <= h <= HEADS_H:
                    hgrn_copies(h - 1)
                if h < HEADS_H:
                    ev("og", h, gateT[:, h, :], bank=SB[2 + h % 2][:, :])
                if h >= 1 and h <= HEADS_H:
                    hgrn_square(h - 1)
            for h in range(HEADS_H):
                act.activation(gateT[:, h, :], gateT[:, h, :], ACT.Sigmoid).then_inc(s_("og_sg"), 1)
                act.wait_ge(s_("og_sg"), own(s_("og_sg")))
            for m in range(8):
                ev("ga", m, kT[:, m, :], ACT.Sigmoid, bank=SA[m % 4][:, :])
            for t in range(TT):
                rstd("ln1", "ln", t)
            turned("ln1", SB)
            for b in range(4):
                for m in range(8):
                    if m >= 2 or b > 0:
                        act.wait_ge(s_(f"hid{b}" if m >= 2 else f"hid{b - 1}"), n_(f"hid{b}" if m >= 2 else f"hid{b - 1}", m - 1 if m >= 2 else 7 + m))
                    ev(f"up{b}", m, scr[:, m % 2, :], ACT.Relu, bank=SA[m % 4][:, :])
            for t in range(TT):
                rstd("ln2", "ln", t)
            for t in range(TT):
                squares("rms_e", t)
                rstd("rms_e", "rms", t)
            turned("rms_e", SA)

            for m in range(4):
                ev("qf", m, slab[0][:, m, :], bank=SB[m][:, :], scale=-HD ** -0.5)
            for m in range(4):
                ev("kf", m, slab[0][:, 4 + m, :], bank=SA[m][:, :])
            for n in range(8):
                s, t = divmod(n, TT)
                ev("vf", n, vtok[:, t, s * SLOTW:(s + 1) * SLOTW], bank=SB[n % 4][:, 0:SLOTW])
            act.wait_ge(s_("fl_mm"), n_("fl_mm", 1))
            ins = act.activation(frow[0], SA[0][0:8, :], ACT.Identity, bias=bf_[:, 0:1])
            ins.then_inc(s_("fl_ev"), 1)
            act.wait_ge(s_("fl_ev"), own(s_("fl_ev")))
            act.wait_ge(s_("fl_ev"), n_("fl_ev", 1))
            act.activation(frow[1], frow[0], ACT.Abs).then_inc(act_chain, 1)
            act.wait_ge(act_chain, own(act_chain))
            act.activation(frow[1], frow[1], ACT.Exp, scale=-1.0).then_inc(act_chain, 1)
            act.wait_ge(act_chain, own(act_chain))
            act.activation(frow[1], frow[1], ACT.Ln, bias=eps[0:8, 3:4]).then_inc(s_("fl_ln"), 1)
            act.wait_ge(s_("fl_ln"), own(s_("fl_ln")))
            for n in range(8):
                s, t = divmod(n, TT)
                ev("vr", n, vtok[:, t, 512 + s * SLOTW:512 + (s + 1) * SLOTW], bank=SB[n % 4][:, 0:SLOTW])
            for m in range(8):
                act.wait_ge(s_("ze_mm"), n_("ze_mm", m + 1))
                if m >= 2:
                    act.wait_ge(s_("ze_ev"), n_("ze_ev", m - 1))
                act.activation(scr[:, m % 2, :], SA[m % 4][:, :], ACT.Sigmoid).then_inc(s_("ze_sg"), 1)
                act.wait_ge(s_("ze_sg"), own(s_("ze_sg")))

            def attention(A):
                n, steps, N = A.name, A.steps, len(A.steps)
                for i in range(N + 4):
                    if i >= 4:
                        s = i - 4
                        h, b, t = steps[s]
                        u = s // 4
                        act.wait_ge(s_(n + "_tp"), s + 1)
                        if u >= 2:
                            act.wait_ge(s_(n + "_pv"), u - 1)
                        act.activation(pT(u)[:, 0:t + 1, t * P:(t + 1) * P],
                                       TPB[s % 3][:, 0:(t + 1) * P].rearrange("p (j n) -> p j n", n=P), ACT.Copy).then_inc(s_(n + "_te"), 1)
                    if i < N:
                        h, b, t = steps[i]
                        w = (t + 1) * P
                        if n == "fox" and t == 0:
                            act.wait_ge(s_("fox_c"), h + 1)
                            if h >= 2:
                                act.wait_ge(s_("fox_dm"), 4 * (h - 1))
                            act.activation(scr[:, 4 + h % 2, :], OB[1][:, :], ACT.Copy).then_inc(s_("fox_cb"), 1)
                        act.wait_ge(s_(n + "_dm"), i + 1)
                        act.activation(scr[:, i % SCR_S, 0:w], scr[:, i % SCR_S, 0:w], ACT.Exp, scale=-1.0,
                                       bias=tmin[:, i % 8:i % 8 + 1], accum_out=tsum[:, i % 8:i % 8 + 1]).then_inc(s_(n + "_ex"), 1)

            act.wait_ge(s_("ze_ev"), n_("ze_ev", 8))
            attention(FOX)

            def pair(m):
                act.wait_ge(s_("rt_pv"), 2 * m + 2)
                if m >= 1:
                    act.wait_ge(s_("rt_mu"), m)
                    act.wait_ge(s_("rt_cen"), m)
                act.activation(scr[:, 0, :], SB[m % 2][:, :], ACT.Copy).then_inc(s_("rt_oc"), 1)
                act.wait_ge(s_("rt_oc"), own(s_("rt_oc")))

            def pair_stats(m):
                act.wait_ge(s_("rt_cen"), m + 1)
                if m >= 1:
                    act.wait_ge(s_("rt_var"), m)
                act.activation(scr[:, 2, :], scr[:, 1, :], ACT.Square).then_inc(s_("rt_sq"), 1)
                act.wait_ge(s_("rt_sq"), own(s_("rt_sq")))
                act.wait_ge(s_("rt_var"), m + 1)
                if m >= 1:
                    act.wait_ge(s_("yr"), m)
                act.activation(scr[:, 3, :], SB[3][:, :], ACT.Ln, bias=eps[:, 2:3]).then_inc(act_chain, 1)
                act.wait_ge(act_chain, own(act_chain))
                act.activation(scr[:, 3, :], scr[:, 3, :], ACT.Exp, scale=-0.5).then_inc(s_("rt_rs"), 1)
                act.wait_ge(s_("rt_rs"), own(s_("rt_rs")))

            for h in range(8):
                for j in range(TT):
                    act.wait_ge(s_("rt_sc"), 4 * h + j + 1)
                    if h >= 2:
                        act.wait_ge(s_("rt_pv"), h - 1)
                    act.activation(pT(h)[:, j, j * P:], SA[j][:, j * P:], ACT.Copy).then_inc(s_("rt_ea"), 1)
                    act.wait_ge(s_("rt_ea"), own(s_("rt_ea")))
                if h % 2 == 0 and h >= 2:
                    pair(h // 2 - 1)
                if h % 2 == 1 and h >= 3:
                    pair_stats((h - 3) // 2)
            pair(3)
            pair_stats(3)
            for t in range(TT):
                squares("rms_o", t)
                rstd("rms_o", "rms", t)
            turned("rms_o", SB)

            for x, name in enumerate(("kc", "vc")):
                for m in range(2):
                    act.wait_ge(s_(name + "_mm"), n_(name + "_mm", m + 1))
                    bank = (SA, SB)[x][m]
                    for o in range(2):
                        r = slice(o * HD, o * HD + HD)
                        act.activation(a2[x][0:HD, 2 * m + o, :], bank[r, :], ACT.Copy)
                        ins = act.activation(a2[x][HD:P, 2 * m + o, 0:SEQ - 1], bank[r, 1:SEQ], ACT.Copy)
                    ins.then_inc(s_(name + "_ev"), 1)
                    act.wait_ge(s_(name + "_ev"), own(s_(name + "_ev")))
            for x in range(2):
                act.wait_ge(s_(("ck_mm", "cv_mm")[x]), n_(("ck_mm", "cv_mm")[x], 2))
                for m in range(2):
                    c = 2 * x + m
                    banks = (SA, SB)[x]
                    act.activation(hbias[:, c:c + 1], banks[2 + m][:, 0:1], ACT.Copy).then_inc(act_chain, 1)
                    act.wait_ge(act_chain, own(act_chain))
                    act.activation(hsig[:, 128 * c:128 * c + NG * NC], banks[m][:, 0:NG * NC], ACT.Sigmoid,
                                   bias=hbias[:, c:c + 1]).then_inc(s_("hid_sg"), 1)
                    act.wait_ge(s_("hid_sg"), own(s_("hid_sg")))
            act.wait_ge(s_("cmp_mm"), n_("cmp_mm", 1))
            act.activation(kcmp, SA[2][:, 0:NG * NC], ACT.Copy).then_inc(s_("cmp_ev"), 1)
            act.wait_ge(s_("cmp_ev"), own(s_("cmp_ev")))
            act.wait_ge(s_("cmp_mm"), n_("cmp_mm", 2))
            act.activation(vcmp, SB[2][0:NC, 0:256], ACT.Copy).then_inc(s_("cmp_ev"), 1)
            act.wait_ge(s_("cmp_ev"), own(s_("cmp_ev")))
            for x, name in enumerate(("ks", "kw")):
                for m in range(2):
                    act.wait_ge(s_(name + "_mm"), n_(name + "_mm", m + 1))
                    for o in range(2):
                        r = slice(o * HD, o * HD + HD)
                        act.activation(kdup[x][0:HD, 2 * m + o, :], (SA, SB)[x][m][r, :], ACT.Copy)
                        ins = act.activation(kdup[x][HD:P, 2 * m + o, :], (SA, SB)[x][m][r, :], ACT.Copy)
                    ins.then_inc(s_(name + "_ev"), 1)
                    act.wait_ge(s_(name + "_ev"), own(s_(name + "_ev")))
            for x, name in enumerate(("vs", "vw")):
                for t in range(TT):
                    ev(name, t, vtok[:, t, x * 256:x * 256 + 256], bank=(SA, SB)[x][t][:, 0:256])
            for m in range(8):
                ev("qo", m, slab[0][:, m, :], bank=SB[m % 4][:, :], scale=-HD ** -0.5)
            for t in range(TT):
                act.wait_ge(s_("gl_ev"), n_("gl_ev", t + 1))
                act.activation(gates[:, t, :], gates[:, t, :], ACT.Sigmoid).then_inc(s_("gate"), 1)
                act.wait_ge(s_("gate"), own(s_("gate")))
            for m in range(8):
                act.wait_ge(s_("zo_mm"), n_("zo_mm", m + 1))
                if m >= 2:
                    act.wait_ge(s_("zo_ev"), n_("zo_ev", m - 1))
                act.activation(scr[:, m % 2, :], SA[m % 4][:, :], ACT.Sigmoid).then_inc(s_("zo_sg"), 1)
                act.wait_ge(s_("zo_sg"), own(s_("zo_sg")))
            for g in range(NG + 1):
                if g < NG:
                    act.wait_ge(s_("cs_d"), g + 1)
                    act.activation(csc[g % 2], csc[g % 2], ACT.Exp, scale=-1.0).then_inc(s_("cs_e"), 1)
                    act.wait_ge(s_("cs_e"), own(s_("cs_e")))
                if g >= 1:
                    for hg in range(4):
                        n = 4 * (g - 1) + hg
                        act.wait_ge(s_("ct_mm"), n + 1)
                        act.activation(pcmp(n), SB[n % 4][0:NC, :], ACT.Copy).then_inc(s_("ct_ev"), 1)
                        act.wait_ge(s_("ct_ev"), own(s_("ct_ev")))
            attention(NSA)
            for t in range(TT):
                squares("rms_f", t)
                rstd("rms_f", "rms", t)

        @block.vector
        def _(dve):
            own = counter()

            def norm(name, kind, gi, dst):
                for i in ([gi, gi + 1] if kind == "ln" else [gi]):
                    dve.wait_ge(gv_in[i % 2], 16 * (i // 2 + 1))
                g = gvec[:, gi % 2, :]
                if kind == "ln":
                    for t in range(TT):
                        st = stat[:, t, 0:12].rearrange("p (a b) -> p a b", a=2)
                        for i in range(2):
                            dve.bn_stats(st[:, i, :], res[:, t, i * 512:(i + 1) * 512]).then_inc(dve_chain, 1)
                            dve.wait_ge(dve_chain, own(dve_chain))
                        dve.bn_aggr(stat[:, t, 15:17], stat[:, t, 0:12]).then_inc(s_(name + "_v"), 1)
                        dve.wait_ge(s_(name + "_v"), own(s_(name + "_v")))
                    for t in range(TT):
                        dve.wait_ge(s_(name + "_v"), n_(name + "_v", t + 1))
                        dve.wait_ge(s_(name + "_r"), n_(name + "_r", t + 1))
                        dve.tensor_scalar(res[:, t, :], res[:, t, :], stat[:, t, 15:16], stat[:, t, 16:17],
                                               ALU.subtract, ALU.mult).then_inc(dve_chain, 1)
                        dve.wait_ge(dve_chain, own(dve_chain))
                        dve.tensor_tensor(res[:, t, :], res[:, t, :], g, ALU.mult).then_inc(dve_chain, 1)
                        dve.wait_ge(dve_chain, own(dve_chain))
                        ins = dve.tensor_tensor(res[:, t, :], res[:, t, :], gvec[:, (gi + 1) % 2, :], ALU.add)
                        ins.then_inc(s_(name + "_y"), 1)
                        dve.wait_ge(s_(name + "_y"), own(s_(name + "_y")))
                    dve.wait_ge(s_(name + "_y"), n_(name + "_y", TT))
                    dve.sem_inc(gv_used, 2)
                else:
                    for t in range(TT):
                        dve.wait_ge(s_(name + "_r"), n_(name + "_r", t + 1))
                        dve.scalar_tensor_tensor(dst[:, t, :], res[:, t, :], stat[:, t, 16:17], g,
                                                 ALU.mult, ALU.mult).then_inc(s_(name + "_y"), 1)
                        dve.wait_ge(s_(name + "_y"), own(s_(name + "_y")))
                    dve.wait_ge(s_(name + "_y"), n_(name + "_y", TT))
                    dve.sem_inc(gv_used, 1)

            def add_into(name, banks, alpha, done=None):
                for n in range(16):
                    s, t = divmod(n, TT)
                    dve.wait_ge(s_(name + "_mm"), n_(name + "_mm", n + 1))
                    r = res[:, t, s * SLOTW:(s + 1) * SLOTW]
                    ins = dve.scalar_tensor_tensor(r, r, alpha, banks[n % 4][:, 0:SLOTW], ALU.mult, ALU.add)
                    ins.then_inc(s_(name + "_ev"), 1)
                    dve.wait_ge(s_(name + "_ev"), own(s_(name + "_ev")))
                dve.wait_ge(s_(name + "_ev"), n_(name + "_ev", 16))
                if done:
                    dve.sem_inc(s_(done), TT)

            dve.memset(pads[:, 0:4 * PADW], 0.0).then_inc(s_("pads"), 1)
            dve.wait_ge(s_("pads"), own(s_("pads")))
            dve.wait_ge(consts_in, NCONST)
            mx, l0, l1 = lbt[:, 0, :], lbt[:, 1, :], lbt[:, 2, :]
            dve.tensor_tensor(mx, lbl[:, 0, :], lbl[:, 1, :], ALU.max).then_inc(dve_chain, 1)
            dve.wait_ge(dve_chain, own(dve_chain))
            dve.tensor_tensor(l0, lbl[:, 0, :], mx, ALU.subtract).then_inc(dve_chain, 1)
            dve.wait_ge(dve_chain, own(dve_chain))
            dve.tensor_tensor(l1, lbl[:, 1, :], mx, ALU.subtract).then_inc(s_("lb_d"), 1)
            dve.wait_ge(s_("lb_d"), own(s_("lb_d")))
            dve.wait_ge(s_("pads"), 1)
            for m in range(8):
                g = m // 2
                dve.wait_ge(s_("pool_ev"), n_("pool_ev", m + 1))
                v = vpad[m % 2]
                cur = v
                for j in range(g + 1):
                    d = 1 << j
                    dst = wpad[j % 2]
                    dve.tensor_tensor(dst[:, CH:], cur[:, CH:], cur[:, CH - d:PADW - d], ALU.add).then_inc(dve_chain, 1)
                    dve.wait_ge(dve_chain, own(dve_chain))
                    cur = dst
                dve.tensor_tensor(cur[:, CH:2 * CH], cur[:, CH:2 * CH], edge[:, g, :], ALU.mult).then_inc(dve_chain, 1)
                dve.wait_ge(dve_chain, own(dve_chain))
                dve.scalar_tensor_tensor(pooledT[:, m, :], cur[:, CH:], 0.5 ** (g + 1), v[:, CH:], ALU.mult,
                                         ALU.subtract).then_inc(s_("pooled"), 1)
                dve.wait_ge(s_("pooled"), own(s_("pooled")))
            for m in range(8):
                dve.wait_ge(s_("wp_mm"), n_("wp_mm", m + 1))
                dve.wait_ge(s_("gb_ev"), n_("gb_ev", m + 1))
                dve.scalar_tensor_tensor(mixT[:, m, :], SA[m % 4][:, :], psc[:, m:m + 1], mixT[:, m, :], ALU.mult,
                                         ALU.mult).then_inc(s_("wp_ev"), 1)
                dve.wait_ge(s_("wp_ev"), own(s_("wp_ev")))
            for m in range(8):
                dve.wait_ge(s_("q_sg"), m + 1)
                dve.scalar_tensor_tensor(qT[:, m, :], SA[m % 4][:, :], float(P) ** -0.5, scr[:, m % 2, :], ALU.mult,
                                         ALU.mult).then_inc(s_("q_ev"), 1)
                dve.wait_ge(s_("q_ev"), own(s_("q_ev")))
            dve.wait_ge(s_("lb_e"), 2)
            dve.tensor_tensor(mx, l0, l1, ALU.add).then_inc(dve_chain, 1)
            dve.wait_ge(dve_chain, own(dve_chain))
            dve.reciprocal(mx, mx).then_inc(dve_chain, 1)
            dve.wait_ge(dve_chain, own(dve_chain))
            dve.tensor_tensor(lbt[:, 3, :], l0, mx, ALU.mult).then_inc(dve_chain, 1)
            dve.wait_ge(dve_chain, own(dve_chain))
            dve.tensor_scalar(lbt[:, 4, :], lbt[:, 3, :], -1.0, 1.0, ALU.mult, ALU.add).then_inc(dve_chain, 1)
            dve.wait_ge(dve_chain, own(dve_chain))
            dve.tensor_scalar(lbt[:, 0, :], lbt[:, 4, :], -1.0, None, ALU.mult).then_inc(s_("lb"), 1)
            dve.wait_ge(s_("lb"), own(s_("lb")))
            dve.wait_ge(s_("lb"), 1)
            dve.memset(mulq[:, :, :], 1.0).then_inc(dve_chain, 1)
            dve.wait_ge(dve_chain, own(dve_chain))
            dve.memset(mulk[:, :, :], 1.0).then_inc(dve_chain, 1)
            dve.wait_ge(dve_chain, own(dve_chain))
            dve.wait_ge(s_("wp_mm"), n_("wp_mm", 8))
            dve.memset(prob[:, :, :], 0.0).then_inc(dve_chain, 1)
            dve.wait_ge(dve_chain, own(dve_chain))

            def hgrn_levels(h):
                b = h % 2
                K = [side[:, 9 * b + i, :] for i in range(5)]
                Q = [qT[:, h, :]] + [side[:, 9 * b + 5 + i, :] for i in range(4)]

                def by(x, n):
                    return x.rearrange("p (s w) -> p s w", s=n)

                def wide(x, n, w):
                    return x.unsqueeze(2).to_broadcast([P, n, w])

                dve.wait_ge(s_("hg_lf"), n_("hg_lf", h + 1))
                if h >= 1:
                    dve.wait_ge(s_("hg_e"), 2 * h)
                dve.tensor_tensor_scan(scr[:, 1, :], segment[:, :], scr[:, 0, :], 0.0, ALU.mult, ALU.add).then_inc(s_("hg_G"), 1)
                dve.wait_ge(s_("hg_G"), own(s_("hg_G")))
                dve.tensor_scalar(kT[:, h, :], kT[:, h, :], lbt[:, 0, h:h + 1], lbt[:, 4, h:h + 1], ALU.mult, ALU.add).then_inc(dve_chain, 1)
                dve.wait_ge(dve_chain, own(dve_chain))
                dve.wait_ge(s_("hg_e"), 2 * h + 2)
                dve.tensor_copy(segdec[:, 0, :], by(scr[:, 2, :], 32)[:, :, CH - 1]).then_inc(dve_chain, 1)
                dve.wait_ge(dve_chain, own(dve_chain))
                dve.tensor_tensor(Q[0], Q[0], scr[:, 2, :], ALU.mult).then_inc(dve_chain, 1)
                dve.wait_ge(dve_chain, own(dve_chain))
                ins = dve.tensor_tensor(kT[:, h, :], kT[:, h, :], scr[:, 0, :], ALU.mult)
                ins.then_inc(s_("hg_lv"), 1)
                dve.wait_ge(s_("hg_lv"), own(s_("hg_lv")))
                dve.wait_ge(s_("hg_lv"), 6 * h + 1)
                dve.sem_inc(s_("hg_k1"), 1)
                if h >= 2:
                    dve.wait_ge(s_("hg_lvl"), 6 * (h - 1))
                dve.tensor_tensor(by(K[0], 32), by(kT[:, h, :], 32), wide(segdec[:, 0, :], 32, CH), ALU.mult)\
                    .then_inc(s_("hg_lv"), 1)
                dve.wait_ge(s_("hg_lv"), own(s_("hg_lv")))
                dve.wait_ge(s_("hg_lv"), 6 * h + 2)
                for l in range(4):
                    n, w = 32 >> l, CH << l
                    seg = segdec[:, l, 0:n].rearrange("p (i o) -> p i o", o=2)
                    mq = mulq[:, l, 0:n].rearrange("p (i o) -> p i o", o=2)
                    mk = mulk[:, l, 0:n].rearrange("p (i o) -> p i o", o=2)
                    dve.tensor_copy(mq[:, :, 1], seg[:, :, 0])
                    if l < 3:
                        dve.tensor_tensor(segdec[:, l + 1, 0:n // 2], seg[:, :, 0], seg[:, :, 1], ALU.mult)
                    dve.tensor_copy(mk[:, :, 0], seg[:, :, 1]).then_inc(dve_chain, 1)
                    dve.wait_ge(dve_chain, own(dve_chain))
                    if l < 3:
                        dve.tensor_tensor(by(Q[l + 1], n), by(Q[l], n), wide(mulq[:, l, 0:n], n, w), ALU.mult)
                        ins = dve.tensor_tensor(by(K[l + 1], n), by(K[l], n), wide(mulk[:, l, 0:n], n, w), ALU.mult)
                    else:
                        dve.tensor_tensor(by(Q[4], 4)[:, 2:4, :], by(Q[3], 4)[:, 2:4, :], wide(mulq[:, 3, 2:4], 2, w), ALU.mult)
                        ins = dve.tensor_tensor(by(K[4], 4)[:, 0:2, :], by(K[3], 4)[:, 0:2, :], wide(mulk[:, 3, 0:2], 2, w), ALU.mult)
                    ins.then_inc(s_("hg_lv"), 1)
                    dve.wait_ge(s_("hg_lv"), own(s_("hg_lv")))
                    dve.wait_ge(s_("hg_lv"), 6 * h + 3 + l)

            def hgrn_masks(h):
                p0 = 4 * (h % 2)
                for i in range(3):
                    r = 6 * h + i
                    dve.wait_ge(s_("hg_lvl"), r + 1)
                    if h >= 2:
                        dve.wait_ge(s_("hg_pv"), h - 1)
                    dve.copy_predicated(diag(prob[:, p0:p0 + 4, :].rearrange("p j n -> p (j n)"), 0, P),
                                        levels[:, i, :].unsqueeze(1).to_broadcast([P, 4, P]),
                                        SA[r % 4][:, :].rearrange("p (j n) -> p j n", j=4)).then_inc(s_("hg_evd"), 1)
                    dve.wait_ge(s_("hg_evd"), own(s_("hg_evd")))
                    dve.wait_ge(s_("hg_evd"), r - 3 * h + 1)

            def hgrn_out(h):
                dve.wait_ge(s_("hg_rs"), h + 1)
                dve.scalar_tensor_tensor(qT[:, h, :], SB[0][:, :], ng[:, h:h + 1], scr[:, 5, :], ALU.mult, ALU.mult)\
                    .then_inc(s_("hg_o"), 1)
                dve.wait_ge(s_("hg_o"), own(s_("hg_o")))

            for h in range(HEADS_H + 2):
                if 1 <= h <= HEADS_H:
                    hgrn_masks(h - 1)
                if h < HEADS_H:
                    hgrn_levels(h)
                if h >= 2:
                    hgrn_out(h - 2)
            for h in range(HEADS_H):
                dve.wait_ge(s_("og_sg"), h + 1)
                dve.wait_ge(s_("hg_o"), h + 1)
                dve.tensor_tensor(gateT[:, h, :], gateT[:, h, :], qT[:, h, :], ALU.mult).then_inc(s_("gated"), 1)
                dve.wait_ge(s_("gated"), own(s_("gated")))
            for m in range(8):
                dve.wait_ge(s_("wa_mm"), n_("wa_mm", m + 1))
                dve.wait_ge(s_("ga_ev"), n_("ga_ev", m + 1))
                dve.tensor_tensor(kT[:, m, :], SB[m % 4][:, :], kT[:, m, :], ALU.mult).then_inc(dve_chain, 1)
                dve.wait_ge(dve_chain, own(dve_chain))
                dve.tensor_tensor(mixT[:, m, :], mixT[:, m, :], kT[:, m, :], ALU.add).then_inc(s_("wa_ev"), 1)
                dve.wait_ge(s_("wa_ev"), own(s_("wa_ev")))
            dve.wait_ge(s_("x_again"), 16 * TT)
            add_into("o1", SA, ALPHA)
            norm("ln1", "ln", 0, res)
            for b in range(4):
                for m in range(8):
                    dve.wait_ge(s_(f"up{b}_ev"), n_(f"up{b}_ev", m + 1))
                    if m == 0 and b >= 2:
                        dve.wait_ge(s_(f"dn{b - 2}_mm"), n_(f"dn{b - 2}_mm", 16))
                    dve.tensor_tensor(slab[2 * (b % 2)][:, m, :], scr[:, m % 2, :], scr[:, m % 2, :], ALU.mult)\
                        .then_inc(s_(f"hid{b}"), 1)
                    dve.wait_ge(s_(f"hid{b}"), own(s_(f"hid{b}")))
                if b == 0:
                    dve.wait_ge(s_("ln1_mm"), n_("ln1_mm", 8))
                add_into(f"dn{b}", SB, ALPHA if b == 0 else 1.0)
            norm("ln2", "ln", 2, res)
            dve.wait_ge(s_("ln2_y"), TT)
            dve.sem_inc(s_("rms_e_x"), TT)
            norm("rms_e", "rms", 4, normed)

            def decayed(name, banks, o):
                for m in range(4):
                    dve.wait_ge(s_(name + "_mm"), n_(name + "_mm", m + 1))
                    dve.tensor_tensor(slab[1][:, o + m, :], banks[m][:, :], slab[3][:, o + m, :], ALU.mult)\
                        .then_inc(s_(name + "_ev"), 1)
                    dve.wait_ge(s_(name + "_ev"), own(s_(name + "_ev")))

            dve.wait_ge(s_("decay_in"), 32)
            decayed("qr", SB, 0)
            decayed("kr", SA, 4)
            dve.wait_ge(s_("fl_ln"), 1)
            dve.memset(frow[3], 1.0).then_inc(dve_chain, 1)
            dve.wait_ge(dve_chain, own(dve_chain))
            dve.scalar_tensor_tensor(frow[2], frow[0], 0.0, frow[1], ALU.min, ALU.subtract).then_inc(dve_chain, 1)
            dve.wait_ge(dve_chain, own(dve_chain))
            dve.tensor_tensor_scan(frow[4], frow[3], frow[2], 0.0, ALU.mult, ALU.add).then_inc(s_("frow"), 1)
            dve.wait_ge(s_("frow"), own(s_("frow")))

            def silu(name, dst):
                for m in range(8):
                    dve.wait_ge(s_(name + "_sg"), n_(name + "_sg", m + 1))
                    dve.tensor_tensor(dst[:, m, :], SA[m % 4][:, :], scr[:, m % 2, :], ALU.mult).then_inc(s_(name + "_ev"), 1)
                    dve.wait_ge(s_(name + "_ev"), own(s_(name + "_ev")))

            silu("ze", slab[5])

            def attention(A):
                n, steps, N = A.name, A.steps, len(A.steps)
                for i in range(N + 1):
                    if i < N:
                        h, b, t = steps[i]
                        w = (t + 1) * P
                        if n == "nsa" and b == 0 and t == 0:
                            dve.tensor_scalar(scr[:, 4 + h % 2, :], dist, SLOPE[h], None, ALU.mult).then_inc(dve_chain, 1)
                            dve.wait_ge(dve_chain, own(dve_chain))
                        dve.wait_ge(s_(n + "_sc"), i + 1)
                        if n == "fox":
                            dve.wait_ge(s_("fox_cb"), h + 1)
                            bias = scr[:, 4 + h % 2, 0:w]
                        else:
                            bias = scr[:, 4 + h % 2, SEQ - w:]
                        if i >= SCR_S:
                            dve.wait_ge(s_(n + "_tp"), i - SCR_S + 1)
                        dve.tensor_tensor_reduce(scr[:, i % SCR_S, 0:w], ps[i % 3][:, 0:w], bias, 1.0, 3e38, ALU.add,
                                                 ALU.min, tmin[:, i % 8:i % 8 + 1]).then_inc(s_(n + "_dm"), 1)
                    if i >= 1:
                        s = i - 1
                        h, b, t = steps[s]
                        w = (t + 1) * P
                        dve.wait_ge(s_(n + "_ex"), s + 1)
                        c = slice(s % 8, s % 8 + 1)
                        dve.reciprocal(trec[:, c], tsum[:, c]).then_inc(dve_chain, 1)
                        dve.wait_ge(dve_chain, own(dve_chain))
                        pr = scr[:, s % SCR_S, 0:w]
                        if n == "fox":
                            ins = dve.tensor_scalar(pr, pr, trec[:, c], None, ALU.mult)
                        else:
                            ins = dve.tensor_scalar(pr, pr, trec[:, c], gates[:, t, 3 * h + 1 + b:3 * h + 2 + b], ALU.mult, ALU.mult)
                        ins.then_inc(s_(n + "_pn"), 1)
                    per = 8 * A.branches
                    if i >= 8 and (i - 8) % per == per - 1:
                        pair_out(A, (i - 8) // per)
                pair_out(A, A.heads // 2 - 1)

            def pair_out(A, m):
                n = A.name
                dve.wait_ge(s_(n + "_pv"), 2 * A.branches * (m + 1))
                ob = OB[0 if n == "fox" else m % 2]
                dve.tensor_tensor(A.y(m), ob[:, :], slab[5][:, m, :], ALU.mult).then_inc(s_(n + "_y"), 1)
                dve.wait_ge(s_(n + "_y"), own(s_(n + "_y")))

            attention(FOX)
            for h in range(8):
                for j in range(TT):
                    dve.wait_ge(s_("rt_ea"), 4 * h + j + 1)
                    dve.tensor_tensor(pT(h)[:, j, j * P:(j + 1) * P], pT(h)[:, j, j * P:(j + 1) * P], tril[:, :], ALU.mult)\
                        .then_inc(s_("rt_ed"), 1)
                    dve.wait_ge(s_("rt_ed"), own(s_("rt_ed")))
                if h % 2 == 1 and h >= 3:
                    ret_out = (h - 3) // 2
                    dve.wait_ge(s_("rt_mu"), ret_out + 1)
                    dve.tensor_tensor(scr[:, 1, :], scr[:, 0, :], SB[2][:, :], ALU.subtract).then_inc(s_("rt_cen"), 1)
                    dve.wait_ge(s_("rt_cen"), own(s_("rt_cen")))
                    dve.wait_ge(s_("rt_rs"), ret_out + 1)
                    dve.scalar_tensor_tensor(scr[:, 4, :], scr[:, 1, :], gng[:, ret_out:ret_out + 1], scr[:, 3, :], ALU.mult, ALU.mult).then_inc(dve_chain, 1)
                    dve.wait_ge(dve_chain, own(dve_chain))
                    dve.tensor_tensor(slab[2][:, 4 + ret_out, :], scr[:, 4, :], slab[5][:, 4 + ret_out, :], ALU.mult)\
                        .then_inc(s_("yr"), 1)
                    dve.wait_ge(s_("yr"), own(s_("yr")))
            ret_out = 3
            dve.wait_ge(s_("rt_mu"), ret_out + 1)
            dve.tensor_tensor(scr[:, 1, :], scr[:, 0, :], SB[2][:, :], ALU.subtract).then_inc(s_("rt_cen"), 1)
            dve.wait_ge(s_("rt_cen"), own(s_("rt_cen")))
            dve.wait_ge(s_("rt_rs"), ret_out + 1)
            dve.scalar_tensor_tensor(scr[:, 4, :], scr[:, 1, :], gng[:, ret_out:ret_out + 1], scr[:, 3, :], ALU.mult, ALU.mult).then_inc(dve_chain, 1)
            dve.wait_ge(dve_chain, own(dve_chain))
            dve.tensor_tensor(slab[2][:, 4 + ret_out, :], scr[:, 4, :], slab[5][:, 4 + ret_out, :], ALU.mult)\
                .then_inc(s_("yr"), 1)
            dve.wait_ge(s_("yr"), own(s_("yr")))
            add_into("oe", SA, 1.0, done="rms_o_x")
            norm("rms_o", "rms", 5, normed)

            for x in range(2):
                for m in range(2):
                    c = 2 * x + m
                    dve.wait_ge(s_("hid_sg"), c + 1)
                    dve.scalar_tensor_tensor(hid[x][:, m, :], (SA, SB)[x][m][:, 0:NG * NC], hbias[:, c:c + 1],
                                             hsig[:, 128 * c:128 * c + NG * NC], ALU.add, ALU.mult).then_inc(s_(("hid_k", "hid_v")[x]), 1)
                    dve.wait_ge(s_(("hid_k", "hid_v")[x]), own(s_(("hid_k", "hid_v")[x])))
            for t in range(TT):
                dve.wait_ge(s_("gl_mm"), n_("gl_mm", t + 1))
                dve.tensor_tensor(gates[:, t, :], SA[t][:, 0:48], bgate[:, :], ALU.add).then_inc(s_("gl_ev"), 1)
                dve.wait_ge(s_("gl_ev"), own(s_("gl_ev")))
            silu("zo", slab[5])

            dve.wait_ge(s_("gate"), TT)
            for g in range(NG):
                b = g % 2
                x3 = csc[b].rearrange("p (a n) -> p a n", n=NC)
                if g >= 2:
                    dve.wait_ge(s_("ct_mm"), 4 * (g - 1))
                dve.wait_ge(s_("cs_mm"), g + 1)
                for hg in range(4):
                    c = slice(hg * TT * NC, (hg + 1) * TT * NC)
                    dve.scalar_tensor_tensor(csc[b][:, c], cdist, SLOPE[4 * g + hg],
                                             SA[2 * b + hg % 2][:, hg // 2 * TT * NC:(hg // 2 + 1) * TT * NC], ALU.mult, ALU.add)\
                        .then_inc(s_("cs_ev"), 1)
                    dve.wait_ge(s_("cs_ev"), own(s_("cs_ev")))
                dve.wait_ge(s_("cs_ev"), 4 * g + 4)
                mn, sm, rc = csmall[:, 0, :], csmall[:, 1, :], csmall[:, 2, :]
                dve.tensor_reduce(mn, x3, AX_X, ALU.min).then_inc(dve_chain, 1)
                dve.wait_ge(dve_chain, own(dve_chain))
                dve.tensor_tensor(x3, x3, mn.unsqueeze(2).to_broadcast([P, 16, NC]), ALU.subtract).then_inc(s_("cs_d"), 1)
                dve.wait_ge(s_("cs_d"), own(s_("cs_d")))
                dve.wait_ge(s_("cs_e"), g + 1)
                dve.tensor_reduce(sm, x3, AX_X, ALU.add).then_inc(dve_chain, 1)
                dve.wait_ge(dve_chain, own(dve_chain))
                dve.reciprocal(rc, sm).then_inc(dve_chain, 1)
                dve.wait_ge(dve_chain, own(dve_chain))
                gt = gates[:, :, :].rearrange("p t (h b) -> p b h t", b=3)[:, 0, 4 * g:4 * g + 4, :]
                dve.tensor_tensor(rc.rearrange("p (h t) -> p h t", h=4), rc.rearrange("p (h t) -> p h t", h=4), gt, ALU.mult).then_inc(dve_chain, 1)
                dve.wait_ge(dve_chain, own(dve_chain))
                dve.tensor_tensor(x3, x3, rc.unsqueeze(2).to_broadcast([P, 16, NC]), ALU.mult).then_inc(dve_chain, 1)
                dve.wait_ge(dve_chain, own(dve_chain))
                x4 = csc[b].rearrange("p (h n) -> p h n", h=4)
                dve.tensor_tensor(x4, x4, cmask.unsqueeze(1).to_broadcast([P, 4, TT * NC]), ALU.mult).then_inc(s_("cs_p"), 1)
                dve.wait_ge(s_("cs_p"), own(s_("cs_p")))
            attention(NSA)
            add_into("oo", SA, 1.0, done="rms_f_x")
            norm("rms_f", "rms", 6, res)


_INS = {
    "x": None, "w_in": None, "lb_logits": None, "hgrn_norm_g": None, "w_a": None, "w_pool": None, "pool_scale": None,
    "w_out": None, "ln1_g": None, "ln1_b": None, "w_up": None, "w_down": None, "ln2_g": None, "ln2_b": None,
    "even_norm_g_2": None, "even_w_in_2": None, "even_b_f_2": None, "even_gn_g_2": None, "even_w_out_2": None,
    "odd_norm_g_2": None, "odd_w_in_2": None, "odd_b_gate_2": None, "odd_pe_k_2": None, "odd_pe_v_2": None,
    "odd_wk1_2": None, "odd_wk2_2": None, "odd_wv1_2": None, "odd_wv2_2": None, "odd_w_out_2": None, "final_g_2": None,
}


def kernel(**inputs):
    import numpy as _np
    import concourse.bacc as _bacc
    from concourse import mybir as _mybir
    from concourse.bass_utils import run_bass_kernel_spmd as _run

    nc = _bacc.Bacc("TRN2", target_bir_lowering=False, num_devices=1)
    arrays, args = {}, {}
    for name in _INS:
        a = _np.ascontiguousarray(inputs[name])
        arrays[f"in_{name}"] = a
        args[name] = nc.dram_tensor(f"in_{name}", a.shape, _mybir.dt.from_np(a.dtype), kind="ExternalInput").ap()
    out = nc.dram_tensor("result", (1, SEQ, DM), F32, kind="ExternalOutput").ap()
    build(nc, args, out)
    r = _run(nc, [arrays], core_ids=[0])
    return r.results[0]["result"]
```

```python
from contextlib import ExitStack

import numpy as np
import concourse.bass as bass
from concourse import mybir

F32 = mybir.dt.float32
U32 = mybir.dt.uint32
F16 = mybir.dt.float16
ALU = mybir.AluOpType
ACT = mybir.ActivationFunctionType
AX_X = mybir.AxisListType.X
RMAX = bass.bass_isa.ReduceOp.max

P = 128
SEQ = 512
DM = 1024
TT = SEQ // P
KC = DM // P
SLOTW = 256
NSLOT = 3
NHIGH = 2
EXPONENT = 0x7F800000
TOP = 2.0 ** 14
LEAST = 2.0 ** -100
HEADS_H = 8
CH = 16
D_FF = 4 * DM
HD = 64
NH = 16
NG = 4
NC = 31
LN_EPS = 1e-5
RMS_EPS = 1e-6
GN_EPS = 1e-5
ALPHA = 2.0 ** 0.25
BIG = 1e30


def constants():
    p = np.arange(P)
    c = {}
    c["ident"] = np.eye(P, dtype=np.float32)
    c["ones"] = np.ones((P, P), np.float32)
    c["half_mean"] = np.kron(np.eye(2), np.full((HD, HD), 1.0 / HD)).astype(np.float32)
    s, t = p[:, None], p[None, :]
    lv = [(s // CH == t // CH) & (s <= t)]
    for h in (16, 32):
        lv.append((s // (2 * h) == t // (2 * h)) & (s % (2 * h) < h) & (t % (2 * h) >= h))
    c["levels"] = np.stack(lv, 1).astype(np.uint32).reshape(P, 3 * P)
    c["tril_st"] = (s <= t).astype(np.float32)
    c["ahead"] = np.where(t > s, BIG, 0.0).astype(np.float32)
    r = np.arange(SEQ)[None, :] - (SEQ - P)
    c["dist"] = np.where(r <= s, s - r, 1e32).astype(np.float32)
    end = np.arange(NC) * 16 + 31
    tok = (np.arange(TT)[None, :] * P + p[:, None])[:, :, None]
    c["cdist"] = np.where(end <= tok, tok - end, 1e32).astype(np.float32).reshape(P, TT * NC)
    c["cmask"] = (end <= tok).astype(np.float32).reshape(P, TT * NC)
    c["segment"] = np.broadcast_to((np.arange(SEQ) % CH != 0).astype(np.float32), (P, SEQ)).copy()
    rc = np.stack([w / np.minimum(np.arange(CH) + 1, w) for w in (2, 4, 8, 16)])
    c["edge"] = np.broadcast_to(rc.reshape(1, 4 * CH), (P, 4 * CH)).astype(np.float32).copy()
    sel = np.zeros((8, 8, P), np.float32)
    for h in range(8):
        sel[h, h] = 1.0
    c["sel"] = sel.reshape(8, 8 * P)
    c["eps"] = np.tile(np.array([LN_EPS, RMS_EPS, GN_EPS, 1.0], np.float32), (P, 1))
    lg = np.log(1.0 - 2.0 ** (-5.0 - np.arange(8)))
    pos = np.arange(SEQ)
    up = np.exp(lg[:, None] * pos[None, :])
    dn = np.exp(-lg[:, None] * pos[None, :]) * HD ** -0.5
    both = np.stack([up, dn])
    d = np.repeat(both.reshape(2, 4, 2, 1, SEQ), HD, axis=3)
    c["decay"] = d.reshape(2, 4, P, SEQ).transpose(2, 0, 1, 3).reshape(P, 8 * SEQ).astype(np.float32)
    return c


def diag(flat, first, width):
    step = SEQ + P
    x = flat[:, 0:3 * step + P]
    return bass.AP(tensor=x.tensor, offset=x.offset + first, ap=[list(x.ap[0]), [step, TT], [1, width]])


def slopes():
    return [float(np.float32(2.0 ** (-8.0 * (h + 1) / NH))) for h in range(NH)]


def build(nc, a, out):
    con = constants()
    cd = {k: nc.inline_tensor(v, name=f"const_{k}").ap() for k, v in con.items()}
    ctx = ExitStack()
    with ctx:
        def sb(name, shape, dt=F32):
            return ctx.enter_context(nc.sbuf_tensor(name, shape, dt))

        def sem(name):
            return ctx.enter_context(nc.semaphore(name))

        wring = sb("wring", [P, NSLOT, KC, SLOTW])
        whigh = sb("whigh", [P, NHIGH, KC, SLOTW], F16)
        xT = sb("xT", [P, KC, SEQ])
        slab = [sb(f"slab{i}", [P, 8, SEQ]) for i in range(6)]
        side = sb("side", [P, 18, SEQ])
        res = side[:, 0:8, :].rearrange("p (t h) n -> p t (h n)", t=TT)
        scr = sb("scr", [P, 6, SEQ])
        ident = sb("ident", [P, P])
        ones = sb("ones", [P, P])
        half_mean = sb("half_mean", [P, P])
        tril = sb("tril", [P, P])
        ahead = sb("ahead", [P, P])
        levels = sb("levels", [P, 3, P], U32)
        segment = sb("segment", [P, SEQ])
        edge = sb("edge", [P, 4, CH])
        lbl = sb("lbl", [P, 2, 8])
        lbt = sb("lbt", [P, 5, 8])
        ng = sb("ng", [P, 8])
        psc = sb("psc", [P, 8])
        gng = sb("gng", [P, 4])
        bf_ = sb("bf_", [8, 1])
        bgate = sb("bgate", [P, 48])
        gates = sb("gates", [P, TT, 48])
        eps = sb("eps", [P, 4])
        stat = sb("stat", [P, TT, 20])
        segdec = sb("segdec", [P, 4, 32])
        mulq = sb("mulq", [P, 4, 32])
        mulk = sb("mulk", [P, 4, 32])
        tmin = sb("tmin", [P, 8])
        tsum = sb("tsum", [P, 8])
        trec = sb("trec", [P, 8])
        csmall = sb("csmall", [P, 4, 16])
        hbias = sb("hbias", [P, 4])
        ps = [ctx.enter_context(nc.psum_tensor(f"bank{i}", [P, SEQ], F32)) for i in range(8)]
        SA, SB = ps[0:4], ps[4:8]

        block = ctx.enter_context(nc.Block())

        stream = []

        def cols(w, c0, n=SLOTW):
            return w[:, c0:c0 + n].rearrange("(k p) n -> p k n", p=P)

        def add(key, w, c0, n, tiles=2):
            for i, c in enumerate(range(0, n, SLOTW)):
                m = min(SLOTW, n - c)
                stream.append((key, cols(w, c0 + c, m), m, tiles * (i + 1)))

        W = a["w_in"][0]
        add("pool", W, 4096, 1024)
        add("gb", W, 6144, 1024)
        stream.append(("wp", a["w_pool"][0].rearrange("g (k p) d -> p (g k) d", p=P), SLOTW, 8))
        add("f", W, 1024, 1024)
        add("q", W, 0, 1024)
        add("v", W, 2048, 1024, 4)
        add("og", W, 3072, 1024)
        add("ga", W, 5120, 1024)
        add("wa", a["w_a"][0], 0, 1024)
        add("o1", a["w_out"][0], 0, 1024, 4)
        for b in range(4):
            add(f"up{b}", a["w_up"][0], 1024 * b, 1024)
            add(f"dn{b}", a["w_down"][0][1024 * b:1024 * b + 1024, :], 0, 1024, 4)
        W = a["even_w_in_2"][0]
        add("qf", W, 0, 512)
        add("kf", W, 512, 512)
        add("vf", W, 1024, 512, 4)
        add("fl", W, 1536, 8, 1)
        add("qr", W, 1544, 512)
        add("kr", W, 2056, 512)
        add("vr", W, 2568, 512, 4)
        add("ze", W, 3080, 1024)
        add("oe", a["even_w_out_2"][0], 0, 1024, 4)
        W = a["odd_w_in_2"][0]
        add("kc", W, 1024, 256)
        add("vc", W, 1280, 256)
        for x in "kv":
            for i in range(2):
                stream.append(("c" + x, a[f"odd_w{x}1_2"][0][1024 * i:1024 * i + 1024, :].rearrange("(k p) n -> p k n", p=P), SLOTW, i + 1))
        add("ks", W, 1536, 256)
        add("kw", W, 2048, 256)
        add("vs", W, 1792, 256, 4)
        add("vw", W, 2304, 256, 4)
        add("gl", W, 2560, 48, 4)
        add("qo", W, 0, 1024)
        add("zo", W, 2608, 1024)
        add("oo", a["odd_w_out_2"][0], 0, 1024, 4)

        SPLIT = {"pool", "gb", "f", "q", "v", "og", "ga", "wa", "up0", "up1", "up2", "up3", "qf", "kf", "vf", "fl", "qr",
                 "kr", "vr", "ze", "kc", "vc", "ks", "kw", "vs", "vw", "gl", "qo", "zo"}
        split_slots = [i for i, (key, *_) in enumerate(stream) if key in SPLIT]
        NSPLIT = len(split_slots)
        wexp = sb("wexp", [P, NSPLIT])
        wsc = sb("wsc", [P, NSPLIT])
        winv = sb("winv", [P, NSPLIT])
        INPUTS = ("tr0", "gated", "ln1", "rms_e", "rms_o")
        xexp = sb("xexp", [P, 8])
        xsc = sb("xsc", [P, 8])
        xinv = sb("xinv", [P, 8])
        xmax = sb("xmax", [P, 4])
        invq = sb("invq", [P, 12])

        def input_of(i):
            key = stream[i][0]
            if key in ("pool", "gb", "f", "q", "v", "og", "ga"):
                return 0
            return 1 if key == "wa" else 2 if key[:2] == "up" else 3 if i < first_slot("kc") else 4

        def first_slot(key):
            return [k for k, *_ in stream].index(key)

        def split_index(key, slot=0):
            return split_slots.index(first_slot(key) + slot)

        def undo(key, slot):
            n = split_index(key, slot)
            return winv[:, n:n + 1]

        QSLOTS = {key: at for key, at in (("q", 0), ("qf", 4), ("qo", 6))}

        def undo_q(key, slot):
            c = QSLOTS[key] + slot
            return invq[:, c:c + 1]

        def halves(x):
            y = x.rearrange("p k n -> p (k n)").bitcast(F16).rearrange("p (k h n) -> p k h n", k=8, h=2)
            return y[:, :, 0, :], y[:, :, 1, :]

        consts_in = sem("consts_in")
        NCONST = 0
        w_in = [sem(f"w_in{j}") for j in range(NSLOT)]
        x_in = [sem(f"x_in{t}") for t in range(TT)]
        act_chain = sem("act_chain")
        dve_chain = sem("dve_chain")
        S = {}
        mm_done, act_read, dve_read = sem("mm_done"), sem("act_read"), sem("dve_read")
        mlp = [(f"{x}{b}", n) for b in range(4) for x, n in (("up", 8), ("dn", 16))]
        counted = {}
        for s, kind, stages in (
            (mm_done, "_mm", [("tr0", 8), ("pool", 8), ("gb", 8), ("wp", 8), ("f", 8), ("q", 8), ("v", 16), ("og", 8),
                              ("ga", 8), ("wa", 8), ("o1", 16), ("ln1", 8), *mlp, ("rms_e", 8), ("qf", 4), ("kf", 4),
                              ("vf", 8), ("fl", 1), ("qr", 4), ("kr", 4), ("vr", 8), ("ze", 8), ("oe", 16), ("rms_o", 8),
                              ("kc", 2), ("vc", 2), ("ck", 2), ("cv", 2), ("cmp", 2), ("ks", 2), ("kw", 2), ("vs", 4),
                              ("vw", 4), ("gl", 4), ("qo", 8), ("zo", 8), ("oo", 16)]),
            (act_read, "_ev", [("pool", 8), ("gb", 8), ("f", 8), ("v", 16), ("og", 8), ("ga", 8),
                               *[x for x in mlp if x[0][0] == "u"], ("qf", 4), ("kf", 4), ("vf", 8), ("fl", 1),
                               ("vr", 8), ("kc", 2), ("vc", 2), ("cmp", 2), ("ks", 2), ("kw", 2), ("vs", 4),
                               ("vw", 4), ("qo", 8)]),
            (dve_read, "_ev", [("tr0", 8), ("wp", 8), ("q", 8), ("wa", 8), ("o1", 16), ("ln1", 8),
                               *[x for x in mlp if x[0][0] == "d"], ("rms_e", 8), ("qr", 4),
                               ("kr", 4), ("ze", 8), ("oe", 16), ("rms_o", 8), ("gl", 4), ("zo", 8), ("oo", 16)]),
        ):
            n = 0
            for stage, results in stages:
                counted[stage + kind] = (s, n)
                n += results

        def s_(name):
            if name in counted:
                return counted[name][0]
            if name not in S:
                S[name] = sem(name)
            return S[name]

        def n_(name, n):
            return n + (counted[name][1] if name in counted else 0)

        def counter():
            counts = {}

            def own(s):
                counts[s] = counts.get(s, 0) + 1
                return counts[s]
            return own

        const_loads = [
            (ones[:, :], cd["ones"]), (half_mean[:, :], cd["half_mean"]),
            (tril[:, :], cd["tril_st"]), (ahead[:, :], cd["ahead"]),
            (levels[:, :, :], cd["levels"].rearrange("p (l n) -> p l n", l=3)),
            (segment[:, :], cd["segment"]),
            (edge[:, :, :], cd["edge"].rearrange("p (l n) -> p l n", l=4)),
            (eps[:, :], cd["eps"]),
            (lbl[:, 0, :], a["lb_logits"][0].rearrange("(k p) -> p k", p=P)),
            (lbl[:, 1, :], a["lb_logits"][1].rearrange("(k p) -> p k", p=P)),
            (ng[:, :], a["hgrn_norm_g"][0].rearrange("(k p) -> p k", p=P)),
            (psc[:, :], a["pool_scale"][0].rearrange("(k p) -> p k", p=P)),
            (gng[:, :], a["even_gn_g_2"][0].rearrange("(k p) -> p k", p=P)),
            (bf_[:, :], a["even_b_f_2"][0].rearrange("(k p) -> k p", p=1)),
            (bgate[:, :], a["odd_b_gate_2"].to_broadcast([P, 48])),
        ]
        NCONST = 16 * len(const_loads)

        def bytok(x):
            return x[:, :, :].rearrange("p (t h) n -> p t (h n)", t=TT)

        ident_in = sem("ident_in")
        gain = {
            "ln1": (scr[:, 2:4, :], a["ln1_g"]), "ln1_b": (scr[:, 4:6, :], a["ln1_b"]),
            "ln2": (scr[:, 2:4, :], a["ln2_g"]), "ln2_b": (scr[:, 4:6, :], a["ln2_b"]),
            "rms_e": (slab[1][:, 0:2, :], a["even_norm_g_2"]), "rms_o": (slab[0][:, 0:2, :], a["odd_norm_g_2"]),
            "rms_f": (bytok(slab[4])[:, 2:4, 512:DM], a["final_g_2"].rearrange("(o n) -> o n", o=1)),
        }

        pooledT, mixT, kT, qT, vslab, gateT = slab
        xhalves = halves(xT[:, :, :])
        ghalves = halves(gateT[:, :, :])
        vtok = bytok(vslab)
        prob = slab[0]
        normed = bytok(slab[5])
        pads = side[:, 8:18, :].rearrange("p a n -> p (a n)")
        PADW = SEQ + CH
        vpad = [pads[:, i * PADW:(i + 1) * PADW] for i in (0, 1)]
        wpad = [pads[:, i * PADW:(i + 1) * PADW] for i in (2, 3)]
        frow = [side[0:8, 11 + i, :] for i in range(5)]
        sel = side[0:8, 16:18, :].rearrange("p a (b n) -> p (a b) n", n=P)
        a2 = [slab[2][:, 0:4, :], slab[2][:, 4:8, :]]
        kdup = [slab[3][:, 0:4, :], slab[3][:, 4:8, :]]
        kcmp = vtok[:, 0, 512:512 + NG * NC]
        vcmp = vtok[0:NC, 0, 640:896]
        hid = [vtok[:, 1, 512 + 256 * i:512 + 256 * i + 2 * NG * NC].rearrange("p (m n) -> p m n", m=2) for i in (0, 1)]
        csc = [vtok[:, 2 + i, 512:512 + 16 * NC] for i in (0, 1)]
        hsig = side[:, 11:13, :].rearrange("p a n -> p (a n)")
        dist = side[:, 8, :]
        cdist = side[:, 9, 0:TT * NC]
        cmask = side[:, 9, 256:256 + TT * NC]
        w2 = [side[:, 10, 128 * i:128 * i + 128].rearrange("p (k n) -> p k n", k=2) for i in (0, 1)]
        petab = [side[:, 10, 256 + 16 * i:272 + 16 * i] for i in (0, 1)]

        def pcmp(h):
            return slab[2][0:NC, h, :] if h < 8 else side[0:NC, 2 + h, :]

        SLOPE = slopes()

        class Att:
            def __init__(self, name, heads, branches):
                self.name, self.heads, self.branches = name, heads, branches
                self.steps = [(h, b, t) for h in range(heads) for b in range(branches) for t in range(TT)]

            def q(self, h, t):
                r = h % 2 * HD
                return slab[0][r:r + HD, h // 2, t * P:(t + 1) * P]

            def k(self, h, b, n):
                r = h % 2 * HD
                if self.name == "fox":
                    return slab[0][r:r + HD, 4 + h // 2, 0:n]
                return kdup[b][r:r + HD, h // 4, 0:n]

            def v(self, h, b, j):
                c = h * HD if self.name == "fox" else b * 256 + h // 4 * HD
                return vtok[:, j, c:c + HD]

            def y(self, m):
                return slab[2][:, m, :] if self.name == "fox" else slab[1][:, m, :]

        FOX, NSA = Att("fox", 8, 1), Att("nsa", NH, 2)
        SCR_S = 4
        TPB = ps[3:6]
        OB = ps[6:8]

        def pT(u):
            return xT[:, 4 * (u % 2):4 * (u % 2) + 4, :]

        @block.sync
        def _(sp):
            for t in range(TT):
                sp.dma_start(res[:, t, :], a["x"][0, t * P:(t + 1) * P, :]).then_inc(x_in[t], 16)
                if t == 0:
                    sp.dma_start(ident[:, :], cd["ident"]).then_inc(ident_in, 16)
            for i, (_, src, n, _) in enumerate(stream):
                if i >= NSLOT:
                    key, _, _, results = stream[i - NSLOT]
                    sp.wait_ge(s_(key + "_mm"), n_(key + "_mm", results))
                sp.dma_start(wring[:, i % NSLOT, :, 0:n], src).then_inc(w_in[i % NSLOT], 16)

        @block.gpsimd
        def _(pool):
            def load_gain(name):
                dst, src = gain[name]
                pool.dma_start(dst, src.to_broadcast([P, DM]).rearrange("p (a n) -> p a n", a=2)).then_inc(s_(name + "_gain"), 16)

            pool.wait_ge(s_("x_max"), 1)
            pool.partition_all_reduce(xexp[:, 0:1], xmax[:, 0:1], P, RMAX).then_inc(s_("x_all"), 1)
            for n in range(NSPLIT):
                if n == 2:
                    pool.wait_ge(s_("x_max"), 2)
                    pool.partition_all_reduce(xexp[:, 1:2], xmax[:, 1:2], P, RMAX).then_inc(s_("x_all"), 1)
                if n == split_index("wa", 1):
                    pool.wait_ge(s_("hg_o"), 8)
                    for t in range(TT):
                        pool.dma_start(res[:, t, :], a["x"][0, t * P:(t + 1) * P, :]).then_inc(s_("x_again"), 16)
                    load_gain("ln1")
                    load_gain("ln1_b")
                if n == split_index("up0", 3):
                    pool.wait_ge(s_("ln1_y"), TT)
                    load_gain("ln2")
                    load_gain("ln2_b")
                    pool.wait_ge(s_("o1_mm"), n_("o1_mm", 16))
                    load_gain("rms_e")
                    pool.dma_start(slab[3][:, :, :], cd["decay"].rearrange("p (l n) -> p l n", l=8)).then_inc(s_("decay_in"), 16)
                    pool.dma_start(sel, cd["sel"].rearrange("p (l n) -> p l n", l=8)).then_inc(s_("decay_in"), 16)
                if n == split_index("kc"):
                    pool.wait_ge(s_("fox_pv"), 8)
                    load_gain("rms_o")
                    pool.dma_start(dist, cd["dist"]).then_inc(s_("nsa_in"), 16)
                    pool.dma_start(cdist, cd["cdist"]).then_inc(s_("nsa_in"), 16)
                    pool.dma_start(cmask, cd["cmask"]).then_inc(s_("nsa_in"), 16)
                    for i, x in enumerate("kv"):
                        pool.dma_start(w2[i], a[f"odd_w{x}2_2"][0].rearrange("(k p) n -> p k n", p=P)).then_inc(s_("nsa_in"), 16)
                        for o in range(2):
                            pool.dma_start(petab[i][HD * o:HD * o + HD, :],
                                           a[f"odd_pe_{x}_2"][0].rearrange("(k l) d -> l d k", l=2)[o],
                                           allow_slow_non_contiguous=True).then_inc(s_("nsa_in"), 16)
                pool.wait_ge(s_("w_max"), n + 1)
                pool.partition_all_reduce(wexp[:, n:n + 1], wsc[:, n:n + 1], P, RMAX).then_inc(s_("w_all"), 1)
            pool.wait_ge(s_("ct_mm"), 16)
            load_gain("rms_f")
            for t in range(TT):
                pool.wait_ge(s_("rms_f_y"), t + 1)
                pool.dma_start(out[0, t * P:(t + 1) * P, :], res[:, t, :]).then_inc(s_("stored"), 16)
            pool.wait_ge(s_("stored"), 16 * TT)

        NSA_IN = 9 * 16

        def low_of(i):
            return wring[:, i % NSLOT, :, :].rearrange("p k n -> p (k n)").bitcast(F16)\
                .rearrange("p (k n) -> p k n", k=KC)[:, :, 0:SLOTW]


        @block.tensor
        def _(pe):
            at = [0]

            def slot(key):
                i = at[0]
                assert stream[i][0] == key, (stream[i][0], key)
                at[0] += 1
                if key in SPLIT:
                    n = split_slots.index(i)
                    pe.wait_ge(s_("w_low"), n + 1)
                    return whigh[:, n % NHIGH, :, :], low_of(i)
                pe.wait_ge(w_in[i % NSLOT], 16 * (i // NSLOT + 1))
                return wring[:, i % NSLOT, :, :]

            def feat_tile(name, w, wcol, src, bank, width=P):
                (wh, wl), (xh, xl) = w, src
                for k in range(KC):
                    pe.matmul(bank, wh[:, k, wcol:wcol + width], xh[:, k, :], start=k == 0, stop=False)
                    pe.matmul(bank, wh[:, k, wcol:wcol + width], xl[:, k, :], start=False, stop=False)
                    mm = pe.matmul(bank, wl[:, k, wcol:wcol + width], xh[:, k, :], start=False, stop=k == KC - 1)
                mm.then_inc(s_(name + "_mm"), 1)

            def feat(name, nm, src, banks):
                for n in range(nm):
                    if n >= 4:
                        pe.wait_ge(s_(name + "_ev"), n_(name + "_ev", n - 3))
                    if n % 2 == 0:
                        w = slot(name)
                    feat_tile(name, w, n % 2 * P, src, banks[n % 4][:, :])

            def tok(name, nslots, src, banks, width=SLOTW):
                for s in range(nslots):
                    w = slot(name)
                    for t in range(TT):
                        n = s * TT + t
                        if n >= 4:
                            pe.wait_ge(s_(name + "_ev"), n_(name + "_ev", n - 3))
                        bank, tt = banks[n % 4][:, 0:width], slice(t * P, (t + 1) * P)
                        for k in range(KC):
                            if name in SPLIT:
                                (wh, wl), (xh, xl) = w, src
                                pe.matmul(bank, xh[:, k, tt], wh[:, k, 0:width], start=k == 0, stop=False)
                                pe.matmul(bank, xh[:, k, tt], wl[:, k, 0:width], start=False, stop=False)
                                mm = pe.matmul(bank, xl[:, k, tt], wh[:, k, 0:width], start=False, stop=k == KC - 1)
                            else:
                                mm = pe.matmul(bank, src[:, k, tt], w[:, k, 0:width], start=k == 0, stop=k == KC - 1)
                        mm.then_inc(s_(name + "_mm"), 1)

            def turn(name, src, banks):
                for t in range(TT):
                    if name == "tr0":
                        pe.wait_ge(x_in[t], 16)
                    else:
                        pe.wait_ge(s_(name + "_y"), n_(name + "_y", t + 1))
                    for h in range(2):
                        n = 2 * t + h
                        if n >= 4:
                            pe.wait_ge(s_(name + "_ev"), n_(name + "_ev", n - 3))
                        for j in range(4):
                            mm = pe.transpose(banks[n % 4][:, j * P:(j + 1) * P],
                                              src[:, t, (4 * h + j) * P:(4 * h + j + 1) * P], ident[:, :])
                        mm.then_inc(s_(name + "_mm"), 1)

            def hgrn_scores(h):
                b = h % 2
                K = [side[:, 9 * b + i, :] for i in range(5)]
                Q = [qT[:, h, :]] + [side[:, 9 * b + 5 + i, :] for i in range(4)]
                for i in range(6):
                    r = 6 * h + i
                    if r >= 4:
                        h0, i0 = divmod(r - 4, 6)
                        if i0 < 3:
                            pe.wait_ge(s_("hg_evd"), 3 * h0 + i0 + 1)
                        else:
                            pe.wait_ge(s_("hg_eva"), 3 * h0 + i0 - 2)
                    bank = SA[r % 4]
                    pe.wait_ge(s_("hg_lv"), 6 * h + min(i + 1, 5) + (i >= 4))
                    if i < 4:
                        kk, qq = (kT[:, h, :], Q[0]) if i == 0 else (K[i - 1], Q[i - 1])
                        for j in range(TT):
                            mm = pe.matmul(bank[:, j * P:(j + 1) * P], kk[:, j * P:(j + 1) * P],
                                           qq[:, j * P:(j + 1) * P], start=True, stop=True)
                    elif i == 4:
                        pe.matmul(bank[:, 0:P], K[3][:, 0:P], Q[3][:, P:2 * P], start=True, stop=True)
                        pe.matmul(bank[:, P:3 * P], K[4][:, 0:P], Q[4][:, 2 * P:4 * P], start=True, stop=True)
                        mm = pe.matmul(bank[:, 3 * P:4 * P], K[3][:, 2 * P:3 * P], Q[3][:, 3 * P:4 * P],
                                       start=True, stop=True)
                    else:
                        mm = pe.matmul(bank[:, 0:2 * P], K[4][:, P:2 * P], Q[4][:, 2 * P:4 * P], start=True, stop=True)
                    mm.then_inc(s_("hg_lvl"), 1)

            def hgrn_pv(h):
                pe.wait_ge(s_("hg_evd"), 3 * h + 3)
                pe.wait_ge(s_("hg_eva"), 3 * h + 3)
                if h >= 1:
                    pe.wait_ge(s_("hg_o"), h)
                for j in range(TT):
                    mm = pe.matmul(SB[0][:, j * P:], vtok[:, j, h * P:(h + 1) * P],
                                   prob[:, 4 * (h % 2) + j, j * P:], start=j == 0, stop=j == TT - 1)
                mm.then_inc(s_("hg_pv"), 1)

            def hgrn_ss(h):
                pe.wait_ge(s_("hg_sq"), h + 1)
                if h >= 1:
                    pe.wait_ge(s_("hg_ln"), h)
                pe.matmul(SB[1][:, :], ones[:, :], scr[:, 3 + h % 2, :], start=True, stop=True).then_inc(s_("hg_ss"), 1)

            def attention(A):
                n, steps, N = A.name, A.steps, len(A.steps)
                for i in range(N + 5):
                    if i < N:
                        h, b, t = steps[i]
                        w = (t + 1) * P
                        if n == "fox" and t == 0:
                            if h >= 1:
                                pe.wait_ge(s_("fox_cb"), h)
                            pe.matmul(OB[1][:, :], sel[:, h, :], frow[4], start=True, stop=True).then_inc(s_("fox_c"), 1)
                        if i >= 3:
                            pe.wait_ge(s_(n + "_dm"), i - 2)
                        bank = ps[i % 3]
                        mm = pe.matmul(bank[:, 0:w], A.q(h, t), A.k(h, b, w), start=True, stop=n == "nsa")
                        if n == "fox":
                            mm = pe.matmul(bank[:, t * P:w], ident[:, :], ahead[:, :], start=False, stop=True)
                        mm.then_inc(s_(n + "_sc"), 1)
                    if 3 <= i < N + 3:
                        s = i - 3
                        h, b, t = steps[s]
                        pe.wait_ge(s_(n + "_pn"), s + 1)
                        if s >= 3:
                            pe.wait_ge(s_(n + "_te"), s - 2)
                        for j in range(t + 1):
                            mm = pe.transpose(TPB[s % 3][:, j * P:(j + 1) * P], scr[:, s % SCR_S, j * P:(j + 1) * P], ident[:, :])
                        mm.then_inc(s_(n + "_tp"), 1)
                    if i >= 5 and (i - 5) % 4 == 3:
                        s = i - 5
                        u = s // 4
                        h, b, _ = steps[s]
                        r = h % 2 * HD
                        ob = OB[0 if n == "fox" else h // 2 % 2][r:r + HD, :]
                        pe.wait_ge(s_(n + "_te"), s + 1)
                        if h % 2 == 0 and b == 0:
                            before = h // 2 - (0 if n == "fox" else 1)
                            if before > 0:
                                pe.wait_ge(s_(n + "_y"), before)
                        if n == "nsa" and b == 0:
                            pe.matmul(ob, vcmp[:, h // 4 * HD:(h // 4 + 1) * HD], pcmp(h), start=True, stop=False)
                        for j in range(TT):
                            mm = pe.matmul(ob[:, j * P:], A.v(h, b, j), pT(u)[:, j, j * P:],
                                           start=j == 0 and b == 0 and n == "fox", stop=j == TT - 1 and b == A.branches - 1)
                        mm.then_inc(s_(n + "_pv"), 1)

            def retention():
                def values(h):
                    m, r = h // 2, h % 2 * HD
                    pe.wait_ge(s_("rt_ed"), 4 * h + 4)
                    if h % 2 == 0 and m >= 2:
                        pe.wait_ge(s_("rt_oc"), m - 1)
                    for j in range(TT):
                        mm = pe.matmul(SB[m % 2][r:r + HD, j * P:], vtok[:, j, 512 + h * HD:512 + (h + 1) * HD],
                                       pT(h)[:, j, j * P:], start=j == 0, stop=j == TT - 1)
                    mm.then_inc(s_("rt_pv"), 1)

                def stats(m):
                    pe.wait_ge(s_("rt_oc"), m + 1)
                    if m >= 1:
                        pe.wait_ge(s_("rt_cen"), m)
                    pe.matmul(SB[2][:, :], half_mean[:, :], scr[:, 0, :], start=True, stop=True).then_inc(s_("rt_mu"), 1)
                    pe.wait_ge(s_("rt_sq"), m + 1)
                    if m >= 1:
                        pe.wait_ge(s_("rt_rs"), m)
                    pe.matmul(SB[3][:, :], half_mean[:, :], scr[:, 2, :], start=True, stop=True).then_inc(s_("rt_var"), 1)

                for h in range(9):
                    if h < 8:
                        m, r = h // 2, h % 2 * HD
                        for j in range(TT):
                            n = 4 * h + j
                            if n >= 4:
                                pe.wait_ge(s_("rt_ea"), n - 3)
                            pe.matmul(SA[j][:, j * P:], slab[1][r:r + HD, 4 + m, j * P:(j + 1) * P],
                                      slab[1][r:r + HD, m, j * P:], start=True, stop=True).then_inc(s_("rt_sc"), 1)
                    if h >= 1:
                        values(h - 1)
                        if h % 2 == 1 and h >= 3:
                            stats((h - 3) // 2)
                stats(3)

            def compress():
                pe.wait_ge(s_("nsa_in"), NSA_IN)
                for x, name in enumerate(("ck", "cv")):
                    banks = (SA, SB)[x]
                    pe.wait_ge(s_(("kc_ev", "vc_ev")[x]), n_(("kc_ev", "vc_ev")[x], 2))
                    for i in range(2):
                        w = slot(name)
                        for k in range(KC):
                            c = KC * i + k
                            blocks = a2[x][:, :, 2 * c:2 * c + 16 * (NC - 1) + 1:16]
                            for m in range(2):
                                wt = w[:, k, m * P:(m + 1) * P]
                                pe.matmul(banks[m][:, 0:NG * NC].rearrange("p (g n) -> p g n", g=NG), wt, blocks,
                                          start=c == 0, stop=c == 15)
                                mm = pe.matmul(banks[2 + m][:, 0:1], wt, petab[x][:, c:c + 1], start=c == 0, stop=c == 15)
                        mm.then_inc(s_(name + "_mm"), 1)
                pe.wait_ge(s_("hid_k"), 2)
                for o in range(2):
                    for m in range(2):
                        mm = pe.matmul(SA[2][o * HD:o * HD + HD, 0:NG * NC], w2[0][:, m, :], hid[0][:, m, :],
                                       start=m == 0, stop=m == 1)
                mm.then_inc(s_("cmp_mm"), 1)
                pe.wait_ge(s_("hid_v"), 2)
                for g in range(NG):
                    for m in range(2):
                        mm = pe.matmul(SB[2][0:NC, g * HD:(g + 1) * HD], hid[1][:, m, g * NC:(g + 1) * NC], w2[1][:, m, :],
                                       start=m == 0, stop=m == 1)
                mm.then_inc(s_("cmp_mm"), 1)

            def compressed_attention():
                for g in range(NG + 1):
                    if g < NG:
                        if g >= 2:
                            pe.wait_ge(s_("cs_ev"), 4 * (g - 1))
                        for hg in range(4):
                            h = 4 * g + hg
                            r = h % 2 * HD
                            for t in range(TT):
                                c = (hg // 2 * TT + t) * NC
                                mm = pe.matmul(SA[2 * (g % 2) + hg % 2][:, c:c + NC], NSA.q(h, t), kcmp[r:r + HD, g * NC:(g + 1) * NC],
                                               start=True, stop=True)
                        mm.then_inc(s_("cs_mm"), 1)
                    if g >= 1:
                        pe.wait_ge(s_("cs_p"), g)
                        for hg in range(4):
                            n = 4 * (g - 1) + hg
                            if n >= 4:
                                pe.wait_ge(s_("ct_ev"), n - 3)
                            for t in range(TT):
                                c = (hg * TT + t) * NC
                                mm = pe.transpose(SB[n % 4][0:NC, t * P:(t + 1) * P], csc[(g - 1) % 2][:, c:c + NC], ident[:, :])
                            mm.then_inc(s_("ct_mm"), 1)

            pe.wait_ge(ident_in, 16)
            turn("tr0", res, SB)
            pe.wait_ge(s_("tr0_ev"), n_("tr0_ev", 8))
            feat("pool", 8, xhalves, SA)
            pe.wait_ge(consts_in, NCONST)
            feat("gb", 8, xhalves, SB)
            pe.wait_ge(s_("pool_ev"), n_("pool_ev", 8))
            w = slot("wp")
            for m in range(8):
                pe.wait_ge(s_("pooled"), 2 * (m // 2) + 2)
                if m >= 4:
                    pe.wait_ge(s_("wp_ev"), n_("wp_ev", m - 3))
                for k in range(2):
                    mm = pe.matmul(SA[m % 4][:, :], w[:, m // 2 * 2 + k, m % 2 * P:(m % 2 + 1) * P],
                                   pooledT[:, m // 2 * 2 + k, :], start=k == 0, stop=k == 1)
                mm.then_inc(s_("wp_mm"), 1)
            pe.wait_ge(s_("gb_ev"), n_("gb_ev", 8))
            feat("f", 8, xhalves, SB)
            pe.wait_ge(s_("wp_ev"), n_("wp_ev", 8))
            feat("q", 8, xhalves, SA)
            pe.wait_ge(s_("f_ev"), n_("f_ev", 8))
            tok("v", 4, xhalves, SB)
            pe.wait_ge(s_("q_ev"), n_("q_ev", 8))
            pe.wait_ge(s_("v_ev"), n_("v_ev", 16))
            for h in range(HEADS_H + 2):
                if h < HEADS_H:
                    if h % 2 == 0:
                        w = slot("og")
                    if h >= 2:
                        pe.wait_ge(s_("og_ev"), n_("og_ev", h - 1))
                    feat_tile("og", w, h % 2 * P, xhalves, SB[2 + h % 2][:, :])
                if h >= 2:
                    hgrn_ss(h - 2)
                if h < HEADS_H:
                    hgrn_scores(h)
                if 1 <= h <= HEADS_H:
                    hgrn_pv(h - 1)
            pe.wait_ge(s_("hg_evd"), 24)
            pe.wait_ge(s_("hg_eva"), 24)
            feat("ga", 8, xhalves, SA)
            pe.wait_ge(s_("gated"), 8)
            feat("wa", 8, ghalves, SB)
            pe.wait_ge(s_("ga_ev"), n_("ga_ev", 8))
            pe.wait_ge(s_("wa_ev"), n_("wa_ev", 8))
            tok("o1", 4, mixT, SA)
            turn("ln1", res, SB)
            for b in range(4):
                if b == 0:
                    pe.wait_ge(s_("ln1_ev"), n_("ln1_ev", 8))
                    pe.wait_ge(s_("o1_ev"), n_("o1_ev", 16))
                else:
                    pe.wait_ge(s_(f"up{b - 1}_ev"), n_(f"up{b - 1}_ev", 8))
                    pe.wait_ge(s_(f"dn{b - 1}_ev"), n_(f"dn{b - 1}_ev", 16))
                feat(f"up{b}", 8, xhalves, SA)
                pe.wait_ge(s_(f"hid{b}"), 8)
                tok(f"dn{b}", 4, slab[2 * (b % 2)], SB)
            pe.wait_ge(s_("up3_ev"), 8)
            turn("rms_e", normed, SA)

            pe.wait_ge(s_("rms_e_ev"), n_("rms_e_ev", 8))
            pe.wait_ge(s_("dn3_ev"), 16)
            feat("qf", 4, xhalves, SB)
            feat("kf", 4, xhalves, SA)
            pe.wait_ge(s_("qf_ev"), n_("qf_ev", 4))
            tok("vf", 2, xhalves, SB)
            w = slot("fl")
            pe.wait_ge(s_("kf_ev"), n_("kf_ev", 4))
            feat_tile("fl", w, 0, xhalves, SA[0][0:8, :], width=8)
            pe.wait_ge(s_("vf_ev"), n_("vf_ev", 8))
            feat("qr", 4, xhalves, SB)
            pe.wait_ge(s_("fl_ev"), n_("fl_ev", 1))
            feat("kr", 4, xhalves, SA)
            pe.wait_ge(s_("qr_ev"), n_("qr_ev", 4))
            tok("vr", 2, xhalves, SB)
            pe.wait_ge(s_("kr_ev"), n_("kr_ev", 4))
            feat("ze", 8, xhalves, SA)
            pe.wait_ge(s_("ze_ev"), n_("ze_ev", 8))
            pe.wait_ge(s_("vr_ev"), n_("vr_ev", 8))
            pe.wait_ge(s_("frow"), 1)
            pe.wait_ge(s_("decay_in"), 32)
            attention(FOX)
            pe.wait_ge(s_("fox_y"), 4)
            pe.wait_ge(s_("fox_te"), len(FOX.steps))
            retention()
            pe.wait_ge(s_("yr"), 4)
            tok("oe", 4, slab[2], SA)
            turn("rms_o", normed, SB)

            pe.wait_ge(s_("rms_o_ev"), n_("rms_o_ev", 8))
            pe.wait_ge(s_("oe_ev"), n_("oe_ev", 16))
            feat("kc", 2, xhalves, SA)
            feat("vc", 2, xhalves, SB)
            compress()
            pe.wait_ge(s_("cmp_ev"), n_("cmp_ev", 2))
            feat("ks", 2, xhalves, SA)
            feat("kw", 2, xhalves, SB)
            pe.wait_ge(s_("ks_ev"), n_("ks_ev", 2))
            tok("vs", 1, xhalves, SA)
            pe.wait_ge(s_("kw_ev"), n_("kw_ev", 2))
            tok("vw", 1, xhalves, SB)
            pe.wait_ge(s_("vs_ev"), n_("vs_ev", 4))
            tok("gl", 1, xhalves, SA, width=48)
            pe.wait_ge(s_("vw_ev"), n_("vw_ev", 4))
            feat("qo", 8, xhalves, SB)
            pe.wait_ge(s_("gl_ev"), n_("gl_ev", 4))
            feat("zo", 8, xhalves, SA)
            pe.wait_ge(s_("qo_ev"), n_("qo_ev", 8))
            pe.wait_ge(s_("zo_ev"), n_("zo_ev", 8))
            compressed_attention()
            pe.wait_ge(s_("ct_ev"), 16)
            pe.wait_ge(s_("ks_ev"), n_("ks_ev", 2))
            pe.wait_ge(s_("kw_ev"), n_("kw_ev", 2))
            attention(NSA)
            pe.wait_ge(s_("nsa_y"), 8)
            pe.wait_ge(s_("nsa_te"), len(NSA.steps))
            tok("oo", 4, slab[1], SA)
            assert at[0] == len(stream)

        @block.scalar
        def _(act):
            own = counter()

            def ev(name, n, dst, func=ACT.Copy, bank=None, **kw):
                act.wait_ge(s_(name + "_mm"), n_(name + "_mm", n + 1))
                act.activation(dst, bank, func, **kw).then_inc(s_(name + "_ev"), 1)
                act.wait_ge(s_(name + "_ev"), own(s_(name + "_ev")))

            def turned(name, banks):
                c = INPUTS.index(name)
                act.wait_ge(s_("x_scale"), c + 1)
                for n in range(8):
                    t, h = divmod(n, 2)
                    act.wait_ge(s_(name + "_mm"), n_(name + "_mm", n + 1))
                    act.activation(xhalves[0][:, 4 * h:4 * h + 4, t * P:(t + 1) * P],
                                   banks[n % 4][:, :].rearrange("p (j n) -> p j n", j=4), ACT.Copy,
                                   scale=xsc[:, c:c + 1]).then_inc(s_("x_high"), 1)

            def high(i):
                if i < len(stream) and stream[i][0] in SPLIT:
                    n, m = split_slots.index(i), stream[i][2]
                    if n >= NHIGH:
                        key, _, _, results = stream[split_slots[n - NHIGH]]
                        act.wait_ge(s_(key + "_mm"), n_(key + "_mm", results))
                    act.wait_ge(s_("w_scale"), n + 1)
                    act.activation(whigh[:, n % NHIGH, :, 0:m], wring[:, i % NSLOT, :, 0:m], ACT.Copy,
                                   scale=wsc[:, n:n + 1]).then_inc(s_("w_high"), 1)

            def period(key, slot=0):
                high(first_slot(key) + slot + 1)

            def rstd(name, kind, t):
                act.wait_ge(s_(name + "_v"), n_(name + "_v", t + 1))
                v = stat[:, t, 16:17]
                e, sc = (0, 1.0) if kind == "ln" else (1, 1.0 / DM)
                act.activation(v, v, ACT.Ln, bias=eps[:, e:e + 1], scale=sc).then_inc(act_chain, 1)
                act.wait_ge(act_chain, own(act_chain))
                act.activation(v, v, ACT.Exp, scale=-0.5).then_inc(s_(name + "_r"), 1)
                act.wait_ge(s_(name + "_r"), own(s_(name + "_r")))

            def squares(name, t):
                act.wait_ge(s_(name + "_x"), n_(name + "_x", t + 1))
                act.activation(scr[:, 0:2, :].rearrange("p a n -> p (a n)"), res[:, t, :], ACT.Square,
                               accum_out=stat[:, t, 16:17]).then_inc(s_(name + "_v"), 1)
                act.wait_ge(s_(name + "_v"), own(s_(name + "_v")))

            for dst, src in const_loads:
                act.dma_start(dst, src, allow_slow_non_contiguous=True).then_inc(consts_in, 16)
            turned("tr0", SB)
            high(0)
            act.wait_ge(s_("pads"), 1)
            for m in range(8):
                if m % 2 == 0:
                    period("pool", m // 2)
                if m >= 2:
                    act.wait_ge(s_("pooled"), m - 1)
                ev("pool", m, vpad[m % 2][:, CH:], bank=SA[m % 4][:, :], scale=undo("pool", m // 2))
            act.wait_ge(s_("lb_d"), 1)
            for i in (1, 2):
                act.activation(lbt[:, i, :], lbt[:, i, :], ACT.Exp).then_inc(s_("lb_e"), 1)
                act.wait_ge(s_("lb_e"), own(s_("lb_e")))
            for m in range(8):
                if m % 2 == 0:
                    period("gb", m // 2)
                ev("gb", m, mixT[:, m, :], ACT.Sigmoid, bank=SB[m % 4][:, :], scale=undo("gb", m // 2))
            period("wp")
            for m in range(8):
                if m % 2 == 0:
                    period("f", m // 2)
                ev("f", m, kT[:, m, :], ACT.Sigmoid, bank=SB[m % 4][:, :], scale=undo("f", m // 2))
            for m in range(8):
                if m % 2 == 0:
                    period("q", m // 2)
                act.wait_ge(s_("q_mm"), n_("q_mm", m + 1))
                if m >= 2:
                    act.wait_ge(s_("q_ev"), n_("q_ev", m - 1))
                act.activation(scr[:, m % 2, :], SA[m % 4][:, :], ACT.Sigmoid, scale=undo("q", m // 2)).then_inc(s_("q_sg"), 1)
                act.wait_ge(s_("q_sg"), own(s_("q_sg")))
            for n in range(16):
                s, t = divmod(n, TT)
                if t == 0:
                    period("v", s)
                ev("v", n, vtok[:, t, s * SLOTW:(s + 1) * SLOTW], bank=SB[n % 4][:, 0:SLOTW], scale=undo("v", s))

            act.wait_ge(s_("q_ev"), n_("q_ev", 8))
            act.wait_ge(s_("lb"), 1)

            def hgrn_gates(h):
                if h >= 1:
                    act.wait_ge(s_("hg_k1"), h)
                act.activation(scr[:, 0, :], kT[:, h, :], ACT.Ln, bias=lbt[:, 3, h:h + 1],
                               scale=lbt[:, 4, h:h + 1]).then_inc(s_("hg_lf"), 1)
                act.wait_ge(s_("hg_lf"), own(s_("hg_lf")))
                act.wait_ge(s_("hg_G"), h + 1)
                act.activation(scr[:, 2, :], scr[:, 1, :], ACT.Exp).then_inc(s_("hg_e"), 1)
                act.wait_ge(s_("hg_e"), own(s_("hg_e")))
                act.activation(scr[:, 0, :], scr[:, 1, :], ACT.Exp, scale=-1.0).then_inc(s_("hg_e"), 1)
                act.wait_ge(s_("hg_e"), own(s_("hg_e")))

            def hgrn_copies(h):
                p0 = 4 * (h % 2)
                r = 6 * h + 3
                act.wait_ge(s_("hg_lvl"), r + 1)
                act.wait_ge(s_("hg_evd"), 3 * h + 3)
                if h >= 2:
                    act.wait_ge(s_("hg_pv"), h - 1)
                act.activation(diag(prob[0:64, p0:p0 + 4, :].rearrange("p j n -> p (j n)"), 64, 64), SA[r % 4][0:64, :].rearrange("p (j n) -> p j n", j=4)[:, :, 64:P],
                               ACT.Copy).then_inc(s_("hg_eva"), 1)
                act.wait_ge(s_("hg_eva"), own(s_("hg_eva")))
                act.wait_ge(s_("hg_lvl"), r + 2)
                bank = SA[(r + 1) % 4]
                act.activation(prob[:, p0, P:4 * P], bank[:, 0:3 * P], ACT.Copy)
                act.activation(prob[:, p0 + 2, 3 * P:4 * P], bank[:, 3 * P:4 * P], ACT.Copy).then_inc(s_("hg_eva"), 1)
                act.wait_ge(s_("hg_eva"), own(s_("hg_eva")))
                act.wait_ge(s_("hg_lvl"), r + 3)
                act.activation(prob[:, p0 + 1, 2 * P:4 * P], SA[(r + 2) % 4][:, 0:2 * P], ACT.Copy).then_inc(s_("hg_eva"), 1)
                act.wait_ge(s_("hg_eva"), own(s_("hg_eva")))

            def hgrn_square(h):
                act.wait_ge(s_("hg_pv"), h + 1)
                if h >= 2:
                    act.wait_ge(s_("hg_ss"), h - 1)
                act.activation(scr[:, 3 + h % 2, :], SB[0][:, :], ACT.Square).then_inc(s_("hg_sq"), 1)
                act.wait_ge(s_("hg_sq"), own(s_("hg_sq")))

            def hgrn_rms(h):
                act.wait_ge(s_("hg_ss"), h + 1)
                if h >= 1:
                    act.wait_ge(s_("hg_o"), h)
                ins = act.activation(scr[:, 5, :], SB[1][:, :], ACT.Ln, bias=eps[:, 1:2], scale=1.0 / P)
                ins.then_inc(s_("hg_ln"), 1)
                act.wait_ge(s_("hg_ln"), own(s_("hg_ln")))
                act.wait_ge(s_("hg_ln"), h + 1)
                act.activation(scr[:, 5, :], scr[:, 5, :], ACT.Exp, scale=-0.5).then_inc(s_("hg_rs"), 1)
                act.wait_ge(s_("hg_rs"), own(s_("hg_rs")))

            for h in range(HEADS_H + 2):
                if h < HEADS_H and h % 2 == 0:
                    period("og", h // 2)
                if h < HEADS_H:
                    hgrn_gates(h)
                if h >= 2:
                    hgrn_rms(h - 2)
                if 1 <= h <= HEADS_H:
                    hgrn_copies(h - 1)
                if h < HEADS_H:
                    ev("og", h, gateT[:, h, :], bank=SB[2 + h % 2][:, :], scale=undo("og", h // 2))
                if h >= 1 and h <= HEADS_H:
                    hgrn_square(h - 1)
            for h in range(HEADS_H):
                act.activation(gateT[:, h, :], gateT[:, h, :], ACT.Sigmoid).then_inc(s_("og_sg"), 1)
                act.wait_ge(s_("og_sg"), own(s_("og_sg")))
            for h in range(HEADS_H):
                act.wait_ge(s_("gate_x"), h + 1)
                act.activation(ghalves[0][:, h, :], qT[:, h, :], ACT.Copy, scale=xsc[:, 1:2]).then_inc(s_("gate_high"), 1)
            for m in range(8):
                if m % 2 == 0:
                    period("ga", m // 2)
                ev("ga", m, kT[:, m, :], ACT.Sigmoid, bank=SA[m % 4][:, :], scale=undo("ga", m // 2))
            for i in range(4):
                period("wa", i)
            for i in range(4):
                period("o1", i)
            for t in range(TT):
                rstd("ln1", "ln", t)
            turned("ln1", SB)
            for b in range(4):
                for m in range(8):
                    if m % 2 == 0:
                        period(f"up{b}", m // 2)
                    if m >= 2 or b > 0:
                        act.wait_ge(s_(f"hid{b}" if m >= 2 else f"hid{b - 1}"), n_(f"hid{b}" if m >= 2 else f"hid{b - 1}", m - 1 if m >= 2 else 7 + m))
                    ev(f"up{b}", m, scr[:, m % 2, :], ACT.Relu, bank=SA[m % 4][:, :], scale=undo(f"up{b}", m // 2))
                for i in range(4):
                    period(f"dn{b}", i)
            for t in range(TT):
                rstd("ln2", "ln", t)
            for t in range(TT):
                squares("rms_e", t)
                rstd("rms_e", "rms", t)
            turned("rms_e", SA)

            for m in range(4):
                if m % 2 == 0:
                    period("qf", m // 2)
                ev("qf", m, slab[0][:, m, :], bank=SB[m][:, :], scale=undo_q("qf", m // 2))
            for m in range(4):
                if m % 2 == 0:
                    period("kf", m // 2)
                ev("kf", m, slab[0][:, 4 + m, :], bank=SA[m][:, :], scale=undo("kf", m // 2))
            for n in range(8):
                s, t = divmod(n, TT)
                if t == 0:
                    period("vf", s)
                ev("vf", n, vtok[:, t, s * SLOTW:(s + 1) * SLOTW], bank=SB[n % 4][:, 0:SLOTW], scale=undo("vf", s))
            period("fl")
            act.wait_ge(s_("fl_mm"), n_("fl_mm", 1))
            ins = act.activation(frow[0], SA[0][0:8, :], ACT.Identity, bias=bf_[:, 0:1], scale=undo("fl", 0)[0:8, :])
            ins.then_inc(s_("fl_ev"), 1)
            act.wait_ge(s_("fl_ev"), own(s_("fl_ev")))
            act.wait_ge(s_("fl_ev"), n_("fl_ev", 1))
            act.activation(frow[1], frow[0], ACT.Abs).then_inc(act_chain, 1)
            act.wait_ge(act_chain, own(act_chain))
            act.activation(frow[1], frow[1], ACT.Exp, scale=-1.0).then_inc(act_chain, 1)
            act.wait_ge(act_chain, own(act_chain))
            act.activation(frow[1], frow[1], ACT.Ln, bias=eps[0:8, 3:4]).then_inc(s_("fl_ln"), 1)
            act.wait_ge(s_("fl_ln"), own(s_("fl_ln")))
            for i in range(2):
                period("qr", i)
            for i in range(2):
                period("kr", i)
            for n in range(8):
                s, t = divmod(n, TT)
                if t == 0:
                    period("vr", s)
                ev("vr", n, vtok[:, t, 512 + s * SLOTW:512 + (s + 1) * SLOTW], bank=SB[n % 4][:, 0:SLOTW], scale=undo("vr", s))
            for m in range(8):
                if m % 2 == 0:
                    period("ze", m // 2)
                act.wait_ge(s_("ze_mm"), n_("ze_mm", m + 1))
                if m >= 2:
                    act.wait_ge(s_("ze_ev"), n_("ze_ev", m - 1))
                act.activation(scr[:, m % 2, :], SA[m % 4][:, :], ACT.Sigmoid, scale=undo("ze", m // 2)).then_inc(s_("ze_sg"), 1)
                act.wait_ge(s_("ze_sg"), own(s_("ze_sg")))

            def attention(A):
                n, steps, N = A.name, A.steps, len(A.steps)
                for i in range(N + 4):
                    if i >= 4:
                        s = i - 4
                        h, b, t = steps[s]
                        u = s // 4
                        act.wait_ge(s_(n + "_tp"), s + 1)
                        if u >= 2:
                            act.wait_ge(s_(n + "_pv"), u - 1)
                        act.activation(pT(u)[:, 0:t + 1, t * P:(t + 1) * P],
                                       TPB[s % 3][:, 0:(t + 1) * P].rearrange("p (j n) -> p j n", n=P), ACT.Copy).then_inc(s_(n + "_te"), 1)
                    if i < N:
                        h, b, t = steps[i]
                        w = (t + 1) * P
                        if n == "fox" and t == 0:
                            act.wait_ge(s_("fox_c"), h + 1)
                            if h >= 2:
                                act.wait_ge(s_("fox_dm"), 4 * (h - 1))
                            act.activation(scr[:, 4 + h % 2, :], OB[1][:, :], ACT.Copy).then_inc(s_("fox_cb"), 1)
                        act.wait_ge(s_(n + "_dm"), i + 1)
                        act.activation(scr[:, i % SCR_S, 0:w], scr[:, i % SCR_S, 0:w], ACT.Exp, scale=-1.0,
                                       bias=tmin[:, i % 8:i % 8 + 1], accum_out=tsum[:, i % 8:i % 8 + 1]).then_inc(s_(n + "_ex"), 1)

            act.wait_ge(s_("ze_ev"), n_("ze_ev", 8))
            attention(FOX)

            def pair(m):
                act.wait_ge(s_("rt_pv"), 2 * m + 2)
                if m >= 1:
                    act.wait_ge(s_("rt_mu"), m)
                    act.wait_ge(s_("rt_cen"), m)
                act.activation(scr[:, 0, :], SB[m % 2][:, :], ACT.Copy).then_inc(s_("rt_oc"), 1)
                act.wait_ge(s_("rt_oc"), own(s_("rt_oc")))

            def pair_stats(m):
                act.wait_ge(s_("rt_cen"), m + 1)
                if m >= 1:
                    act.wait_ge(s_("rt_var"), m)
                act.activation(scr[:, 2, :], scr[:, 1, :], ACT.Square).then_inc(s_("rt_sq"), 1)
                act.wait_ge(s_("rt_sq"), own(s_("rt_sq")))
                act.wait_ge(s_("rt_var"), m + 1)
                if m >= 1:
                    act.wait_ge(s_("yr"), m)
                act.activation(scr[:, 3, :], SB[3][:, :], ACT.Ln, bias=eps[:, 2:3]).then_inc(act_chain, 1)
                act.wait_ge(act_chain, own(act_chain))
                act.activation(scr[:, 3, :], scr[:, 3, :], ACT.Exp, scale=-0.5).then_inc(s_("rt_rs"), 1)
                act.wait_ge(s_("rt_rs"), own(s_("rt_rs")))

            for h in range(8):
                for j in range(TT):
                    act.wait_ge(s_("rt_sc"), 4 * h + j + 1)
                    if h >= 2:
                        act.wait_ge(s_("rt_pv"), h - 1)
                    act.activation(pT(h)[:, j, j * P:], SA[j][:, j * P:], ACT.Copy).then_inc(s_("rt_ea"), 1)
                    act.wait_ge(s_("rt_ea"), own(s_("rt_ea")))
                if h % 2 == 0 and h >= 2:
                    pair(h // 2 - 1)
                if h % 2 == 1 and h >= 3:
                    pair_stats((h - 3) // 2)
            pair(3)
            pair_stats(3)
            for i in range(4):
                period("oe", i)
            for t in range(TT):
                squares("rms_o", t)
                rstd("rms_o", "rms", t)
            turned("rms_o", SB)

            for x, name in enumerate(("kc", "vc")):
                period(name)
                for m in range(2):
                    act.wait_ge(s_(name + "_mm"), n_(name + "_mm", m + 1))
                    bank = (SA, SB)[x][m]
                    for o in range(2):
                        r = slice(o * HD, o * HD + HD)
                        act.activation(a2[x][0:HD, 2 * m + o, :], bank[r, :], ACT.Copy, scale=undo(name, 0)[r, :])
                        ins = act.activation(a2[x][HD:P, 2 * m + o, 0:SEQ - 1], bank[r, 1:SEQ], ACT.Copy, scale=undo(name, 0)[r, :])
                    ins.then_inc(s_(name + "_ev"), 1)
                    act.wait_ge(s_(name + "_ev"), own(s_(name + "_ev")))
            for x in range(2):
                period("ck" if x == 0 else "cv", 0)
                if x == 0:
                    period("ck", 1)
                act.wait_ge(s_(("ck_mm", "cv_mm")[x]), n_(("ck_mm", "cv_mm")[x], 2))
                for m in range(2):
                    c = 2 * x + m
                    banks = (SA, SB)[x]
                    act.activation(hbias[:, c:c + 1], banks[2 + m][:, 0:1], ACT.Copy).then_inc(act_chain, 1)
                    act.wait_ge(act_chain, own(act_chain))
                    act.activation(hsig[:, 128 * c:128 * c + NG * NC], banks[m][:, 0:NG * NC], ACT.Sigmoid,
                                   bias=hbias[:, c:c + 1]).then_inc(s_("hid_sg"), 1)
                    act.wait_ge(s_("hid_sg"), own(s_("hid_sg")))
            period("cv", 1)
            act.wait_ge(s_("cmp_mm"), n_("cmp_mm", 1))
            act.activation(kcmp, SA[2][:, 0:NG * NC], ACT.Copy).then_inc(s_("cmp_ev"), 1)
            act.wait_ge(s_("cmp_ev"), own(s_("cmp_ev")))
            act.wait_ge(s_("cmp_mm"), n_("cmp_mm", 2))
            act.activation(vcmp, SB[2][0:NC, 0:256], ACT.Copy).then_inc(s_("cmp_ev"), 1)
            act.wait_ge(s_("cmp_ev"), own(s_("cmp_ev")))
            for x, name in enumerate(("ks", "kw")):
                period(name)
                for m in range(2):
                    act.wait_ge(s_(name + "_mm"), n_(name + "_mm", m + 1))
                    for o in range(2):
                        r = slice(o * HD, o * HD + HD)
                        act.activation(kdup[x][0:HD, 2 * m + o, :], (SA, SB)[x][m][r, :], ACT.Copy, scale=undo(name, 0)[r, :])
                        ins = act.activation(kdup[x][HD:P, 2 * m + o, :], (SA, SB)[x][m][r, :], ACT.Copy, scale=undo(name, 0)[r, :])
                    ins.then_inc(s_(name + "_ev"), 1)
                    act.wait_ge(s_(name + "_ev"), own(s_(name + "_ev")))
            for x, name in enumerate(("vs", "vw")):
                period(name)
                for t in range(TT):
                    ev(name, t, vtok[:, t, x * 256:x * 256 + 256], bank=(SA, SB)[x][t][:, 0:256], scale=undo(name, 0))
            period("gl")
            for m in range(8):
                if m % 2 == 0:
                    period("qo", m // 2)
                ev("qo", m, slab[0][:, m, :], bank=SB[m % 4][:, :], scale=undo_q("qo", m // 2))
            for t in range(TT):
                act.wait_ge(s_("gl_ev"), n_("gl_ev", t + 1))
                act.activation(gates[:, t, :], gates[:, t, :], ACT.Sigmoid).then_inc(s_("gate"), 1)
                act.wait_ge(s_("gate"), own(s_("gate")))
            for m in range(8):
                if m % 2 == 0:
                    period("zo", m // 2)
                act.wait_ge(s_("zo_mm"), n_("zo_mm", m + 1))
                if m >= 2:
                    act.wait_ge(s_("zo_ev"), n_("zo_ev", m - 1))
                act.activation(scr[:, m % 2, :], SA[m % 4][:, :], ACT.Sigmoid, scale=undo("zo", m // 2)).then_inc(s_("zo_sg"), 1)
                act.wait_ge(s_("zo_sg"), own(s_("zo_sg")))
            for g in range(NG + 1):
                if g < NG:
                    act.wait_ge(s_("cs_d"), g + 1)
                    act.activation(csc[g % 2], csc[g % 2], ACT.Exp, scale=-1.0).then_inc(s_("cs_e"), 1)
                    act.wait_ge(s_("cs_e"), own(s_("cs_e")))
                if g >= 1:
                    for hg in range(4):
                        n = 4 * (g - 1) + hg
                        act.wait_ge(s_("ct_mm"), n + 1)
                        act.activation(pcmp(n), SB[n % 4][0:NC, :], ACT.Copy).then_inc(s_("ct_ev"), 1)
                        act.wait_ge(s_("ct_ev"), own(s_("ct_ev")))
            attention(NSA)
            for t in range(TT):
                squares("rms_f", t)
                rstd("rms_f", "rms", t)

        @block.vector
        def _(dve):
            own = counter()

            def scale_of(e, sc, inv, factor):
                dve.tensor_scalar(e, e, LEAST, None, ALU.max).then_inc(dve_chain, 1)
                dve.wait_ge(dve_chain, own(dve_chain))
                dve.tensor_scalar(e.bitcast(U32), e.bitcast(U32), EXPONENT, None, ALU.bitwise_and).then_inc(dve_chain, 1)
                dve.wait_ge(dve_chain, own(dve_chain))
                if factor is None:
                    dve.tensor_scalar(inv, e, 1.0 / TOP, None, ALU.mult)
                else:
                    dve.tensor_scalar(inv, e, 1.0 / TOP, factor, ALU.mult, ALU.mult)
                dve.reciprocal(sc, e).then_inc(dve_chain, 1)
                dve.wait_ge(dve_chain, own(dve_chain))
                return dve.tensor_scalar(sc, sc, TOP, None, ALU.mult)

            def input_scale(name):
                c = slice(INPUTS.index(name), INPUTS.index(name) + 1)
                scale_of(xexp[:, c], xsc[:, c], xinv[:, c], None).then_inc(s_("x_scale"), 1)
                dve.wait_ge(s_("x_scale"), own(s_("x_scale")))

            def norm_bound(name):
                c = slice(INPUTS.index(name), INPUTS.index(name) + 1)
                dve.wait_ge(s_(name + "_gain"), 16)
                dve.tensor_reduce(xexp[:, c], gain[name][0], mybir.AxisListType.XY, ALU.max, apply_absolute_value=True).then_inc(dve_chain, 1)
                dve.wait_ge(dve_chain, own(dve_chain))
                if name == "ln1":
                    dve.wait_ge(s_(name + "_b_gain"), 16)
                    dve.tensor_reduce(xmax[:, 2:3], gain["ln1_b"][0], mybir.AxisListType.XY, ALU.max, apply_absolute_value=True)
                    dve.tensor_scalar(xexp[:, c], xexp[:, c], float(DM) ** 0.5, None, ALU.mult).then_inc(dve_chain, 1)
                    dve.wait_ge(dve_chain, own(dve_chain))
                    dve.tensor_tensor(xexp[:, c], xexp[:, c], xmax[:, 2:3], ALU.add).then_inc(dve_chain, 1)
                else:
                    dve.tensor_scalar(xexp[:, c], xexp[:, c], float(DM) ** 0.5, None, ALU.mult).then_inc(dve_chain, 1)
                dve.wait_ge(dve_chain, own(dve_chain))
                input_scale(name)

            def measure(i):
                if i < len(stream) and stream[i][0] in SPLIT:
                    key, _, m, _ = stream[i]
                    n = split_slots.index(i)
                    c = slice(n, n + 1)
                    dve.wait_ge(w_in[i % NSLOT], 16 * (i // NSLOT + 1))
                    dve.tensor_reduce(wsc[:, c], wring[:, i % NSLOT, :, 0:m], mybir.AxisListType.XY, ALU.max,
                                      apply_absolute_value=True).then_inc(s_("w_max"), 1)
                    dve.wait_ge(s_("w_all"), n + 1)
                    x = input_of(i)
                    last = scale_of(wexp[:, c], wsc[:, c], winv[:, c], xinv[:, x:x + 1])
                    if key in QSLOTS:
                        q = QSLOTS[key] + i - first_slot(key)
                        last = dve.tensor_scalar(invq[:, q:q + 1], winv[:, c], float(P) ** -0.5 if key == "q" else -HD ** -0.5,
                                                 None, ALU.mult)
                    last.then_inc(s_("w_scale"), 1)
                    dve.wait_ge(s_("w_scale"), own(s_("w_scale")))

            def low(i):
                if i < len(stream) and stream[i][0] in SPLIT:
                    n, m = split_slots.index(i), stream[i][2]
                    dve.wait_ge(s_("w_high"), n + 1)
                    dve.scalar_tensor_tensor(low_of(i)[:, :, 0:m], wring[:, i % NSLOT, :, 0:m], wsc[:, n:n + 1],
                                             whigh[:, n % NHIGH, :, 0:m], ALU.mult, ALU.subtract).then_inc(s_("w_low"), 1)

            def before(key, slot=0):
                low(first_slot(key) + slot + 1)

            def after(key, slot=0):
                measure(first_slot(key) + slot + 2)

            def turned_low(name, banks, ns):
                i = INPUTS.index(name)
                for n in ns:
                    t, h = divmod(n, 2)
                    dve.wait_ge(s_("x_high"), 8 * (i - (i > 0)) + n + 1)
                    dve.scalar_tensor_tensor(xhalves[1][:, 4 * h:4 * h + 4, t * P:(t + 1) * P],
                                             banks[n % 4][:, :].rearrange("p (j n) -> p j n", j=4), xsc[:, i:i + 1],
                                             xhalves[0][:, 4 * h:4 * h + 4, t * P:(t + 1) * P], ALU.mult,
                                             ALU.subtract).then_inc(s_(name + "_ev"), 1)

            def folded(x):
                return x.rearrange("p (a n) -> p a n", a=2)

            def norm(name, kind, dst, banks=None):
                dve.wait_ge(s_(name + "_gain"), 16)
                g = gain[name][0]
                if kind == "ln":
                    dve.wait_ge(s_(name + "_b_gain"), 16)
                    for t in range(TT):
                        st = stat[:, t, 0:12].rearrange("p (a b) -> p a b", a=2)
                        for i in range(2):
                            ins = dve.bn_stats(st[:, i, :], res[:, t, i * 512:(i + 1) * 512])
                        ins.then_inc(dve_chain, 1)
                        dve.wait_ge(dve_chain, own(dve_chain))
                        dve.bn_aggr(stat[:, t, 15:17], stat[:, t, 0:12]).then_inc(s_(name + "_v"), 1)
                        dve.wait_ge(s_(name + "_v"), own(s_(name + "_v")))
                for t in range(TT):
                    dve.wait_ge(s_(name + "_r"), n_(name + "_r", t + 1))
                    if kind == "ln":
                        dve.tensor_scalar(res[:, t, :], res[:, t, :], stat[:, t, 15:16], stat[:, t, 16:17],
                                          ALU.subtract, ALU.mult).then_inc(dve_chain, 1)
                        dve.wait_ge(dve_chain, own(dve_chain))
                        dve.tensor_tensor(folded(res[:, t, :]), folded(res[:, t, :]), g, ALU.mult).then_inc(dve_chain, 1)
                        dve.wait_ge(dve_chain, own(dve_chain))
                        ins = dve.tensor_tensor(folded(res[:, t, :]), folded(res[:, t, :]), gain[name + "_b"][0], ALU.add)
                    else:
                        ins = dve.scalar_tensor_tensor(folded(dst[:, t, :]), folded(res[:, t, :]), stat[:, t, 16:17], g,
                                                       ALU.mult, ALU.mult)
                    ins.then_inc(s_(name + "_y"), 1)
                    if banks and t >= 1:
                        turned_low(name, banks, range(2 * t - 2, 2 * t))
                if banks:
                    turned_low(name, banks, range(6, 8))

            def add_into(name, banks, alpha, done=None):
                for n in range(16):
                    s, t = divmod(n, TT)
                    if t == 0:
                        before(name, s)
                    dve.wait_ge(s_(name + "_mm"), n_(name + "_mm", n + 1))
                    r = res[:, t, s * SLOTW:(s + 1) * SLOTW]
                    ins = dve.scalar_tensor_tensor(r, r, alpha, banks[n % 4][:, 0:SLOTW], ALU.mult, ALU.add)
                    ins.then_inc(s_(name + "_ev"), 1)
                    if t == TT - 1:
                        after(name, s)
                dve.wait_ge(s_(name + "_ev"), n_(name + "_ev", 16))
                if done:
                    dve.sem_inc(s_(done), TT)

            dve.memset(pads[:, 0:4 * PADW], 0.0).then_inc(s_("pads"), 1)
            dve.wait_ge(s_("pads"), own(s_("pads")))
            for t in range(TT):
                dve.wait_ge(x_in[t], 16)
                dve.tensor_reduce(xmax[:, t:t + 1], res[:, t, :], AX_X, ALU.max, apply_absolute_value=True).then_inc(dve_chain, 1)
                dve.wait_ge(dve_chain, own(dve_chain))
            dve.tensor_reduce(xmax[:, 0:1], xmax[:, 0:4], AX_X, ALU.max).then_inc(s_("x_max"), 1)
            dve.wait_ge(s_("x_all"), 1)
            input_scale("tr0")
            turned_low("tr0", SB, range(8))
            measure(0)
            low(0)
            measure(1)
            dve.wait_ge(consts_in, NCONST)
            dve.tensor_reduce(xmax[:, 1:2], ng[:, :], AX_X, ALU.max, apply_absolute_value=True).then_inc(s_("x_max"), 1)
            dve.wait_ge(s_("x_all"), 2)
            dve.tensor_scalar(xexp[:, 1:2], xexp[:, 1:2], float(P) ** 0.5, None, ALU.mult).then_inc(dve_chain, 1)
            dve.wait_ge(dve_chain, own(dve_chain))
            input_scale("gated")
            mx, l0, l1 = lbt[:, 0, :], lbt[:, 1, :], lbt[:, 2, :]
            dve.tensor_tensor(mx, lbl[:, 0, :], lbl[:, 1, :], ALU.max).then_inc(dve_chain, 1)
            dve.wait_ge(dve_chain, own(dve_chain))
            dve.tensor_tensor(l0, lbl[:, 0, :], mx, ALU.subtract).then_inc(dve_chain, 1)
            dve.wait_ge(dve_chain, own(dve_chain))
            dve.tensor_tensor(l1, lbl[:, 1, :], mx, ALU.subtract).then_inc(s_("lb_d"), 1)
            dve.wait_ge(s_("lb_d"), own(s_("lb_d")))
            for m in range(8):
                g = m // 2
                if m % 2 == 0:
                    before("pool", g)
                dve.wait_ge(s_("pool_ev"), n_("pool_ev", m + 1))
                v = vpad[m % 2]
                cur = v
                for j in range(g + 1):
                    d = 1 << j
                    dst = wpad[j % 2]
                    dve.tensor_tensor(dst[:, CH:], cur[:, CH:], cur[:, CH - d:PADW - d], ALU.add).then_inc(dve_chain, 1)
                    dve.wait_ge(dve_chain, own(dve_chain))
                    cur = dst
                dve.tensor_tensor(cur[:, CH:2 * CH], cur[:, CH:2 * CH], edge[:, g, :], ALU.mult).then_inc(dve_chain, 1)
                dve.wait_ge(dve_chain, own(dve_chain))
                dve.scalar_tensor_tensor(pooledT[:, m, :], cur[:, CH:], 0.5 ** (g + 1), v[:, CH:], ALU.mult,
                                         ALU.subtract).then_inc(s_("pooled"), 1)
                dve.wait_ge(s_("pooled"), own(s_("pooled")))
                if m % 2 == 1:
                    after("pool", g)
            for i in range(4):
                before("gb", i)
                after("gb", i)
            before("wp")
            for m in range(8):
                dve.wait_ge(s_("wp_mm"), n_("wp_mm", m + 1))
                dve.wait_ge(s_("gb_ev"), n_("gb_ev", m + 1))
                dve.scalar_tensor_tensor(mixT[:, m, :], SA[m % 4][:, :], psc[:, m:m + 1], mixT[:, m, :], ALU.mult,
                                         ALU.mult).then_inc(s_("wp_ev"), 1)
                dve.wait_ge(s_("wp_ev"), own(s_("wp_ev")))
            after("wp")
            for i in range(4):
                before("f", i)
                after("f", i)
            for m in range(8):
                if m % 2 == 0:
                    before("q", m // 2)
                dve.wait_ge(s_("q_sg"), m + 1)
                dve.scalar_tensor_tensor(qT[:, m, :], SA[m % 4][:, :], undo_q("q", m // 2), scr[:, m % 2, :], ALU.mult,
                                         ALU.mult).then_inc(s_("q_ev"), 1)
                dve.wait_ge(s_("q_ev"), own(s_("q_ev")))
                if m % 2 == 1:
                    after("q", m // 2)
            dve.wait_ge(s_("lb_e"), 2)
            dve.tensor_tensor(mx, l0, l1, ALU.add).then_inc(dve_chain, 1)
            dve.wait_ge(dve_chain, own(dve_chain))
            dve.reciprocal(mx, mx).then_inc(dve_chain, 1)
            dve.wait_ge(dve_chain, own(dve_chain))
            dve.tensor_tensor(lbt[:, 3, :], l0, mx, ALU.mult).then_inc(dve_chain, 1)
            dve.wait_ge(dve_chain, own(dve_chain))
            dve.tensor_scalar(lbt[:, 4, :], lbt[:, 3, :], -1.0, 1.0, ALU.mult, ALU.add).then_inc(dve_chain, 1)
            dve.wait_ge(dve_chain, own(dve_chain))
            dve.tensor_scalar(lbt[:, 0, :], lbt[:, 4, :], -1.0, None, ALU.mult).then_inc(s_("lb"), 1)
            dve.wait_ge(s_("lb"), own(s_("lb")))
            dve.wait_ge(s_("lb"), 1)
            for i in range(4):
                before("v", i)
                after("v", i)
            dve.memset(mulq[:, :, :], 1.0).then_inc(dve_chain, 1)
            dve.wait_ge(dve_chain, own(dve_chain))
            dve.memset(mulk[:, :, :], 1.0).then_inc(dve_chain, 1)
            dve.wait_ge(dve_chain, own(dve_chain))
            dve.wait_ge(s_("wp_mm"), n_("wp_mm", 8))
            dve.memset(prob[:, :, :], 0.0).then_inc(dve_chain, 1)
            dve.wait_ge(dve_chain, own(dve_chain))

            def hgrn_levels(h):
                b = h % 2
                K = [side[:, 9 * b + i, :] for i in range(5)]
                Q = [qT[:, h, :]] + [side[:, 9 * b + 5 + i, :] for i in range(4)]

                def by(x, n):
                    return x.rearrange("p (s w) -> p s w", s=n)

                def wide(x, n, w):
                    return x.unsqueeze(2).to_broadcast([P, n, w])

                dve.wait_ge(s_("hg_lf"), n_("hg_lf", h + 1))
                if h >= 1:
                    dve.wait_ge(s_("hg_e"), 2 * h)
                dve.tensor_tensor_scan(scr[:, 1, :], segment[:, :], scr[:, 0, :], 0.0, ALU.mult, ALU.add).then_inc(s_("hg_G"), 1)
                dve.wait_ge(s_("hg_G"), own(s_("hg_G")))
                dve.tensor_scalar(kT[:, h, :], kT[:, h, :], lbt[:, 0, h:h + 1], lbt[:, 4, h:h + 1], ALU.mult, ALU.add).then_inc(dve_chain, 1)
                dve.wait_ge(dve_chain, own(dve_chain))
                dve.wait_ge(s_("hg_e"), 2 * h + 2)
                dve.tensor_copy(segdec[:, 0, :], by(scr[:, 2, :], 32)[:, :, CH - 1]).then_inc(dve_chain, 1)
                dve.wait_ge(dve_chain, own(dve_chain))
                dve.tensor_tensor(Q[0], Q[0], scr[:, 2, :], ALU.mult).then_inc(dve_chain, 1)
                dve.wait_ge(dve_chain, own(dve_chain))
                ins = dve.tensor_tensor(kT[:, h, :], kT[:, h, :], scr[:, 0, :], ALU.mult)
                ins.then_inc(s_("hg_lv"), 1)
                dve.wait_ge(s_("hg_lv"), own(s_("hg_lv")))
                dve.wait_ge(s_("hg_lv"), 6 * h + 1)
                dve.sem_inc(s_("hg_k1"), 1)
                if h >= 2:
                    dve.wait_ge(s_("hg_lvl"), 6 * (h - 1))
                dve.tensor_tensor(by(K[0], 32), by(kT[:, h, :], 32), wide(segdec[:, 0, :], 32, CH), ALU.mult)\
                    .then_inc(s_("hg_lv"), 1)
                dve.wait_ge(s_("hg_lv"), own(s_("hg_lv")))
                dve.wait_ge(s_("hg_lv"), 6 * h + 2)
                for l in range(4):
                    n, w = 32 >> l, CH << l
                    seg = segdec[:, l, 0:n].rearrange("p (i o) -> p i o", o=2)
                    mq = mulq[:, l, 0:n].rearrange("p (i o) -> p i o", o=2)
                    mk = mulk[:, l, 0:n].rearrange("p (i o) -> p i o", o=2)
                    dve.tensor_copy(mq[:, :, 1], seg[:, :, 0])
                    if l < 3:
                        dve.tensor_tensor(segdec[:, l + 1, 0:n // 2], seg[:, :, 0], seg[:, :, 1], ALU.mult)
                    dve.tensor_copy(mk[:, :, 0], seg[:, :, 1]).then_inc(dve_chain, 1)
                    dve.wait_ge(dve_chain, own(dve_chain))
                    if l < 3:
                        dve.tensor_tensor(by(Q[l + 1], n), by(Q[l], n), wide(mulq[:, l, 0:n], n, w), ALU.mult)
                        ins = dve.tensor_tensor(by(K[l + 1], n), by(K[l], n), wide(mulk[:, l, 0:n], n, w), ALU.mult)
                    else:
                        dve.tensor_tensor(by(Q[4], 4)[:, 2:4, :], by(Q[3], 4)[:, 2:4, :], wide(mulq[:, 3, 2:4], 2, w), ALU.mult)
                        ins = dve.tensor_tensor(by(K[4], 4)[:, 0:2, :], by(K[3], 4)[:, 0:2, :], wide(mulk[:, 3, 0:2], 2, w), ALU.mult)
                    ins.then_inc(s_("hg_lv"), 1)
                    dve.wait_ge(s_("hg_lv"), own(s_("hg_lv")))
                    dve.wait_ge(s_("hg_lv"), 6 * h + 3 + l)

            def hgrn_masks(h):
                p0 = 4 * (h % 2)
                for i in range(3):
                    r = 6 * h + i
                    dve.wait_ge(s_("hg_lvl"), r + 1)
                    if h >= 2:
                        dve.wait_ge(s_("hg_pv"), h - 1)
                    dve.copy_predicated(diag(prob[:, p0:p0 + 4, :].rearrange("p j n -> p (j n)"), 0, P),
                                        levels[:, i, :].unsqueeze(1).to_broadcast([P, 4, P]),
                                        SA[r % 4][:, :].rearrange("p (j n) -> p j n", j=4)).then_inc(s_("hg_evd"), 1)
                    dve.wait_ge(s_("hg_evd"), own(s_("hg_evd")))
                    dve.wait_ge(s_("hg_evd"), r - 3 * h + 1)

            def hgrn_out(h):
                dve.wait_ge(s_("hg_rs"), h + 1)
                dve.scalar_tensor_tensor(qT[:, h, :], SB[0][:, :], ng[:, h:h + 1], scr[:, 5, :], ALU.mult, ALU.mult)\
                    .then_inc(s_("hg_o"), 1)
                dve.wait_ge(s_("hg_o"), own(s_("hg_o")))

            for h in range(HEADS_H + 2):
                if 1 <= h <= HEADS_H:
                    hgrn_masks(h - 1)
                if h < HEADS_H and h % 2 == 0:
                    before("og", h // 2)
                if h < HEADS_H:
                    hgrn_levels(h)
                if h < HEADS_H and h % 2 == 1:
                    after("og", h // 2)
                if h >= 2:
                    hgrn_out(h - 2)
            for h in range(HEADS_H):
                dve.wait_ge(s_("og_sg"), h + 1)
                dve.wait_ge(s_("hg_o"), h + 1)
                dve.tensor_tensor(qT[:, h, :], gateT[:, h, :], qT[:, h, :], ALU.mult).then_inc(s_("gate_x"), 1)
            for h in range(HEADS_H):
                dve.wait_ge(s_("gate_high"), h + 1)
                dve.scalar_tensor_tensor(ghalves[1][:, h, :], qT[:, h, :], xsc[:, 1:2], ghalves[0][:, h, :], ALU.mult,
                                         ALU.subtract).then_inc(s_("gated"), 1)
            for i in range(4):
                before("ga", i)
                after("ga", i)
            for m in range(8):
                if m % 2 == 0:
                    before("wa", m // 2)
                dve.wait_ge(s_("wa_mm"), n_("wa_mm", m + 1))
                dve.wait_ge(s_("ga_ev"), n_("ga_ev", m + 1))
                dve.scalar_tensor_tensor(kT[:, m, :], SB[m % 4][:, :], undo("wa", m // 2), kT[:, m, :], ALU.mult, ALU.mult).then_inc(dve_chain, 1)
                dve.wait_ge(dve_chain, own(dve_chain))
                dve.tensor_tensor(mixT[:, m, :], mixT[:, m, :], kT[:, m, :], ALU.add).then_inc(s_("wa_ev"), 1)
                dve.wait_ge(s_("wa_ev"), own(s_("wa_ev")))
                if m % 2 == 1:
                    after("wa", m // 2)
            norm_bound("ln1")
            dve.wait_ge(s_("x_again"), 16 * TT)
            add_into("o1", SA, ALPHA)
            norm("ln1", "ln", res, SB)
            for b in range(4):
                for m in range(8):
                    if m % 2 == 0:
                        before(f"up{b}", m // 2)
                    dve.wait_ge(s_(f"up{b}_ev"), n_(f"up{b}_ev", m + 1))
                    if m == 0 and b >= 2:
                        dve.wait_ge(s_(f"dn{b - 2}_mm"), n_(f"dn{b - 2}_mm", 16))
                    dve.tensor_tensor(slab[2 * (b % 2)][:, m, :], scr[:, m % 2, :], scr[:, m % 2, :], ALU.mult)\
                        .then_inc(s_(f"hid{b}"), 1)
                    dve.wait_ge(s_(f"hid{b}"), own(s_(f"hid{b}")))
                    if m % 2 == 1:
                        after(f"up{b}", m // 2)
                if b == 3:
                    norm_bound("rms_e")
                if b == 0:
                    dve.wait_ge(s_("ln1_mm"), n_("ln1_mm", 8))
                add_into(f"dn{b}", SB, ALPHA if b == 0 else 1.0)
            norm("ln2", "ln", res)
            dve.wait_ge(s_("ln2_y"), TT)
            dve.sem_inc(s_("rms_e_x"), TT)
            norm("rms_e", "rms", normed, SA)

            def decayed(name, banks, o):
                for m in range(4):
                    if m % 2 == 0:
                        before(name, m // 2)
                    dve.wait_ge(s_(name + "_mm"), n_(name + "_mm", m + 1))
                    dve.scalar_tensor_tensor(slab[1][:, o + m, :], banks[m][:, :], undo(name, m // 2), slab[3][:, o + m, :],
                                             ALU.mult, ALU.mult).then_inc(s_(name + "_ev"), 1)
                    if m % 2 == 1:
                        after(name, m // 2)

            for key, slots in (("qf", 2), ("kf", 2), ("vf", 2), ("fl", 1)):
                for i in range(slots):
                    before(key, i)
                    after(key, i)
            dve.wait_ge(s_("decay_in"), 32)
            decayed("qr", SB, 0)
            decayed("kr", SA, 4)
            before("vr", 0)
            dve.wait_ge(s_("fl_ln"), 1)
            dve.memset(frow[3], 1.0).then_inc(dve_chain, 1)
            dve.wait_ge(dve_chain, own(dve_chain))
            dve.scalar_tensor_tensor(frow[2], frow[0], 0.0, frow[1], ALU.min, ALU.subtract).then_inc(dve_chain, 1)
            dve.wait_ge(dve_chain, own(dve_chain))
            dve.tensor_tensor_scan(frow[4], frow[3], frow[2], 0.0, ALU.mult, ALU.add).then_inc(s_("frow"), 1)
            dve.wait_ge(s_("frow"), own(s_("frow")))

            after("vr", 0)
            before("vr", 1)
            after("vr", 1)

            def silu(name, dst):
                for m in range(8):
                    if m % 2 == 0:
                        before(name, m // 2)
                    dve.wait_ge(s_(name + "_sg"), n_(name + "_sg", m + 1))
                    dve.scalar_tensor_tensor(dst[:, m, :], SA[m % 4][:, :], undo(name, m // 2), scr[:, m % 2, :], ALU.mult,
                                             ALU.mult).then_inc(s_(name + "_ev"), 1)
                    if m % 2 == 1:
                        after(name, m // 2)

            silu("ze", slab[5])

            def attention(A):
                n, steps, N = A.name, A.steps, len(A.steps)
                for i in range(N + 1):
                    if i < N:
                        h, b, t = steps[i]
                        w = (t + 1) * P
                        if n == "nsa" and b == 0 and t == 0:
                            dve.tensor_scalar(scr[:, 4 + h % 2, :], dist, SLOPE[h], None, ALU.mult).then_inc(dve_chain, 1)
                            dve.wait_ge(dve_chain, own(dve_chain))
                        dve.wait_ge(s_(n + "_sc"), i + 1)
                        if n == "fox":
                            dve.wait_ge(s_("fox_cb"), h + 1)
                            bias = scr[:, 4 + h % 2, 0:w]
                        else:
                            bias = scr[:, 4 + h % 2, SEQ - w:]
                        if i >= SCR_S:
                            dve.wait_ge(s_(n + "_tp"), i - SCR_S + 1)
                        dve.tensor_tensor_reduce(scr[:, i % SCR_S, 0:w], ps[i % 3][:, 0:w], bias, 1.0, 3e38, ALU.add,
                                                 ALU.min, tmin[:, i % 8:i % 8 + 1]).then_inc(s_(n + "_dm"), 1)
                    if i >= 1:
                        s = i - 1
                        h, b, t = steps[s]
                        w = (t + 1) * P
                        dve.wait_ge(s_(n + "_ex"), s + 1)
                        c = slice(s % 8, s % 8 + 1)
                        dve.reciprocal(trec[:, c], tsum[:, c]).then_inc(dve_chain, 1)
                        dve.wait_ge(dve_chain, own(dve_chain))
                        pr = scr[:, s % SCR_S, 0:w]
                        if n == "fox":
                            ins = dve.tensor_scalar(pr, pr, trec[:, c], None, ALU.mult)
                        else:
                            ins = dve.tensor_scalar(pr, pr, trec[:, c], gates[:, t, 3 * h + 1 + b:3 * h + 2 + b], ALU.mult, ALU.mult)
                        ins.then_inc(s_(n + "_pn"), 1)
                    per = 8 * A.branches
                    if i >= 8 and (i - 8) % per == per - 1:
                        pair_out(A, (i - 8) // per)
                pair_out(A, A.heads // 2 - 1)

            def pair_out(A, m):
                n = A.name
                dve.wait_ge(s_(n + "_pv"), 2 * A.branches * (m + 1))
                ob = OB[0 if n == "fox" else m % 2]
                dve.tensor_tensor(A.y(m), ob[:, :], slab[5][:, m, :], ALU.mult).then_inc(s_(n + "_y"), 1)
                dve.wait_ge(s_(n + "_y"), own(s_(n + "_y")))

            attention(FOX)
            for h in range(8):
                for j in range(TT):
                    dve.wait_ge(s_("rt_ea"), 4 * h + j + 1)
                    dve.tensor_tensor(pT(h)[:, j, j * P:(j + 1) * P], pT(h)[:, j, j * P:(j + 1) * P], tril[:, :], ALU.mult)\
                        .then_inc(s_("rt_ed"), 1)
                    dve.wait_ge(s_("rt_ed"), own(s_("rt_ed")))
                if h % 2 == 1 and h >= 3:
                    ret_out = (h - 3) // 2
                    dve.wait_ge(s_("rt_mu"), ret_out + 1)
                    dve.tensor_tensor(scr[:, 1, :], scr[:, 0, :], SB[2][:, :], ALU.subtract).then_inc(s_("rt_cen"), 1)
                    dve.wait_ge(s_("rt_cen"), own(s_("rt_cen")))
                    dve.wait_ge(s_("rt_rs"), ret_out + 1)
                    dve.scalar_tensor_tensor(scr[:, 4, :], scr[:, 1, :], gng[:, ret_out:ret_out + 1], scr[:, 3, :], ALU.mult, ALU.mult).then_inc(dve_chain, 1)
                    dve.wait_ge(dve_chain, own(dve_chain))
                    dve.tensor_tensor(slab[2][:, 4 + ret_out, :], scr[:, 4, :], slab[5][:, 4 + ret_out, :], ALU.mult)\
                        .then_inc(s_("yr"), 1)
                    dve.wait_ge(s_("yr"), own(s_("yr")))
            ret_out = 3
            dve.wait_ge(s_("rt_mu"), ret_out + 1)
            dve.tensor_tensor(scr[:, 1, :], scr[:, 0, :], SB[2][:, :], ALU.subtract).then_inc(s_("rt_cen"), 1)
            dve.wait_ge(s_("rt_cen"), own(s_("rt_cen")))
            dve.wait_ge(s_("rt_rs"), ret_out + 1)
            dve.scalar_tensor_tensor(scr[:, 4, :], scr[:, 1, :], gng[:, ret_out:ret_out + 1], scr[:, 3, :], ALU.mult, ALU.mult).then_inc(dve_chain, 1)
            dve.wait_ge(dve_chain, own(dve_chain))
            dve.tensor_tensor(slab[2][:, 4 + ret_out, :], scr[:, 4, :], slab[5][:, 4 + ret_out, :], ALU.mult)\
                .then_inc(s_("yr"), 1)
            dve.wait_ge(s_("yr"), own(s_("yr")))
            norm_bound("rms_o")
            add_into("oe", SA, 1.0, done="rms_o_x")
            norm("rms_o", "rms", normed, SB)
            for key, slots in (("kc", 1), ("vc", 1), ("ck", 2)):
                for i in range(slots):
                    before(key, i)
                    after(key, i)

            for x in range(2):
                for m in range(2):
                    c = 2 * x + m
                    dve.wait_ge(s_("hid_sg"), c + 1)
                    dve.scalar_tensor_tensor(hid[x][:, m, :], (SA, SB)[x][m][:, 0:NG * NC], hbias[:, c:c + 1],
                                             hsig[:, 128 * c:128 * c + NG * NC], ALU.add, ALU.mult).then_inc(s_(("hid_k", "hid_v")[x]), 1)
                    dve.wait_ge(s_(("hid_k", "hid_v")[x]), own(s_(("hid_k", "hid_v")[x])))
            for key, slots in (("cv", 2), ("ks", 1), ("kw", 1), ("vs", 1), ("vw", 1)):
                for i in range(slots):
                    before(key, i)
                    after(key, i)
            before("gl")
            for t in range(TT):
                dve.wait_ge(s_("gl_mm"), n_("gl_mm", t + 1))
                dve.scalar_tensor_tensor(gates[:, t, :], SA[t][:, 0:48], undo("gl", 0), bgate[:, :], ALU.mult, ALU.add).then_inc(s_("gl_ev"), 1)
                dve.wait_ge(s_("gl_ev"), own(s_("gl_ev")))
            after("gl")
            for i in range(4):
                before("qo", i)
                after("qo", i)
            silu("zo", slab[5])

            dve.wait_ge(s_("gate"), TT)
            for g in range(NG):
                b = g % 2
                x3 = csc[b].rearrange("p (a n) -> p a n", n=NC)
                if g >= 2:
                    dve.wait_ge(s_("ct_mm"), 4 * (g - 1))
                dve.wait_ge(s_("cs_mm"), g + 1)
                for hg in range(4):
                    c = slice(hg * TT * NC, (hg + 1) * TT * NC)
                    dve.scalar_tensor_tensor(csc[b][:, c], cdist, SLOPE[4 * g + hg],
                                             SA[2 * b + hg % 2][:, hg // 2 * TT * NC:(hg // 2 + 1) * TT * NC], ALU.mult, ALU.add)\
                        .then_inc(s_("cs_ev"), 1)
                    dve.wait_ge(s_("cs_ev"), own(s_("cs_ev")))
                dve.wait_ge(s_("cs_ev"), 4 * g + 4)
                mn, sm, rc = csmall[:, 0, :], csmall[:, 1, :], csmall[:, 2, :]
                dve.tensor_reduce(mn, x3, AX_X, ALU.min).then_inc(dve_chain, 1)
                dve.wait_ge(dve_chain, own(dve_chain))
                dve.tensor_tensor(x3, x3, mn.unsqueeze(2).to_broadcast([P, 16, NC]), ALU.subtract).then_inc(s_("cs_d"), 1)
                dve.wait_ge(s_("cs_d"), own(s_("cs_d")))
                dve.wait_ge(s_("cs_e"), g + 1)
                dve.tensor_reduce(sm, x3, AX_X, ALU.add).then_inc(dve_chain, 1)
                dve.wait_ge(dve_chain, own(dve_chain))
                dve.reciprocal(rc, sm).then_inc(dve_chain, 1)
                dve.wait_ge(dve_chain, own(dve_chain))
                gt = gates[:, :, :].rearrange("p t (h b) -> p b h t", b=3)[:, 0, 4 * g:4 * g + 4, :]
                dve.tensor_tensor(rc.rearrange("p (h t) -> p h t", h=4), rc.rearrange("p (h t) -> p h t", h=4), gt, ALU.mult).then_inc(dve_chain, 1)
                dve.wait_ge(dve_chain, own(dve_chain))
                dve.tensor_tensor(x3, x3, rc.unsqueeze(2).to_broadcast([P, 16, NC]), ALU.mult).then_inc(dve_chain, 1)
                dve.wait_ge(dve_chain, own(dve_chain))
                x4 = csc[b].rearrange("p (h n) -> p h n", h=4)
                dve.tensor_tensor(x4, x4, cmask.unsqueeze(1).to_broadcast([P, 4, TT * NC]), ALU.mult).then_inc(s_("cs_p"), 1)
                dve.wait_ge(s_("cs_p"), own(s_("cs_p")))
            attention(NSA)
            add_into("oo", SA, 1.0, done="rms_f_x")
            norm("rms_f", "rms", res)


_INS = {
    "x": None, "w_in": None, "lb_logits": None, "hgrn_norm_g": None, "w_a": None, "w_pool": None, "pool_scale": None,
    "w_out": None, "ln1_g": None, "ln1_b": None, "w_up": None, "w_down": None, "ln2_g": None, "ln2_b": None,
    "even_norm_g_2": None, "even_w_in_2": None, "even_b_f_2": None, "even_gn_g_2": None, "even_w_out_2": None,
    "odd_norm_g_2": None, "odd_w_in_2": None, "odd_b_gate_2": None, "odd_pe_k_2": None, "odd_pe_v_2": None,
    "odd_wk1_2": None, "odd_wk2_2": None, "odd_wv1_2": None, "odd_wv2_2": None, "odd_w_out_2": None, "final_g_2": None,
}


def kernel(**inputs):
    import numpy as _np
    import concourse.bacc as _bacc
    from concourse import mybir as _mybir
    from concourse.bass_utils import run_bass_kernel_spmd as _run

    nc = _bacc.Bacc("TRN2", target_bir_lowering=False, num_devices=1)
    arrays, args = {}, {}
    for name in _INS:
        a = _np.ascontiguousarray(inputs[name])
        arrays[f"in_{name}"] = a
        args[name] = nc.dram_tensor(f"in_{name}", a.shape, _mybir.dt.from_np(a.dtype), kind="ExternalInput").ap()
    out = nc.dram_tensor("result", (1, SEQ, DM), F32, kind="ExternalOutput").ap()
    build(nc, args, out)
    r = _run(nc, [arrays], core_ids=[0])
    return r.results[0]["result"]
```

```python
from contextlib import ExitStack

import numpy as np
import concourse.bass as bass
from concourse import mybir

F32 = mybir.dt.float32
U32 = mybir.dt.uint32
F16 = mybir.dt.float16
ALU = mybir.AluOpType
ACT = mybir.ActivationFunctionType
AX_X = mybir.AxisListType.X
RMAX = bass.bass_isa.ReduceOp.max

P = 128
SEQ = 512
DM = 1024
TT = SEQ // P
KC = DM // P
SLOTW = 256
NSLOT = 3
NHIGH = 3
EXPONENT = 0x7F800000
TOP = 2.0 ** 14
LEAST = 2.0 ** -100
HEADS_H = 8
CH = 16
D_FF = 4 * DM
HD = 64
NH = 16
NG = 4
NC = 31
LN_EPS = 1e-5
RMS_EPS = 1e-6
GN_EPS = 1e-5
ALPHA = 2.0 ** 0.25
BIG = 1e30


def constants():
    p = np.arange(P)
    c = {}
    c["ident"] = np.eye(P, dtype=np.float32)
    c["ones"] = np.ones((P, P), np.float32)
    c["half_mean"] = np.kron(np.eye(2), np.full((HD, HD), 1.0 / HD)).astype(np.float32)
    s, t = p[:, None], p[None, :]
    lv = [(s // CH == t // CH) & (s <= t)]
    for h in (16, 32):
        lv.append((s // (2 * h) == t // (2 * h)) & (s % (2 * h) < h) & (t % (2 * h) >= h))
    c["levels"] = np.stack(lv, 1).astype(np.uint32).reshape(P, 3 * P)
    c["tril_st"] = (s <= t).astype(np.float32)
    c["ahead"] = np.where(t > s, BIG, 0.0).astype(np.float32)
    r = np.arange(SEQ)[None, :] - (SEQ - P)
    c["dist"] = np.where(r <= s, s - r, 1e32).astype(np.float32)
    end = np.arange(NC) * 16 + 31
    tok = (np.arange(TT)[None, :] * P + p[:, None])[:, :, None]
    c["cdist"] = np.where(end <= tok, tok - end, 1e32).astype(np.float32).reshape(P, TT * NC)
    c["cmask"] = (end <= tok).astype(np.float32).reshape(P, TT * NC)
    c["segment"] = np.broadcast_to((np.arange(SEQ) % CH != 0).astype(np.float32), (P, SEQ)).copy()
    rc = np.stack([w / np.minimum(np.arange(CH) + 1, w) for w in (2, 4, 8, 16)])
    c["edge"] = np.broadcast_to(rc.reshape(1, 4 * CH), (P, 4 * CH)).astype(np.float32).copy()
    sel = np.zeros((8, 8, P), np.float32)
    for h in range(8):
        sel[h, h] = 1.0
    c["sel"] = sel.reshape(8, 8 * P)
    c["eps"] = np.tile(np.array([LN_EPS, RMS_EPS, GN_EPS, 1.0], np.float32), (P, 1))
    lg = np.log(1.0 - 2.0 ** (-5.0 - np.arange(8)))
    pos = np.arange(SEQ)
    up = np.exp(lg[:, None] * pos[None, :])
    dn = np.exp(-lg[:, None] * pos[None, :]) * HD ** -0.5
    both = np.stack([up, dn])
    d = np.repeat(both.reshape(2, 4, 2, 1, SEQ), HD, axis=3)
    c["decay"] = d.reshape(2, 4, P, SEQ).transpose(2, 0, 1, 3).reshape(P, 8 * SEQ).astype(np.float32)
    return c


def diag(flat, first, width):
    step = SEQ + P
    x = flat[:, 0:3 * step + P]
    return bass.AP(tensor=x.tensor, offset=x.offset + first, ap=[list(x.ap[0]), [step, TT], [1, width]])


def slopes():
    return [float(np.float32(2.0 ** (-8.0 * (h + 1) / NH))) for h in range(NH)]


def build(nc, a, out):
    con = constants()
    cd = {k: nc.inline_tensor(v, name=f"const_{k}").ap() for k, v in con.items()}
    ctx = ExitStack()
    with ctx:
        def sb(name, shape, dt=F32):
            return ctx.enter_context(nc.sbuf_tensor(name, shape, dt))

        def sem(name):
            return ctx.enter_context(nc.semaphore(name))

        wring = sb("wring", [P, NSLOT, KC, SLOTW])
        whigh = sb("whigh", [P, NHIGH, KC, SLOTW], F16)
        xT = sb("xT", [P, KC, SEQ])
        slab = [sb(f"slab{i}", [P, 8, SEQ]) for i in range(6)]
        side = sb("side", [P, 18, SEQ])
        res = side[:, 0:8, :].rearrange("p (t h) n -> p t (h n)", t=TT)
        scr = sb("scr", [P, 6, SEQ])
        ident = sb("ident", [P, P])
        ones = sb("ones", [P, P])
        half_mean = sb("half_mean", [P, P])
        tril = sb("tril", [P, P])
        ahead = sb("ahead", [P, P])
        levels = sb("levels", [P, 3, P], U32)
        segment = sb("segment", [P, SEQ])
        edge = sb("edge", [P, 4, CH])
        lbl = sb("lbl", [P, 2, 8])
        lbt = sb("lbt", [P, 5, 8])
        ng = sb("ng", [P, 8])
        psc = sb("psc", [P, 8])
        gng = sb("gng", [P, 4])
        bf_ = sb("bf_", [8, 1])
        bgate = sb("bgate", [P, 48])
        gates = sb("gates", [P, TT, 48])
        eps = sb("eps", [P, 4])
        stat = sb("stat", [P, TT, 20])
        segdec = sb("segdec", [P, 4, 32])
        mulq = sb("mulq", [P, 4, 32])
        mulk = sb("mulk", [P, 4, 32])
        tmin = sb("tmin", [P, 8])
        tsum = sb("tsum", [P, 8])
        trec = sb("trec", [P, 8])
        csmall = sb("csmall", [P, 4, 16])
        hbias = sb("hbias", [P, 4])
        ps = [ctx.enter_context(nc.psum_tensor(f"bank{i}", [P, SEQ], F32)) for i in range(8)]
        SA, SB = ps[0:4], ps[4:8]

        block = ctx.enter_context(nc.Block())

        stream = []
        PAIRED = {"o1", "dn3", "oe", "oo"}

        def cols(w, c0, n=SLOTW):
            return w[:, c0:c0 + n].rearrange("(k p) n -> p k n", p=P)

        def add(key, w, c0, n, tiles=2):
            for i, c in enumerate(range(0, n, SLOTW)):
                m = min(SLOTW, n - c)
                last = 15 if key in PAIRED and i == 2 else tiles * (i + 1)
                stream.append((key, cols(w, c0 + c, m), m, last))

        W = a["w_in"][0]
        add("pool", W, 4096, 1024)
        add("gb", W, 6144, 1024)
        add("f", W, 1024, 1024)
        stream.append(("wp", a["w_pool"][0].rearrange("g (k p) d -> p (g k) d", p=P), SLOTW, 8))
        add("q", W, 0, 1024)
        add("v", W, 2048, 1024, 4)
        for i in range(4):
            for key, c0 in (("og", 3072), ("ga", 5120)):
                stream.append((key, cols(W, c0 + SLOTW * i, SLOTW), SLOTW, 2 * i + 2))
        add("wa", a["w_a"][0], 0, 1024)
        add("o1", a["w_out"][0], 0, 1024, 4)
        MLP = [("up", 0), ("up", 1), ("dn", 0), ("up", 2), ("dn", 1), ("up", 3), ("dn", 2), ("dn", 3)]
        for kind, b in MLP:
            if kind == "up":
                add(f"up{b}", a["w_up"][0], 1024 * b, 1024)
            else:
                add(f"dn{b}", a["w_down"][0][1024 * b:1024 * b + 1024, :], 0, 1024, 4)
        W = a["even_w_in_2"][0]
        add("qf", W, 0, 512)
        add("kf", W, 512, 512)
        add("vf", W, 1024, 512, 4)
        add("fl", W, 1536, 8, 1)
        add("qr", W, 1544, 512)
        add("kr", W, 2056, 512)
        add("vr", W, 2568, 512, 4)
        add("ze", W, 3080, 1024)
        add("oe", a["even_w_out_2"][0], 0, 1024, 4)
        W = a["odd_w_in_2"][0]
        add("kc", W, 1024, 256)
        add("vc", W, 1280, 256)
        for x in "kv":
            for i in range(2):
                stream.append(("c" + x, a[f"odd_w{x}1_2"][0][1024 * i:1024 * i + 1024, :].rearrange("(k p) n -> p k n", p=P), SLOTW, i + 1))
        add("ks", W, 1536, 256)
        add("kw", W, 2048, 256)
        add("vs", W, 1792, 256, 4)
        add("vw", W, 2304, 256, 4)
        add("gl", W, 2560, 48, 4)
        add("qo", W, 0, 1024)
        add("zo", W, 2608, 1024)
        add("oo", a["odd_w_out_2"][0], 0, 1024, 4)

        SPLIT = {"pool", "gb", "f", "q", "v", "og", "ga", "wa", "up0", "up1", "up2", "up3", "dn0", "dn1", "dn2", "dn3", "qf", "kf", "vf", "fl", "qr",
                 "kr", "vr", "ze", "kc", "vc", "ks", "kw", "vs", "vw", "gl", "qo", "zo"}
        split_slots = [i for i, (key, *_) in enumerate(stream) if key in SPLIT]
        NSPLIT = len(split_slots)
        wexp = sb("wexp", [P, NSPLIT])
        wsc = sb("wsc", [P, NSPLIT])
        winv = sb("winv", [P, NSPLIT])
        INPUTS = ("tr0", "gated", "ln1", "rms_e", "rms_o")
        HIDDEN = len(INPUTS)
        xexp = sb("xexp", [P, HIDDEN + 4])
        xsc = sb("xsc", [P, HIDDEN + 4])
        xinv = sb("xinv", [P, HIDDEN + 4])
        xmax = sb("xmax", [P, 4])
        hmax = sb("hmax", [P, 2, 8])
        invq = sb("invq", [P, 12])

        def input_of(i):
            key = stream[i][0]
            if key in ("pool", "gb", "f", "q", "v", "og", "ga"):
                return 0
            if key[:2] == "dn":
                return HIDDEN + int(key[2])
            return 1 if key == "wa" else 2 if key[:2] == "up" else 3 if i < first_slot("kc") else 4

        def first_slot(key):
            return slot_at(key, 0)

        def slot_at(key, slot):
            return [i for i, (k, *_) in enumerate(stream) if k == key][slot]

        def split_index(key, slot=0):
            return split_slots.index(slot_at(key, slot))

        def undo(key, slot):
            n = split_index(key, slot)
            return winv[:, n:n + 1]

        QSLOTS = {key: at for key, at in (("q", 0), ("qf", 4), ("qo", 6))}

        def undo_q(key, slot):
            c = QSLOTS[key] + slot
            return invq[:, c:c + 1]

        def halves(x):
            y = x.rearrange("p k n -> p (k n)").bitcast(F16).rearrange("p (k h n) -> p k h n", k=8, h=2)
            return y[:, :, 0, :], y[:, :, 1, :]

        consts_in = sem("consts_in")
        NCONST = 0
        w_in = [sem(f"w_in{j}") for j in range(NSLOT)]
        x_in = [sem(f"x_in{t}") for t in range(TT)]
        act_chain = sem("act_chain")
        dve_chain = sem("dve_chain")
        S = {}
        mm_done, act_read, dve_read = sem("mm_done"), sem("act_read"), sem("dve_read")
        mlp = [(f"{x}{b}", {"up": 8, "dn": 16}[x]) for x, b in MLP]
        counted = {}
        for s, kind, stages in (
            (mm_done, "_mm", [("tr0", 8), ("pool", 8), ("gb", 8), ("f", 8), ("wp", 8), ("q", 8), ("v", 16), ("wa", 8), ("o1", 16), *mlp, ("qf", 4), ("kf", 4),
                              ("vf", 8), ("fl", 1), ("qr", 4), ("kr", 4), ("vr", 8), ("ze", 8), ("oe", 16),
                              ("kc", 2), ("vc", 2), ("ck", 2), ("cv", 2), ("cmp", 2), ("ks", 2), ("kw", 2), ("vs", 4),
                              ("vw", 4), ("gl", 4), ("qo", 8), ("zo", 8), ("oo", 16)]),
            (act_read, "_ev", [("pool", 8), ("gb", 8), ("f", 8), ("v", 16),
                               *[x for x in mlp if x[0][0] == "u"], ("qf", 4), ("kf", 4), ("vf", 8), ("fl", 1),
                               ("vr", 8), ("kc", 2), ("vc", 2), ("cmp", 2), ("ks", 2), ("kw", 2), ("vs", 4),
                               ("vw", 4), ("qo", 8)]),
            (dve_read, "_ev", [("tr0", 8), ("wp", 8), ("q", 8), ("wa", 8), ("o1", 16),
                               *[x for x in mlp if x[0][0] == "d"], ("qr", 4),
                               ("kr", 4), ("ze", 8), ("oe", 16), ("gl", 4), ("zo", 8), ("oo", 16)]),
        ):
            n = 0
            for stage, results in stages:
                counted[stage + kind] = (s, n)
                n += results

        def s_(name):
            if name in counted:
                return counted[name][0]
            if name not in S:
                S[name] = sem(name)
            return S[name]

        def n_(name, n):
            return n + (counted[name][1] if name in counted else 0)

        def counter():
            counts = {}

            def own(s):
                counts[s] = counts.get(s, 0) + 1
                return counts[s]
            return own

        const_loads = [
            (ones[:, :], cd["ones"]), (half_mean[:, :], cd["half_mean"]),
            (tril[:, :], cd["tril_st"]), (ahead[:, :], cd["ahead"]),
            (levels[:, :, :], cd["levels"].rearrange("p (l n) -> p l n", l=3)),
            (segment[:, :], cd["segment"]),
            (edge[:, :, :], cd["edge"].rearrange("p (l n) -> p l n", l=4)),
            (eps[:, :], cd["eps"]),
            (lbl[:, 0, :], a["lb_logits"][0].rearrange("(k p) -> p k", p=P)),
            (lbl[:, 1, :], a["lb_logits"][1].rearrange("(k p) -> p k", p=P)),
            (ng[:, :], a["hgrn_norm_g"][0].rearrange("(k p) -> p k", p=P)),
            (psc[:, :], a["pool_scale"][0].rearrange("(k p) -> p k", p=P)),
            (gng[:, :], a["even_gn_g_2"][0].rearrange("(k p) -> p k", p=P)),
            (bf_[:, :], a["even_b_f_2"][0].rearrange("(k p) -> k p", p=1)),
            (bgate[:, :], a["odd_b_gate_2"].to_broadcast([P, 48])),
        ]
        NCONST = 16 * len(const_loads)

        def bytok(x):
            return x[:, :, :].rearrange("p (t h) n -> p t (h n)", t=TT)

        ident_in = sem("ident_in")
        gain = {
            "ln1": (scr[:, 2:4, :], a["ln1_g"]), "ln1_b": (scr[:, 4:6, :], a["ln1_b"]),
            "ln2": (scr[:, 2:4, :], a["ln2_g"]), "ln2_b": (scr[:, 4:6, :], a["ln2_b"]),
            "rms_e": (slab[1][:, 0:2, :], a["even_norm_g_2"]), "rms_o": (slab[0][:, 0:2, :], a["odd_norm_g_2"]),
            "rms_f": (bytok(slab[4])[:, 2:4, 512:DM], a["final_g_2"].rearrange("(o n) -> o n", o=1)),
        }

        pooledT, mixT, kT, qT, vslab, gateT = slab
        xhalves = halves(xT[:, :, :])
        ghalves = halves(gateT[:, :, :])

        def hidden(b):
            x = slab[2 * (b % 2)][:, :, :]
            high = slab[4][:, 4 * (b % 2):4 * (b % 2) + 4, :].rearrange("p k n -> p (k n)").bitcast(F16)
            return x, (high.rearrange("p (k n) -> p k n", k=8), halves(x)[0])

        vtok = bytok(vslab)
        prob = slab[0]
        normed = bytok(slab[5])
        pads = side[:, 8:18, :].rearrange("p a n -> p (a n)")
        PADW = SEQ + CH
        vpad = [pads[:, i * PADW:(i + 1) * PADW] for i in (0, 1)]
        wpad = [pads[:, i * PADW:(i + 1) * PADW] for i in (2, 3)]
        frow = [side[0:8, 11 + i, :] for i in range(5)]
        sel = side[0:8, 16:18, :].rearrange("p a (b n) -> p (a b) n", n=P)
        a2 = [slab[2][:, 0:4, :], slab[2][:, 4:8, :]]
        kdup = [slab[3][:, 0:4, :], slab[3][:, 4:8, :]]
        kcmp = vtok[:, 0, 512:512 + NG * NC]
        vcmp = vtok[0:NC, 0, 640:896]
        hid = [vtok[:, 1, 512 + 256 * i:512 + 256 * i + 2 * NG * NC].rearrange("p (m n) -> p m n", m=2) for i in (0, 1)]
        csc = [vtok[:, 2 + i, 512:512 + 16 * NC] for i in (0, 1)]
        hsig = side[:, 11:13, :].rearrange("p a n -> p (a n)")
        dist = side[:, 8, :]
        cdist = side[:, 9, 0:TT * NC]
        cmask = side[:, 9, 256:256 + TT * NC]
        w2 = [side[:, 10, 128 * i:128 * i + 128].rearrange("p (k n) -> p k n", k=2) for i in (0, 1)]
        petab = [side[:, 10, 256 + 16 * i:272 + 16 * i] for i in (0, 1)]

        def pcmp(h):
            return slab[2][0:NC, h, :] if h < 8 else side[0:NC, 2 + h, :]

        SLOPE = slopes()

        class Att:
            def __init__(self, name, heads, branches):
                self.name, self.heads, self.branches = name, heads, branches
                self.steps = [(h, b, t) for h in range(heads) for b in range(branches) for t in range(TT)]

            def q(self, h, t):
                r = h % 2 * HD
                return slab[0][r:r + HD, h // 2, t * P:(t + 1) * P]

            def k(self, h, b, n):
                r = h % 2 * HD
                if self.name == "fox":
                    return slab[0][r:r + HD, 4 + h // 2, 0:n]
                return kdup[b][r:r + HD, h // 4, 0:n]

            def v(self, h, b, j):
                c = h * HD if self.name == "fox" else b * 256 + h // 4 * HD
                return vtok[:, j, c:c + HD]

            def y(self, m):
                return slab[2][:, m, :] if self.name == "fox" else slab[1][:, m, :]

        FOX, NSA = Att("fox", 8, 1), Att("nsa", NH, 2)
        SCR_S = 4
        TPB = ps[3:6]
        OB = ps[6:8]

        def pT(u):
            return xT[:, 4 * (u % 2):4 * (u % 2) + 4, :]

        @block.sync
        def _(sp):
            for t in range(TT):
                sp.dma_start(res[:, t, :], a["x"][0, t * P:(t + 1) * P, :]).then_inc(x_in[t], 16)
                if t == 0:
                    sp.dma_start(ident[:, :], cd["ident"]).then_inc(ident_in, 16)
            for i, (_, src, n, _) in enumerate(stream):
                if i >= NSLOT:
                    key, _, _, results = stream[i - NSLOT]
                    sp.wait_ge(s_(key + "_mm"), n_(key + "_mm", results))
                sp.dma_start(wring[:, i % NSLOT, :, 0:n], src).then_inc(w_in[i % NSLOT], 16)

        @block.gpsimd
        def _(pool):
            def load_gain(name):
                dst, src = gain[name]
                pool.dma_start(dst, src.to_broadcast([P, DM]).rearrange("p (a n) -> p a n", a=2)).then_inc(s_(name + "_gain"), 16)

            pool.wait_ge(s_("x_max"), 1)
            pool.partition_all_reduce(xexp[:, 0:1], xmax[:, 0:1], P, RMAX).then_inc(s_("x_all"), 1)
            for n in range(NSPLIT):
                if n == 2:
                    pool.wait_ge(s_("x_max"), 2)
                    pool.partition_all_reduce(xexp[:, 1:2], xmax[:, 1:2], P, RMAX).then_inc(s_("x_all"), 1)
                if n == split_index("wa", 2):
                    pool.wait_ge(s_("hg_o"), 8)
                    for t in range(TT):
                        pool.dma_start(res[:, t, :], a["x"][0, t * P:(t + 1) * P, :]).then_inc(s_("x_again"), 16)
                    load_gain("ln1")
                    load_gain("ln1_b")
                for b, place in enumerate((("up1", 2), ("dn0", 2), ("dn1", 2), ("dn2", 2))):
                    if n == split_index(*place):
                        pool.wait_ge(s_("hid_max"), b + 1)
                        pool.partition_all_reduce(xexp[:, HIDDEN + b:HIDDEN + b + 1], xmax[:, b:b + 1], P, RMAX).then_inc(s_("hid_all"), 1)
                if n == split_index("up0", 3):
                    pool.wait_ge(s_("ln1_y"), TT)
                    load_gain("ln2")
                    load_gain("ln2_b")
                    pool.wait_ge(s_("o1_mm"), n_("o1_mm", 16))
                    load_gain("rms_e")
                    pool.dma_start(slab[3][:, :, :], cd["decay"].rearrange("p (l n) -> p l n", l=8)).then_inc(s_("decay_in"), 16)
                    pool.dma_start(sel, cd["sel"].rearrange("p (l n) -> p l n", l=8)).then_inc(s_("decay_in"), 16)
                if n == split_index("kc"):
                    pool.wait_ge(s_("fox_pv"), 8)
                    load_gain("rms_o")
                    pool.dma_start(dist, cd["dist"]).then_inc(s_("nsa_in"), 16)
                    pool.dma_start(cdist, cd["cdist"]).then_inc(s_("nsa_in"), 16)
                    pool.dma_start(cmask, cd["cmask"]).then_inc(s_("nsa_in"), 16)
                    for i, x in enumerate("kv"):
                        pool.dma_start(w2[i], a[f"odd_w{x}2_2"][0].rearrange("(k p) n -> p k n", p=P)).then_inc(s_("nsa_in"), 16)
                        for o in range(2):
                            pool.dma_start(petab[i][HD * o:HD * o + HD, :],
                                           a[f"odd_pe_{x}_2"][0].rearrange("(k l) d -> l d k", l=2)[o],
                                           allow_slow_non_contiguous=True).then_inc(s_("nsa_in"), 16)
                pool.wait_ge(s_("w_max"), n + 1)
                pool.partition_all_reduce(wexp[:, n:n + 1], wsc[:, n:n + 1], P, RMAX).then_inc(s_("w_all"), 1)
            pool.wait_ge(s_("ct_mm"), 16)
            load_gain("rms_f")
            for t in range(TT):
                pool.wait_ge(s_("rms_f_y"), t + 1)
                pool.dma_start(out[0, t * P:(t + 1) * P, :], res[:, t, :]).then_inc(s_("stored"), 16)
            pool.wait_ge(s_("stored"), 16 * TT)

        NSA_IN = 9 * 16

        def low_of(i):
            return wring[:, i % NSLOT, :, :].rearrange("p k n -> p (k n)").bitcast(F16)\
                .rearrange("p (k n) -> p k n", k=KC)[:, :, 0:SLOTW]


        @block.tensor
        def _(pe):
            at = [0]

            def slot(key):
                i = at[0]
                assert stream[i][0] == key, (stream[i][0], key)
                at[0] += 1
                if key in SPLIT:
                    n = split_slots.index(i)
                    pe.wait_ge(s_("w_low"), n + 1)
                    return whigh[:, n % NHIGH, :, :], low_of(i)
                pe.wait_ge(w_in[i % NSLOT], 16 * (i // NSLOT + 1))
                return wring[:, i % NSLOT, :, :]

            def feat_tile(name, w, wcol, src, bank, width=P):
                (wh, wl), (xh, xl) = w, src
                for k in range(KC):
                    pe.matmul(bank, wh[:, k, wcol:wcol + width], xh[:, k, :], start=k == 0, stop=False)
                    pe.matmul(bank, wh[:, k, wcol:wcol + width], xl[:, k, :], start=False, stop=False)
                    mm = pe.matmul(bank, wl[:, k, wcol:wcol + width], xh[:, k, :], start=False, stop=k == KC - 1)
                mm.then_inc(s_(name + "_mm"), 1)

            def feat(name, nm, src, banks, first=0, late=None, nlate=1):
                if late:
                    (xh, xl), w = src, [slot(name), slot(name)]
                    for chunks in (range(KC - nlate), range(KC - nlate, KC)):
                        for n in range(4):
                            if chunks[0] > 0 and n == 0:
                                pe.wait_ge(*late)
                            (wh, wl), ww, bank = w[n // 2], slice(n % 2 * P, n % 2 * P + P), banks[n][:, :]
                            for k in chunks:
                                pe.matmul(bank, wh[:, k, ww], xh[:, k, :], start=k == 0, stop=False)
                                pe.matmul(bank, wh[:, k, ww], xl[:, k, :], start=False, stop=False)
                                mm = pe.matmul(bank, wl[:, k, ww], xh[:, k, :], start=False, stop=k == KC - 1)
                            if chunks[0] > 0:
                                mm.then_inc(s_(name + "_mm"), 1)
                    first = 4
                for n in range(first, nm):
                    if n >= 4:
                        pe.wait_ge(s_(name + "_ev"), n_(name + "_ev", n - 3))
                    if n % 2 == 0:
                        w = slot(name)
                    feat_tile(name, w, n % 2 * P, src, banks[n % len(banks)][:, :])

            def tok_tile(name, w, t, src, bank):
                tt = slice(t * P, (t + 1) * P)
                for k in range(KC):
                    if name in SPLIT:
                        (wh, wl), (xh, xl) = w, src
                        width = bank.shape[-1]
                        pe.matmul(bank, xh[:, k, tt], wh[:, k, 0:width], start=k == 0, stop=False)
                        pe.matmul(bank, xh[:, k, tt], wl[:, k, 0:width], start=False, stop=False)
                        mm = pe.matmul(bank, xl[:, k, tt], wh[:, k, 0:width], start=False, stop=k == KC - 1)
                    else:
                        mm = pe.matmul(bank, src[:, k, tt], w[:, k, :], start=k == 0, stop=k == KC - 1)
                mm.then_inc(s_(name + "_mm"), 1)

            def tok(name, nslots, src, banks, width=SLOTW, late=None, nlate=1, between=None):
                if late:
                    w = slot(name)
                    for chunks in (range(KC - nlate), range(KC - nlate, KC)):
                        for t in range(TT):
                            if between and chunks[0] == 0 and t == 1:
                                between()
                            if chunks[0] > 0 and t == 0:
                                pe.wait_ge(*late)
                            for k in chunks:
                                mm = pe.matmul(banks[t][:, 0:width], src[:, k, t * P:(t + 1) * P], w[:, k, :],
                                               start=k == 0, stop=k == KC - 1)
                            if chunks[0] > 0:
                                mm.then_inc(s_(name + "_mm"), 1)
                for s in range(1 if late else 0, nslots):
                    w = slot(name)
                    for t in range(TT):
                        n = s * TT + t
                        if n >= 4:
                            pe.wait_ge(s_(name + "_ev"), n_(name + "_ev", n - 3))
                        tok_tile(name, w, t, src, banks[n % 4][:, 0:width])

            def turn_tile(name, src, banks, t):
                for h in range(2):
                    n = 2 * t + h
                    if n >= len(banks):
                        pe.wait_ge(s_(name + "_ev"), n_(name + "_ev", n - 3))
                    for j in range(4):
                        mm = pe.transpose(banks[n % len(banks)][:, j * P:(j + 1) * P],
                                          src[:, t, (4 * h + j) * P:(4 * h + j + 1) * P], ident[:, :])
                    mm.then_inc(s_(name + "_mm"), 1)

            def tok_and_norm(name, src, banks, norm, nsrc, nbanks, lag, key, fbanks, late, nlate=1, between=None):
                tok(name, 2, src, banks, late=late, nlate=nlate, between=between)
                w2, w3 = slot(name), slot(name)
                for t in range(TT):
                    for s, w in enumerate((w2, w3)):
                        n = 8 + 2 * t + s
                        pe.wait_ge(s_(name + "_ev"), n_(name + "_ev", n - 3))
                        tok_tile(name, w, t, src, banks[n % 4][:, 0:SLOTW])
                    if norm and t >= lag:
                        pe.wait_ge(s_(norm + "_y"), t - lag + 1)
                        turn_tile(norm, nsrc, nbanks, t - lag)
                if not norm:
                    return
                for t in range(TT - lag, TT - 1):
                    pe.wait_ge(s_(norm + "_y"), t + 1)
                    turn_tile(norm, nsrc, nbanks, t)
                pe.wait_ge(s_(name + "_ev"), n_(name + "_ev", 16))
                pe.wait_ge(s_(norm + "_ev"), n_(norm + "_ev", 6))
                wh, wl = slot(key)
                xh, xl = xhalves
                for part in (slice(0, 3 * P), slice(3 * P, SEQ)):
                    if part.start > 0:
                        pe.wait_ge(s_(norm + "_y"), TT)
                        turn_tile(norm, nsrc, nbanks, TT - 1)
                        pe.wait_ge(s_(norm + "_ev"), n_(norm + "_ev", 8))
                    for m in range(2):
                        for k in range(KC):
                            bank, ww = fbanks[m][:, part], slice(m * P, (m + 1) * P)
                            pe.matmul(bank, wh[:, k, ww], xh[:, k, part], start=k == 0, stop=False)
                            pe.matmul(bank, wh[:, k, ww], xl[:, k, part], start=False, stop=False)
                            mm = pe.matmul(bank, wl[:, k, ww], xh[:, k, part], start=False, stop=k == KC - 1)
                        if part.start > 0:
                            mm.then_inc(s_(key + "_mm"), 1)

            def hgrn_scores(h):
                b = h % 2
                K = [side[:, 9 * b + i, :] for i in range(5)]
                Q = [qT[:, h, :]] + [side[:, 9 * b + 5 + i, :] for i in range(4)]
                for i in range(6):
                    r = 6 * h + i
                    if r >= 4:
                        h0, i0 = divmod(r - 4, 6)
                        if i0 < 3:
                            pe.wait_ge(s_("hg_evd"), 3 * h0 + i0 + 1)
                        else:
                            pe.wait_ge(s_("hg_eva"), 3 * h0 + i0 - 2)
                    bank = SA[r % 4]
                    pe.wait_ge(s_("hg_lv"), 6 * h + min(i + 1, 5) + (i >= 4))
                    if i < 4:
                        kk, qq = (kT[:, h, :], Q[0]) if i == 0 else (K[i - 1], Q[i - 1])
                        for j in range(TT):
                            mm = pe.matmul(bank[:, j * P:(j + 1) * P], kk[:, j * P:(j + 1) * P],
                                           qq[:, j * P:(j + 1) * P], start=True, stop=True)
                    elif i == 4:
                        pe.matmul(bank[:, 0:P], K[3][:, 0:P], Q[3][:, P:2 * P], start=True, stop=True)
                        pe.matmul(bank[:, P:3 * P], K[4][:, 0:P], Q[4][:, 2 * P:4 * P], start=True, stop=True)
                        mm = pe.matmul(bank[:, 3 * P:4 * P], K[3][:, 2 * P:3 * P], Q[3][:, 3 * P:4 * P],
                                       start=True, stop=True)
                    else:
                        mm = pe.matmul(bank[:, 0:2 * P], K[4][:, P:2 * P], Q[4][:, 2 * P:4 * P], start=True, stop=True)
                    mm.then_inc(s_("hg_lvl"), 1)

            def hgrn_pv(h):
                pe.wait_ge(s_("hg_evd"), 3 * h + 3)
                pe.wait_ge(s_("hg_eva"), 3 * h + 3)
                if h >= 1:
                    pe.wait_ge(s_("hg_o"), h)
                for j in range(TT):
                    mm = pe.matmul(SB[0][:, j * P:], vtok[:, j, h * P:(h + 1) * P],
                                   prob[:, 4 * (h % 2) + j, j * P:], start=j == 0, stop=j == TT - 1)
                mm.then_inc(s_("hg_pv"), 1)

            def hgrn_ss(h):
                pe.wait_ge(s_("hg_sq"), h + 1)
                if h >= 1:
                    pe.wait_ge(s_("hg_ln"), h)
                pe.matmul(SB[1][:, :], ones[:, :], scr[:, 3 + h % 2, :], start=True, stop=True).then_inc(s_("hg_ss"), 1)

            def attention(A):
                n, steps, N = A.name, A.steps, len(A.steps)
                for i in range(N + 5):
                    if i < N:
                        h, b, t = steps[i]
                        w = (t + 1) * P
                        if n == "fox" and t == 0:
                            if h >= 1:
                                pe.wait_ge(s_("fox_cb"), h)
                            pe.matmul(OB[1][:, :], sel[:, h, :], frow[4], start=True, stop=True).then_inc(s_("fox_c"), 1)
                        if i >= 3:
                            pe.wait_ge(s_(n + "_dm"), i - 2)
                        bank = ps[i % 3]
                        mm = pe.matmul(bank[:, 0:w], A.q(h, t), A.k(h, b, w), start=True, stop=n == "nsa")
                        if n == "fox":
                            mm = pe.matmul(bank[:, t * P:w], ident[:, :], ahead[:, :], start=False, stop=True)
                        mm.then_inc(s_(n + "_sc"), 1)
                    if 3 <= i < N + 3:
                        s = i - 3
                        h, b, t = steps[s]
                        pe.wait_ge(s_(n + "_pn"), s + 1)
                        if s >= 3:
                            pe.wait_ge(s_(n + "_te"), s - 2)
                        for j in range(t + 1):
                            mm = pe.transpose(TPB[s % 3][:, j * P:(j + 1) * P], scr[:, s % SCR_S, j * P:(j + 1) * P], ident[:, :])
                        mm.then_inc(s_(n + "_tp"), 1)
                    if i >= 5 and (i - 5) % 4 == 3:
                        s = i - 5
                        u = s // 4
                        h, b, _ = steps[s]
                        r = h % 2 * HD
                        ob = OB[0 if n == "fox" else h // 2 % 2][r:r + HD, :]
                        pe.wait_ge(s_(n + "_te"), s + 1)
                        if h % 2 == 0 and b == 0:
                            before = h // 2 - (0 if n == "fox" else 1)
                            if before > 0:
                                pe.wait_ge(s_(n + "_y"), before)
                        if n == "nsa" and b == 0:
                            pe.matmul(ob, vcmp[:, h // 4 * HD:(h // 4 + 1) * HD], pcmp(h), start=True, stop=False)
                        for j in range(TT):
                            mm = pe.matmul(ob[:, j * P:], A.v(h, b, j), pT(u)[:, j, j * P:],
                                           start=j == 0 and b == 0 and n == "fox", stop=j == TT - 1 and b == A.branches - 1)
                        mm.then_inc(s_(n + "_pv"), 1)

            def retention():
                def values(h):
                    m, r = h // 2, h % 2 * HD
                    pe.wait_ge(s_("rt_ed"), 4 * h + 4)
                    if h % 2 == 0 and m >= 2:
                        pe.wait_ge(s_("rt_oc"), m - 1)
                    for j in range(TT):
                        mm = pe.matmul(SB[m % 2][r:r + HD, j * P:], vtok[:, j, 512 + h * HD:512 + (h + 1) * HD],
                                       pT(h)[:, j, j * P:], start=j == 0, stop=j == TT - 1)
                    mm.then_inc(s_("rt_pv"), 1)

                def means(m):
                    pe.wait_ge(s_("rt_oc"), m + 1)
                    if m >= 1:
                        pe.wait_ge(s_("rt_cen"), m)
                    pe.matmul(SB[2][:, :], half_mean[:, :], scr[:, 0, :], start=True, stop=True).then_inc(s_("rt_mu"), 1)

                def variances(m):
                    pe.wait_ge(s_("rt_sq"), m + 1)
                    if m >= 1:
                        pe.wait_ge(s_("rt_rs"), m)
                    pe.matmul(SB[3][:, :], half_mean[:, :], scr[:, 2, :], start=True, stop=True).then_inc(s_("rt_var"), 1)

                for h in range(9):
                    if h < 8:
                        m, r = h // 2, h % 2 * HD
                        for j in range(TT):
                            n = 4 * h + j
                            if n >= 4:
                                pe.wait_ge(s_("rt_ea"), n - 3)
                            pe.matmul(SA[j][:, j * P:], slab[1][r:r + HD, 4 + m, j * P:(j + 1) * P],
                                      slab[1][r:r + HD, m, j * P:], start=True, stop=True).then_inc(s_("rt_sc"), 1)
                    if h % 2 == 1 and h >= 3:
                        means((h - 3) // 2)
                    if h >= 1:
                        values(h - 1)
                    if h % 2 == 1 and h >= 3:
                        variances((h - 3) // 2)
                means(3)
                return lambda: variances(3)

            def compress():
                pe.wait_ge(s_("nsa_in"), NSA_IN)
                for x, name in enumerate(("ck", "cv")):
                    banks = (SA, SB)[x]
                    pe.wait_ge(s_(("kc_ev", "vc_ev")[x]), n_(("kc_ev", "vc_ev")[x], 2))
                    for i in range(2):
                        w = slot(name)
                        for k in range(KC):
                            c = KC * i + k
                            blocks = a2[x][:, :, 2 * c:2 * c + 16 * (NC - 1) + 1:16]
                            for m in range(2):
                                wt = w[:, k, m * P:(m + 1) * P]
                                pe.matmul(banks[m][:, 0:NG * NC].rearrange("p (g n) -> p g n", g=NG), wt, blocks,
                                          start=c == 0, stop=c == 15)
                                mm = pe.matmul(banks[2 + m][:, 0:1], wt, petab[x][:, c:c + 1], start=c == 0, stop=c == 15)
                        mm.then_inc(s_(name + "_mm"), 1)
                pe.wait_ge(s_("hid_k"), 2)
                for o in range(2):
                    for m in range(2):
                        mm = pe.matmul(SA[2][o * HD:o * HD + HD, 0:NG * NC], w2[0][:, m, :], hid[0][:, m, :],
                                       start=m == 0, stop=m == 1)
                mm.then_inc(s_("cmp_mm"), 1)
                pe.wait_ge(s_("hid_v"), 2)
                for g in range(NG):
                    for m in range(2):
                        mm = pe.matmul(SB[2][0:NC, g * HD:(g + 1) * HD], hid[1][:, m, g * NC:(g + 1) * NC], w2[1][:, m, :],
                                       start=m == 0, stop=m == 1)
                mm.then_inc(s_("cmp_mm"), 1)

            def compressed_attention():
                for g in range(NG + 1):
                    if g < NG:
                        if g >= 2:
                            pe.wait_ge(s_("cs_ev"), 4 * (g - 1))
                        for hg in range(4):
                            h = 4 * g + hg
                            r = h % 2 * HD
                            for t in range(TT):
                                c = (hg // 2 * TT + t) * NC
                                mm = pe.matmul(SA[2 * (g % 2) + hg % 2][:, c:c + NC], NSA.q(h, t), kcmp[r:r + HD, g * NC:(g + 1) * NC],
                                               start=True, stop=True)
                        mm.then_inc(s_("cs_mm"), 1)
                    if g >= 1:
                        pe.wait_ge(s_("cs_p"), g)
                        for hg in range(4):
                            n = 4 * (g - 1) + hg
                            if n >= 4:
                                pe.wait_ge(s_("ct_ev"), n - 3)
                            for t in range(TT):
                                c = (hg * TT + t) * NC
                                mm = pe.transpose(SB[n % 4][0:NC, t * P:(t + 1) * P], csc[(g - 1) % 2][:, c:c + NC], ident[:, :])
                            mm.then_inc(s_("ct_mm"), 1)

            pe.wait_ge(ident_in, 16)
            for t in range(TT):
                pe.wait_ge(x_in[t], 16)
                turn_tile("tr0", res, ps, t)
            pe.wait_ge(s_("tr0_ev"), n_("tr0_ev", 8))
            feat("pool", 8, xhalves, SA)
            pe.wait_ge(consts_in, NCONST)
            feat("gb", 8, xhalves, SB)
            pe.wait_ge(s_("pool_ev"), n_("pool_ev", 8))
            feat("f", 8, xhalves, SA)
            pe.wait_ge(s_("gb_ev"), n_("gb_ev", 8))
            w = slot("wp")
            for m in range(8):
                pe.wait_ge(s_("pooled"), 2 * (m // 2) + 2)
                if m >= 4:
                    pe.wait_ge(s_("wp_ev"), n_("wp_ev", m - 3))
                for k in range(2):
                    mm = pe.matmul(SB[m % 4][:, :], w[:, m // 2 * 2 + k, m % 2 * P:(m % 2 + 1) * P],
                                   pooledT[:, m // 2 * 2 + k, :], start=k == 0, stop=k == 1)
                mm.then_inc(s_("wp_mm"), 1)
            pe.wait_ge(s_("f_ev"), n_("f_ev", 8))
            feat("q", 8, xhalves, SA)
            pe.wait_ge(s_("wp_ev"), n_("wp_ev", 8))
            tok("v", 4, xhalves, SB)
            pe.wait_ge(s_("q_ev"), n_("q_ev", 8))
            pe.wait_ge(s_("v_ev"), n_("v_ev", 16))
            for h in range(HEADS_H + 2):
                if h >= 2:
                    hgrn_ss(h - 2)
                for key in (("ga", "og"), ("og", "ga"))[h % 2]:
                    if key == "ga" and 1 <= h <= HEADS_H:
                        if h % 2 == 1:
                            wg = slot("ga")
                        if h >= 2:
                            pe.wait_ge(s_("ga_ev"), h - 1)
                        feat_tile("ga", wg, (h - 1) % 2 * P, xhalves, SB[3][:, :])
                    if key == "og" and h < HEADS_H:
                        if h % 2 == 0:
                            wo = slot("og")
                        if h >= 1:
                            pe.wait_ge(s_("og_ev"), h)
                        feat_tile("og", wo, h % 2 * P, xhalves, SB[2][:, :])
                if 1 <= h <= HEADS_H:
                    hgrn_pv(h - 1)
                if h < HEADS_H:
                    hgrn_scores(h)
            pe.wait_ge(s_("hg_evd"), 24)
            pe.wait_ge(s_("hg_eva"), 24)
            pe.wait_ge(s_("ga_ev"), n_("ga_ev", 8))
            pe.wait_ge(s_("gated"), 6)
            feat("wa", 8, ghalves, ps, late=(s_("gated"), 8), nlate=2)
            pe.wait_ge(s_("wa_ev"), n_("wa_ev", 7))
            tok_and_norm("o1", mixT, SA, "ln1", res, SB, 1, "up0", SA, (s_("wa_ev"), n_("wa_ev", 8)))
            for i, (kind, b) in enumerate(MLP):
                banks = (SA, SB)[i % 2]
                if i >= 2:
                    before, bb = MLP[i - 2]
                    pe.wait_ge(s_(f"{before}{bb}_ev"), n_(f"{before}{bb}_ev", 8 if before == "up" else 16))
                if kind == "up":
                    feat(f"up{b}", 8, xhalves, banks, first=0 if b else 2)
                else:
                    pe.wait_ge(s_("hid_low"), 4 * (b + 1))
                    if b < 3:
                        tok(f"dn{b}", 4, hidden(b)[1], banks)
            tok_and_norm("dn3", hidden(3)[1], SB, "rms_e", normed, SA, 2, "qf", SB, None)

            feat("qf", 4, xhalves, SB, first=2)
            feat("kf", 4, xhalves, SA)
            pe.wait_ge(s_("qf_ev"), n_("qf_ev", 4))
            tok("vf", 2, xhalves, SB)
            w = slot("fl")
            pe.wait_ge(s_("kf_ev"), n_("kf_ev", 4))
            feat_tile("fl", w, 0, xhalves, SA[0][0:8, :], width=8)
            pe.wait_ge(s_("vf_ev"), n_("vf_ev", 8))
            feat("qr", 4, xhalves, SB)
            pe.wait_ge(s_("fl_ev"), n_("fl_ev", 1))
            feat("kr", 4, xhalves, SA)
            pe.wait_ge(s_("qr_ev"), n_("qr_ev", 4))
            tok("vr", 2, xhalves, SB)
            pe.wait_ge(s_("kr_ev"), n_("kr_ev", 4))
            feat("ze", 8, xhalves, SA)
            pe.wait_ge(s_("ze_ev"), n_("ze_ev", 8))
            pe.wait_ge(s_("vr_ev"), n_("vr_ev", 8))
            pe.wait_ge(s_("frow"), 1)
            pe.wait_ge(s_("decay_in"), 32)
            attention(FOX)
            pe.wait_ge(s_("fox_y"), 4)
            pe.wait_ge(s_("fox_te"), len(FOX.steps))
            last_variances = retention()
            pe.wait_ge(s_("rt_ea"), 32)
            pe.wait_ge(s_("yr"), 2)
            tok_and_norm("oe", slab[2], SA, "rms_o", normed, SB, 1, "kc", SA, (s_("yr"), 4), nlate=2, between=last_variances)

            feat("vc", 2, xhalves, SB)
            compress()
            pe.wait_ge(s_("cmp_ev"), n_("cmp_ev", 2))
            feat("ks", 2, xhalves, SA)
            feat("kw", 2, xhalves, SB)
            pe.wait_ge(s_("ks_ev"), n_("ks_ev", 2))
            tok("vs", 1, xhalves, SA)
            pe.wait_ge(s_("kw_ev"), n_("kw_ev", 2))
            tok("vw", 1, xhalves, SB)
            pe.wait_ge(s_("vs_ev"), n_("vs_ev", 4))
            tok("gl", 1, xhalves, SA, width=48)
            pe.wait_ge(s_("vw_ev"), n_("vw_ev", 4))
            feat("qo", 8, xhalves, SB)
            pe.wait_ge(s_("gl_ev"), n_("gl_ev", 4))
            feat("zo", 8, xhalves, SA)
            pe.wait_ge(s_("qo_ev"), n_("qo_ev", 8))
            pe.wait_ge(s_("zo_ev"), n_("zo_ev", 8))
            compressed_attention()
            pe.wait_ge(s_("ct_ev"), 16)
            pe.wait_ge(s_("ks_ev"), n_("ks_ev", 2))
            pe.wait_ge(s_("kw_ev"), n_("kw_ev", 2))
            attention(NSA)
            pe.wait_ge(s_("nsa_y"), 7)
            pe.wait_ge(s_("nsa_te"), len(NSA.steps))
            tok_and_norm("oo", slab[1], SA, None, None, None, 0, None, None, (s_("nsa_y"), 8))
            assert at[0] == len(stream)

        @block.scalar
        def _(act):
            own = counter()

            def ev(name, n, dst, func=ACT.Copy, bank=None, **kw):
                act.wait_ge(s_(name + "_mm"), n_(name + "_mm", n + 1))
                act.activation(dst, bank, func, **kw).then_inc(s_(name + "_ev"), 1)
                act.wait_ge(s_(name + "_ev"), own(s_(name + "_ev")))

            def root(name, kind, t):
                act.wait_ge(s_(name + "_v"), t + 1)
                c = 16 if kind == "ln" else 17
                e, sc = (0, 1.0) if kind == "ln" else (1, 1.0 / DM)
                act.activation(stat[:, t, c:c + 1], stat[:, t, c:c + 1], ACT.Sqrt, bias=eps[:, e:e + 1],
                               scale=sc).then_inc(s_(name + "_r"), 1)

            def squares(name, t, x):
                act.wait_ge(s_(x), t + 1)
                act.activation(scr[:, 0:2, :].rearrange("p a n -> p (a n)"), res[:, t, :], ACT.Square,
                               accum_out=stat[:, t, 17:18]).then_inc(s_(name + "_v"), 1)

            def norms(ln, rms, banks, key, x=None):
                lag = 2 if ln and rms else 1
                for t in range(TT):
                    if ln and t >= lag:
                        turned(rms or ln, banks, t - lag)
                    if key and t == 2:
                        high(slot_at(key, 0))
                    if ln:
                        root(ln, "ln", t)
                    if rms:
                        squares(rms, t, x or ln + "_y")
                        root(rms, "rms", t)
                    if not ln and banks and t >= lag:
                        turned(rms, banks, t - lag)
                if banks:
                    for t in range(TT - lag, TT):
                        if t == TT - 1:
                            high(slot_at(key, 1) if key != "kc" else slot_at("vc", 0))
                        turned(rms or ln, banks, t)

            def turned(name, banks, t):
                c = INPUTS.index(name)
                act.wait_ge(s_("x_scale"), c + 1)
                for h in range(2):
                    n = 2 * t + h
                    act.wait_ge(s_(name + "_mm"), n_(name + "_mm", n + 1))
                    act.activation(xhalves[0][:, 4 * h:4 * h + 4, t * P:(t + 1) * P],
                                   banks[n % len(banks)][:, :].rearrange("p (j n) -> p j n", j=4), ACT.Copy,
                                   scale=xsc[:, c:c + 1]).then_inc(s_("x_high"), 1)

            split_before = set()

            def high(i):
                if i < len(stream) and stream[i][0] in SPLIT and i not in split_before:
                    split_before.add(i)
                    n, m = split_slots.index(i), stream[i][2]
                    if n >= NHIGH:
                        key, _, _, results = stream[split_slots[n - NHIGH]]
                        act.wait_ge(s_(key + "_mm"), n_(key + "_mm", results))
                    act.wait_ge(s_("w_scale"), n + 1)
                    act.activation(whigh[:, n % NHIGH, :, 0:m], wring[:, i % NSLOT, :, 0:m], ACT.Copy,
                                   scale=wsc[:, n:n + 1]).then_inc(s_("w_high"), 1)

            def period(key, slot=0):
                high(slot_at(key, slot) + 1)

            def rstd(name, kind, t):
                act.wait_ge(s_(name + "_v"), n_(name + "_v", t + 1))
                v = stat[:, t, 16:17]
                e, sc = (0, 1.0) if kind == "ln" else (1, 1.0 / DM)
                act.activation(v, v, ACT.Ln, bias=eps[:, e:e + 1], scale=sc).then_inc(act_chain, 1)
                act.wait_ge(act_chain, own(act_chain))
                act.activation(v, v, ACT.Exp, scale=-0.5).then_inc(s_(name + "_r"), 1)
                act.wait_ge(s_(name + "_r"), own(s_(name + "_r")))

            for dst, src in const_loads:
                act.dma_start(dst, src, allow_slow_non_contiguous=True).then_inc(consts_in, 16)
            for t in range(TT):
                turned("tr0", ps, t)
            high(0)
            act.wait_ge(s_("pads"), 1)
            for m in range(8):
                if m % 2 == 0:
                    period("pool", m // 2)
                if m >= 2:
                    act.wait_ge(s_("pooled"), m - 1)
                ev("pool", m, vpad[m % 2][:, CH:], bank=SA[m % 4][:, :], scale=undo("pool", m // 2))
            act.wait_ge(s_("lb_d"), 1)
            for i in (1, 2):
                act.activation(lbt[:, i, :], lbt[:, i, :], ACT.Exp).then_inc(s_("lb_e"), 1)
                act.wait_ge(s_("lb_e"), own(s_("lb_e")))
            for m in range(8):
                if m % 2 == 0:
                    period("gb", m // 2)
                ev("gb", m, mixT[:, m, :], ACT.Sigmoid, bank=SB[m % 4][:, :], scale=undo("gb", m // 2))
            for m in range(8):
                if m % 2 == 0:
                    period("f", m // 2)
                ev("f", m, kT[:, m, :], ACT.Sigmoid, bank=SA[m % 4][:, :], scale=undo("f", m // 2))
            period("wp")
            for m in range(8):
                if m % 2 == 0:
                    period("q", m // 2)
                act.wait_ge(s_("q_mm"), n_("q_mm", m + 1))
                if m >= 2:
                    act.wait_ge(s_("q_ev"), n_("q_ev", m - 1))
                act.activation(scr[:, m % 2, :], SA[m % 4][:, :], ACT.Sigmoid, scale=undo("q", m // 2)).then_inc(s_("q_sg"), 1)
                act.wait_ge(s_("q_sg"), own(s_("q_sg")))
            for n in range(16):
                s, t = divmod(n, TT)
                if t == 0:
                    period("v", s)
                ev("v", n, vtok[:, t, s * SLOTW:(s + 1) * SLOTW], bank=SB[n % 4][:, 0:SLOTW], scale=undo("v", s))

            act.wait_ge(s_("q_ev"), n_("q_ev", 8))
            act.wait_ge(s_("lb"), 1)

            def hgrn_gates(h):
                if h < HEADS_H:
                    if h >= 1:
                        act.wait_ge(s_("hg_k1"), h)
                    act.activation(scr[:, 0, :], kT[:, h, :], ACT.Ln, bias=lbt[:, 3, h:h + 1],
                                   scale=lbt[:, 4, h:h + 1]).then_inc(s_("hg_lf"), 1)
                if h >= 2:
                    act.wait_ge(s_("hg_ss"), h - 1)
                    if h >= 3:
                        act.wait_ge(s_("hg_o"), h - 2)
                    act.activation(scr[:, 5, :], SB[1][:, :], ACT.Ln, bias=eps[:, 1:2], scale=1.0 / P).then_inc(s_("hg_ln"), 1)
                if h < HEADS_H:
                    act.wait_ge(s_("hg_G"), h + 1)
                    act.activation(scr[:, 2, :], scr[:, 1, :], ACT.Exp).then_inc(s_("hg_e"), 1)
                    act.activation(scr[:, 0, :], scr[:, 1, :], ACT.Exp, scale=-1.0).then_inc(s_("hg_e"), 1)
                if h >= 2:
                    act.wait_ge(s_("hg_ln"), h - 1)
                    act.activation(scr[:, 5, :], scr[:, 5, :], ACT.Exp, scale=-0.5).then_inc(s_("hg_rs"), 1)

            def hgrn_copies(h):
                p0 = 4 * (h % 2)
                r = 6 * h + 3
                act.wait_ge(s_("hg_lvl"), r + 1)
                act.wait_ge(s_("hg_evd"), 3 * h + 3)
                if h >= 2:
                    act.wait_ge(s_("hg_pv"), h - 1)
                act.activation(diag(prob[0:64, p0:p0 + 4, :].rearrange("p j n -> p (j n)"), 64, 64), SA[r % 4][0:64, :].rearrange("p (j n) -> p j n", j=4)[:, :, 64:P],
                               ACT.Copy).then_inc(s_("hg_eva"), 1)
                act.wait_ge(s_("hg_eva"), own(s_("hg_eva")))
                act.wait_ge(s_("hg_lvl"), r + 2)
                bank = SA[(r + 1) % 4]
                act.activation(prob[:, p0, P:4 * P], bank[:, 0:3 * P], ACT.Copy)
                act.activation(prob[:, p0 + 2, 3 * P:4 * P], bank[:, 3 * P:4 * P], ACT.Copy).then_inc(s_("hg_eva"), 1)
                act.wait_ge(s_("hg_eva"), own(s_("hg_eva")))
                act.wait_ge(s_("hg_lvl"), r + 3)
                act.activation(prob[:, p0 + 1, 2 * P:4 * P], SA[(r + 2) % 4][:, 0:2 * P], ACT.Copy).then_inc(s_("hg_eva"), 1)
                act.wait_ge(s_("hg_eva"), own(s_("hg_eva")))

            def hgrn_square(h):
                act.wait_ge(s_("hg_pv"), h + 1)
                if h >= 2:
                    act.wait_ge(s_("hg_ss"), h - 1)
                act.activation(scr[:, 3 + h % 2, :], SB[0][:, :], ACT.Square).then_inc(s_("hg_sq"), 1)
                act.wait_ge(s_("hg_sq"), own(s_("hg_sq")))

            first_og = first_slot("og")
            for h in range(HEADS_H + 2):
                hgrn_gates(h)
                if 1 <= h <= HEADS_H:
                    hgrn_copies(h - 1)
                    ev("ga", h - 1, kT[:, h - 1, :], ACT.Sigmoid, bank=SB[3][:, :], scale=undo("ga", (h - 1) // 2))
                if h < HEADS_H:
                    ev("og", h, gateT[:, h, :], ACT.Sigmoid, bank=SB[2][:, :], scale=undo("og", h // 2))
                if h <= HEADS_H:
                    high(first_og + h + 1)
                if h >= 2:
                    act.wait_ge(s_("gate_x"), h - 1)
                    act.activation(ghalves[0][:, h - 2, :], qT[:, h - 2, :], ACT.Copy, scale=xsc[:, 1:2]).then_inc(s_("gate_high"), 1)
                if 1 <= h <= HEADS_H:
                    hgrn_square(h - 1)
            high(slot_at("wa", 2))
            for i in range(4):
                period("wa", i)
            norms("ln1", None, SB, "up0")
            for t in range(TT):
                act.activation(res[:, t, :], res[:, t, :], ACT.Copy, scale=ALPHA).then_inc(s_("res_scaled"), 1)

            def hidden_high(b, q):
                act.wait_ge(s_("hid_scale"), b + 1)
                if b >= 2:
                    act.wait_ge(s_(f"dn{b - 2}_mm"), n_(f"dn{b - 2}_mm", 16))
                x, (high_half, _) = hidden(b)
                rows = slice(2 * q, 2 * q + 2)
                act.activation(high_half[:, rows, :], x[:, rows, :], ACT.Copy, scale=xsc[:, HIDDEN + b:HIDDEN + b + 1]).then_inc(s_("hid_high"), 1)

            for i, (kind, b) in enumerate(MLP):
                split_behind = {1: 0, 2: 1, 4: 2, 6: 3}.get(i)
                if kind == "up":
                    for m in range(8):
                        if m % 2 == 0:
                            period(f"up{b}", m // 2)
                        if m >= 2:
                            act.wait_ge(s_(f"hid{b}"), m - 1)
                        elif b > 0:
                            act.wait_ge(s_(f"hid{b - 1}"), 7 + m)
                        ev(f"up{b}", m, scr[:, m % 2, :], ACT.Relu, bank=(SA, SB)[i % 2][m % 4][:, :], scale=undo(f"up{b}", m // 2))
                        if m < 4 and split_behind is not None:
                            hidden_high(split_behind, m)
                elif b < 3:
                    for m in range(4):
                        period(f"dn{b}", m)
                        if m in (1, 2) and split_behind is not None:
                            hidden_high(split_behind, 2 * m - 2)
                            hidden_high(split_behind, 2 * m - 1)
            for i in range(3):
                period("dn3", i)
            norms("ln2", "rms_e", SA, "qf")

            for m in range(4):
                if m % 2 == 0:
                    period("qf", m // 2)
                ev("qf", m, slab[0][:, m, :], bank=SB[m][:, :], scale=undo_q("qf", m // 2))
            for m in range(4):
                if m % 2 == 0:
                    period("kf", m // 2)
                ev("kf", m, slab[0][:, 4 + m, :], bank=SA[m][:, :], scale=undo("kf", m // 2))
            for n in range(8):
                s, t = divmod(n, TT)
                if t == 0:
                    period("vf", s)
                ev("vf", n, vtok[:, t, s * SLOTW:(s + 1) * SLOTW], bank=SB[n % 4][:, 0:SLOTW], scale=undo("vf", s))
            period("fl")
            act.wait_ge(s_("fl_mm"), n_("fl_mm", 1))
            ins = act.activation(frow[0], SA[0][0:8, :], ACT.Identity, bias=bf_[:, 0:1], scale=undo("fl", 0)[0:8, :])
            ins.then_inc(s_("fl_ev"), 1)
            act.wait_ge(s_("fl_ev"), own(s_("fl_ev")))
            act.wait_ge(s_("fl_ev"), n_("fl_ev", 1))
            act.activation(frow[1], frow[0], ACT.Abs).then_inc(act_chain, 1)
            act.wait_ge(act_chain, own(act_chain))
            act.activation(frow[1], frow[1], ACT.Exp, scale=-1.0).then_inc(act_chain, 1)
            act.wait_ge(act_chain, own(act_chain))
            act.activation(frow[1], frow[1], ACT.Ln, bias=eps[0:8, 3:4]).then_inc(s_("fl_ln"), 1)
            act.wait_ge(s_("fl_ln"), own(s_("fl_ln")))
            for i in range(2):
                period("qr", i)
            for i in range(2):
                period("kr", i)
            for n in range(8):
                s, t = divmod(n, TT)
                if t == 0:
                    period("vr", s)
                ev("vr", n, vtok[:, t, 512 + s * SLOTW:512 + (s + 1) * SLOTW], bank=SB[n % 4][:, 0:SLOTW], scale=undo("vr", s))
            for m in range(8):
                if m % 2 == 0:
                    period("ze", m // 2)
                act.wait_ge(s_("ze_mm"), n_("ze_mm", m + 1))
                if m >= 2:
                    act.wait_ge(s_("ze_ev"), n_("ze_ev", m - 1))
                act.activation(scr[:, m % 2, :], SA[m % 4][:, :], ACT.Sigmoid, scale=undo("ze", m // 2)).then_inc(s_("ze_sg"), 1)
                act.wait_ge(s_("ze_sg"), own(s_("ze_sg")))

            def attention(A):
                n, steps, N = A.name, A.steps, len(A.steps)
                for i in range(N + 4):
                    if i >= 4:
                        s = i - 4
                        h, b, t = steps[s]
                        u = s // 4
                        act.wait_ge(s_(n + "_tp"), s + 1)
                        if u >= 2:
                            act.wait_ge(s_(n + "_pv"), u - 1)
                        act.activation(pT(u)[:, 0:t + 1, t * P:(t + 1) * P],
                                       TPB[s % 3][:, 0:(t + 1) * P].rearrange("p (j n) -> p j n", n=P), ACT.Copy).then_inc(s_(n + "_te"), 1)
                    if i < N:
                        h, b, t = steps[i]
                        w = (t + 1) * P
                        if n == "fox" and t == 0:
                            act.wait_ge(s_("fox_c"), h + 1)
                            if h >= 2:
                                act.wait_ge(s_("fox_dm"), 4 * (h - 1))
                            act.activation(scr[:, 4 + h % 2, :], OB[1][:, :], ACT.Copy).then_inc(s_("fox_cb"), 1)
                        act.wait_ge(s_(n + "_dm"), i + 1)
                        act.activation(scr[:, i % SCR_S, 0:w], scr[:, i % SCR_S, 0:w], ACT.Exp, scale=-1.0,
                                       bias=tmin[:, i % 8:i % 8 + 1], accum_out=tsum[:, i % 8:i % 8 + 1]).then_inc(s_(n + "_ex"), 1)

            act.wait_ge(s_("ze_ev"), n_("ze_ev", 8))
            attention(FOX)

            def pair(m):
                act.wait_ge(s_("rt_pv"), 2 * m + 2)
                if m >= 1:
                    act.wait_ge(s_("rt_mu"), m)
                    act.wait_ge(s_("rt_cen"), m)
                act.activation(scr[:, 0, :], SB[m % 2][:, :], ACT.Copy).then_inc(s_("rt_oc"), 1)
                act.wait_ge(s_("rt_oc"), own(s_("rt_oc")))

            def pair_stats(m):
                act.wait_ge(s_("rt_cen"), m + 1)
                if m >= 1:
                    act.wait_ge(s_("rt_var"), m)
                act.activation(scr[:, 2, :], scr[:, 1, :], ACT.Square).then_inc(s_("rt_sq"), 1)
                act.wait_ge(s_("rt_sq"), own(s_("rt_sq")))
                act.wait_ge(s_("rt_var"), m + 1)
                if m >= 1:
                    act.wait_ge(s_("yr"), m)
                act.activation(scr[:, 3, :], SB[3][:, :], ACT.Sqrt, bias=eps[:, 2:3]).then_inc(s_("rt_rs"), 1)

            for h in range(8):
                for j in range(TT):
                    act.wait_ge(s_("rt_sc"), 4 * h + j + 1)
                    if h >= 2:
                        act.wait_ge(s_("rt_pv"), h - 1)
                    act.activation(pT(h)[:, j, j * P:], SA[j][:, j * P:], ACT.Copy).then_inc(s_("rt_ea"), 1)
                    act.wait_ge(s_("rt_ea"), own(s_("rt_ea")))
                if h % 2 == 0 and h >= 2:
                    pair(h // 2 - 1)
                if h % 2 == 1 and h >= 3:
                    pair_stats((h - 3) // 2)
            pair(3)
            pair_stats(3)
            norms(None, "rms_o", SB, "kc", x="oe_x")

            for x, name in enumerate(("kc", "vc")):
                period(name)
                for m in range(2):
                    act.wait_ge(s_(name + "_mm"), n_(name + "_mm", m + 1))
                    bank = (SA, SB)[x][m]
                    for o in range(2):
                        r = slice(o * HD, o * HD + HD)
                        act.activation(a2[x][0:HD, 2 * m + o, :], bank[r, :], ACT.Copy, scale=undo(name, 0)[r, :])
                        ins = act.activation(a2[x][HD:P, 2 * m + o, 0:SEQ - 1], bank[r, 1:SEQ], ACT.Copy, scale=undo(name, 0)[r, :])
                    ins.then_inc(s_(name + "_ev"), 1)
                    act.wait_ge(s_(name + "_ev"), own(s_(name + "_ev")))
            for x in range(2):
                if x == 1:
                    period("cv", 1)
                act.wait_ge(s_(("ck_mm", "cv_mm")[x]), n_(("ck_mm", "cv_mm")[x], 2))
                for m in range(2):
                    c = 2 * x + m
                    banks = (SA, SB)[x]
                    act.activation(hbias[:, c:c + 1], banks[2 + m][:, 0:1], ACT.Copy).then_inc(act_chain, 1)
                    act.wait_ge(act_chain, own(act_chain))
                    act.activation(hsig[:, 128 * c:128 * c + NG * NC], banks[m][:, 0:NG * NC], ACT.Sigmoid,
                                   bias=hbias[:, c:c + 1]).then_inc(s_("hid_sg"), 1)
                    act.wait_ge(s_("hid_sg"), own(s_("hid_sg")))
            act.wait_ge(s_("cmp_mm"), n_("cmp_mm", 1))
            act.activation(kcmp, SA[2][:, 0:NG * NC], ACT.Copy).then_inc(s_("cmp_ev"), 1)
            act.wait_ge(s_("cmp_ev"), own(s_("cmp_ev")))
            act.wait_ge(s_("cmp_mm"), n_("cmp_mm", 2))
            act.activation(vcmp, SB[2][0:NC, 0:256], ACT.Copy).then_inc(s_("cmp_ev"), 1)
            act.wait_ge(s_("cmp_ev"), own(s_("cmp_ev")))
            for x, name in enumerate(("ks", "kw")):
                period(name)
                for m in range(2):
                    act.wait_ge(s_(name + "_mm"), n_(name + "_mm", m + 1))
                    for o in range(2):
                        r = slice(o * HD, o * HD + HD)
                        act.activation(kdup[x][0:HD, 2 * m + o, :], (SA, SB)[x][m][r, :], ACT.Copy, scale=undo(name, 0)[r, :])
                        ins = act.activation(kdup[x][HD:P, 2 * m + o, :], (SA, SB)[x][m][r, :], ACT.Copy, scale=undo(name, 0)[r, :])
                    ins.then_inc(s_(name + "_ev"), 1)
                    act.wait_ge(s_(name + "_ev"), own(s_(name + "_ev")))
            for x, name in enumerate(("vs", "vw")):
                period(name)
                for t in range(TT):
                    ev(name, t, vtok[:, t, x * 256:x * 256 + 256], bank=(SA, SB)[x][t][:, 0:256], scale=undo(name, 0))
            period("gl")
            for m in range(8):
                if m % 2 == 0:
                    period("qo", m // 2)
                ev("qo", m, slab[0][:, m, :], bank=SB[m % 4][:, :], scale=undo_q("qo", m // 2))
            for t in range(TT):
                act.wait_ge(s_("gl_ev"), n_("gl_ev", t + 1))
                act.activation(gates[:, t, :], gates[:, t, :], ACT.Sigmoid).then_inc(s_("gate"), 1)
                act.wait_ge(s_("gate"), own(s_("gate")))
            for m in range(8):
                if m % 2 == 0:
                    period("zo", m // 2)
                act.wait_ge(s_("zo_mm"), n_("zo_mm", m + 1))
                if m >= 2:
                    act.wait_ge(s_("zo_ev"), n_("zo_ev", m - 1))
                act.activation(scr[:, m % 2, :], SA[m % 4][:, :], ACT.Sigmoid, scale=undo("zo", m // 2)).then_inc(s_("zo_sg"), 1)
                act.wait_ge(s_("zo_sg"), own(s_("zo_sg")))
            for g in range(NG + 1):
                if g < NG:
                    act.wait_ge(s_("cs_d"), g + 1)
                    act.activation(csc[g % 2], csc[g % 2], ACT.Exp, scale=-1.0).then_inc(s_("cs_e"), 1)
                    act.wait_ge(s_("cs_e"), own(s_("cs_e")))
                if g >= 1:
                    for hg in range(4):
                        n = 4 * (g - 1) + hg
                        act.wait_ge(s_("ct_mm"), n + 1)
                        act.activation(pcmp(n), SB[n % 4][0:NC, :], ACT.Copy).then_inc(s_("ct_ev"), 1)
                        act.wait_ge(s_("ct_ev"), own(s_("ct_ev")))
            attention(NSA)
            norms(None, "rms_f", None, None, x="oo_x")

        @block.vector
        def _(dve):
            own = counter()

            def scale_of(e, sc, inv, factor):
                dve.tensor_scalar(e, e, LEAST, None, ALU.max).then_inc(dve_chain, 1)
                dve.wait_ge(dve_chain, own(dve_chain))
                dve.tensor_scalar(e.bitcast(U32), e.bitcast(U32), EXPONENT, None, ALU.bitwise_and).then_inc(dve_chain, 1)
                dve.wait_ge(dve_chain, own(dve_chain))
                if factor is None:
                    dve.tensor_scalar(inv, e, 1.0 / TOP, None, ALU.mult)
                else:
                    dve.tensor_scalar(inv, e, 1.0 / TOP, factor, ALU.mult, ALU.mult)
                dve.reciprocal(sc, e).then_inc(dve_chain, 1)
                dve.wait_ge(dve_chain, own(dve_chain))
                return dve.tensor_scalar(sc, sc, TOP, None, ALU.mult)

            def input_scale(name):
                c = slice(INPUTS.index(name), INPUTS.index(name) + 1)
                scale_of(xexp[:, c], xsc[:, c], xinv[:, c], None).then_inc(s_("x_scale"), 1)
                dve.wait_ge(s_("x_scale"), own(s_("x_scale")))

            def norm_bound(name):
                c = slice(INPUTS.index(name), INPUTS.index(name) + 1)
                dve.wait_ge(s_(name + "_gain"), 16)
                dve.tensor_reduce(xexp[:, c], gain[name][0], mybir.AxisListType.XY, ALU.max, apply_absolute_value=True).then_inc(dve_chain, 1)
                dve.wait_ge(dve_chain, own(dve_chain))
                if name == "ln1":
                    dve.wait_ge(s_(name + "_b_gain"), 16)
                    dve.tensor_reduce(xmax[:, 2:3], gain["ln1_b"][0], mybir.AxisListType.XY, ALU.max, apply_absolute_value=True)
                    dve.tensor_scalar(xexp[:, c], xexp[:, c], float(DM) ** 0.5, None, ALU.mult).then_inc(dve_chain, 1)
                    dve.wait_ge(dve_chain, own(dve_chain))
                    dve.tensor_tensor(xexp[:, c], xexp[:, c], xmax[:, 2:3], ALU.add).then_inc(dve_chain, 1)
                else:
                    dve.tensor_scalar(xexp[:, c], xexp[:, c], float(DM) ** 0.5, None, ALU.mult).then_inc(dve_chain, 1)
                dve.wait_ge(dve_chain, own(dve_chain))
                input_scale(name)

            measured, split_before = set(), set()

            def measure(i):
                if i < len(stream) and stream[i][0] in SPLIT and i not in measured:
                    measured.add(i)
                    key, _, m, _ = stream[i]
                    n = split_slots.index(i)
                    c = slice(n, n + 1)
                    dve.wait_ge(w_in[i % NSLOT], 16 * (i // NSLOT + 1))
                    dve.tensor_reduce(wsc[:, c], wring[:, i % NSLOT, :, 0:m], mybir.AxisListType.XY, ALU.max,
                                      apply_absolute_value=True).then_inc(s_("w_max"), 1)
                    dve.wait_ge(s_("w_all"), n + 1)
                    x = input_of(i)
                    last = scale_of(wexp[:, c], wsc[:, c], winv[:, c], xinv[:, x:x + 1])
                    if key in QSLOTS:
                        q = QSLOTS[key] + i - first_slot(key)
                        last = dve.tensor_scalar(invq[:, q:q + 1], winv[:, c], float(P) ** -0.5 if key == "q" else -HD ** -0.5,
                                                 None, ALU.mult)
                    last.then_inc(s_("w_scale"), 1)
                    dve.wait_ge(s_("w_scale"), own(s_("w_scale")))

            def low(i):
                if i < len(stream) and stream[i][0] in SPLIT and i not in split_before:
                    split_before.add(i)
                    n, m = split_slots.index(i), stream[i][2]
                    dve.wait_ge(s_("w_high"), n + 1)
                    dve.scalar_tensor_tensor(low_of(i)[:, :, 0:m], wring[:, i % NSLOT, :, 0:m], wsc[:, n:n + 1],
                                             whigh[:, n % NHIGH, :, 0:m], ALU.mult, ALU.subtract).then_inc(s_("w_low"), 1)

            def before(key, slot=0):
                low(slot_at(key, slot) + 1)

            def after(key, slot=0):
                measure(slot_at(key, slot) + 2)

            def turned_low(name, banks, t):
                i = INPUTS.index(name)
                for h in range(2):
                    n = 2 * t + h
                    dve.wait_ge(s_("x_high"), 8 * (i - (i > 0)) + n + 1)
                    dve.scalar_tensor_tensor(xhalves[1][:, 4 * h:4 * h + 4, t * P:(t + 1) * P],
                                             banks[n % len(banks)][:, :].rearrange("p (j n) -> p j n", j=4), xsc[:, i:i + 1],
                                             xhalves[0][:, 4 * h:4 * h + 4, t * P:(t + 1) * P], ALU.mult,
                                             ALU.subtract).then_inc(s_(name + "_ev"), 1)

            def folded(x):
                return x.rearrange("p (a n) -> p a n", a=2)

            def layer_norm(name, t):
                x = folded(res[:, t, :])
                for i in range(2):
                    ins = dve.bn_stats(stat[:, t, 6 * i:6 * i + 6], res[:, t, i * 512:(i + 1) * 512])
                ins.then_inc(dve_chain, 1)
                dve.wait_ge(dve_chain, own(dve_chain))
                dve.bn_aggr(stat[:, t, 15:17], stat[:, t, 0:12]).then_inc(s_(name + "_v"), 1)
                dve.wait_ge(s_(name + "_v"), t + 1)
                dve.scalar_tensor_tensor(x, x, stat[:, t, 15:16], gain[name][0], ALU.subtract, ALU.mult).then_inc(dve_chain, 1)
                return own(dve_chain)

            def layer_norm_end(name, t, scaled):
                x = folded(res[:, t, :])
                dve.wait_ge(s_(name + "_r"), t + 1)
                dve.wait_ge(dve_chain, scaled)
                dve.reciprocal(stat[:, t, 16:17], stat[:, t, 16:17]).then_inc(dve_chain, 1)
                dve.wait_ge(dve_chain, own(dve_chain))
                dve.scalar_tensor_tensor(x, x, stat[:, t, 16:17], gain[name + "_b"][0], ALU.mult, ALU.add).then_inc(s_(name + "_y"), 1)

            def rms_norm(name, dst, t):
                dve.wait_ge(s_(name + "_r"), t + 1)
                dve.reciprocal(stat[:, t, 17:18], stat[:, t, 17:18]).then_inc(dve_chain, 1)
                dve.wait_ge(dve_chain, own(dve_chain))
                dve.scalar_tensor_tensor(folded(dst[:, t, :]), folded(res[:, t, :]), stat[:, t, 17:18], gain[name][0],
                                         ALU.mult, ALU.mult).then_inc(s_(name + "_y"), 1)

            def add(name, n, s, t, banks, alpha):
                dve.wait_ge(s_(name + "_mm"), n_(name + "_mm", n + 1))
                r = res[:, t, s * SLOTW:(s + 1) * SLOTW]
                if name in SPLIT:
                    ins = dve.scalar_tensor_tensor(r, banks[n % 4][:, 0:SLOTW], undo(name, s), r, ALU.mult, ALU.add)
                else:
                    ins = dve.scalar_tensor_tensor(r, r, alpha, banks[n % 4][:, 0:SLOTW], ALU.mult, ALU.add)
                ins.then_inc(s_(name + "_ev"), 1)

            def add_into(name, banks, block):
                if block is not None:
                    hidden_scale(block)
                for s in range(4):
                    before(name, s)
                    for t in range(TT):
                        add(name, 4 * s + t, s, t, banks, 1.0)
                        if t == 0 and block is not None and s >= 1:
                            hidden_low(block, s - 1)
                        if t == 1:
                            after(name, s)
                        if (s, t) == (3, 1) and block is not None:
                            hidden_low(block, 3)

            def hidden_scale(b):
                dve.wait_ge(s_("hid_rows"), 8 * (b + 1))
                dve.tensor_reduce(xmax[:, b:b + 1], hmax[:, b % 2, :], AX_X, ALU.max).then_inc(s_("hid_max"), 1)
                c = slice(HIDDEN + b, HIDDEN + b + 1)
                dve.wait_ge(s_("hid_all"), b + 1)
                scale_of(xexp[:, c], xsc[:, c], xinv[:, c], None).then_inc(s_("hid_scale"), 1)
                dve.wait_ge(s_("hid_scale"), b + 1)

            def hidden_low(b, q):
                dve.wait_ge(s_("hid_high"), 4 * b + q + 1)
                x, (high_half, low_half) = hidden(b)
                rows = slice(2 * q, 2 * q + 2)
                dve.scalar_tensor_tensor(low_half[:, rows, :], x[:, rows, :], xsc[:, HIDDEN + b:HIDDEN + b + 1],
                                         high_half[:, rows, :], ALU.mult, ALU.subtract).then_inc(s_("hid_low"), 1)

            def add_and_norm(name, banks, alpha, ln, rms, dst, nbanks, key):
                for s in range(2):
                    before(name, s)
                    if s == 1:
                        measure(slot_at(name, 3))
                    for t in range(TT):
                        add(name, 4 * s + t, s, t, banks, alpha)
                        if t == 1:
                            after(name, s)
                low(slot_at(name, 3))
                for g in ([ln, ln + "_b"] if ln else []) + ([rms] if rms else []):
                    dve.wait_ge(s_(g + "_gain"), 16)
                for t in range(TT):
                    for s in (2, 3):
                        add(name, 8 + 2 * t + s - 2, s, t, banks, alpha)
                    dve.wait_ge(s_(name + "_ev"), n_(name + "_ev", 10 + 2 * t))
                    if ln:
                        if rms and t >= 1:
                            rms_norm(rms, dst, t - 1)
                        scaled = layer_norm(ln, t)
                        lag = 2 if rms else 1
                        if t >= lag:
                            turned_low(rms or ln, nbanks, t - lag)
                        layer_norm_end(ln, t, scaled)
                    else:
                        dve.sem_inc(s_(name + "_x"), 1)
                        rms_norm(rms, dst, t)
                        if nbanks and t >= 1:
                            turned_low(rms, nbanks, t - 1)
                    if key and t == 1:
                        measure(slot_at(key, 0))
                    if key and t == 2:
                        low(slot_at(key, 0))
                if rms and ln:
                    turned_low(rms, nbanks, 2)
                    rms_norm(rms, dst, TT - 1)
                if nbanks:
                    following = slot_at("vc", 0) if key == "kc" else slot_at(key, 1)
                    measure(following)
                    low(following)
                    turned_low(rms or ln, nbanks, 3)

            dve.memset(pads[:, 0:4 * PADW], 0.0).then_inc(s_("pads"), 1)
            dve.wait_ge(s_("pads"), own(s_("pads")))
            for t in range(TT):
                dve.wait_ge(x_in[t], 16)
                dve.tensor_reduce(xmax[:, t:t + 1], res[:, t, :], AX_X, ALU.max, apply_absolute_value=True).then_inc(dve_chain, 1)
                dve.wait_ge(dve_chain, own(dve_chain))
            dve.tensor_reduce(xmax[:, 0:1], xmax[:, 0:4], AX_X, ALU.max).then_inc(s_("x_max"), 1)
            dve.wait_ge(s_("x_all"), 1)
            input_scale("tr0")
            turned_low("tr0", ps, 0)
            measure(0)
            for t in range(1, TT):
                turned_low("tr0", ps, t)
            low(0)
            measure(1)
            dve.wait_ge(consts_in, NCONST)
            dve.tensor_reduce(xmax[:, 1:2], ng[:, :], AX_X, ALU.max, apply_absolute_value=True).then_inc(s_("x_max"), 1)
            dve.wait_ge(s_("x_all"), 2)
            dve.tensor_scalar(xexp[:, 1:2], xexp[:, 1:2], float(P) ** 0.5, None, ALU.mult).then_inc(dve_chain, 1)
            dve.wait_ge(dve_chain, own(dve_chain))
            input_scale("gated")
            mx, l0, l1 = lbt[:, 0, :], lbt[:, 1, :], lbt[:, 2, :]
            dve.tensor_tensor(mx, lbl[:, 0, :], lbl[:, 1, :], ALU.max).then_inc(dve_chain, 1)
            dve.wait_ge(dve_chain, own(dve_chain))
            dve.tensor_tensor(l0, lbl[:, 0, :], mx, ALU.subtract).then_inc(dve_chain, 1)
            dve.wait_ge(dve_chain, own(dve_chain))
            dve.tensor_tensor(l1, lbl[:, 1, :], mx, ALU.subtract).then_inc(s_("lb_d"), 1)
            dve.wait_ge(s_("lb_d"), own(s_("lb_d")))
            for m in range(8):
                g = m // 2
                if m % 2 == 0:
                    before("pool", g)
                dve.wait_ge(s_("pool_ev"), n_("pool_ev", m + 1))
                v = vpad[m % 2]
                cur = v
                for j in range(g + 1):
                    d = 1 << j
                    dst = wpad[j % 2]
                    dve.tensor_tensor(dst[:, CH:], cur[:, CH:], cur[:, CH - d:PADW - d], ALU.add).then_inc(dve_chain, 1)
                    dve.wait_ge(dve_chain, own(dve_chain))
                    cur = dst
                dve.tensor_tensor(cur[:, CH:2 * CH], cur[:, CH:2 * CH], edge[:, g, :], ALU.mult).then_inc(dve_chain, 1)
                dve.wait_ge(dve_chain, own(dve_chain))
                dve.scalar_tensor_tensor(pooledT[:, m, :], cur[:, CH:], 0.5 ** (g + 1), v[:, CH:], ALU.mult,
                                         ALU.subtract).then_inc(s_("pooled"), 1)
                dve.wait_ge(s_("pooled"), own(s_("pooled")))
                if m % 2 == 0:
                    after("pool", g)
            for i in range(4):
                before("gb", i)
                after("gb", i)
            for i in range(4):
                before("f", i)
                after("f", i)
            before("wp")
            for m in range(8):
                dve.wait_ge(s_("wp_mm"), n_("wp_mm", m + 1))
                dve.wait_ge(s_("gb_ev"), n_("gb_ev", m + 1))
                dve.scalar_tensor_tensor(mixT[:, m, :], SB[m % 4][:, :], psc[:, m:m + 1], mixT[:, m, :], ALU.mult,
                                         ALU.mult).then_inc(s_("wp_ev"), 1)
                dve.wait_ge(s_("wp_ev"), own(s_("wp_ev")))
            after("wp")
            for m in range(8):
                if m % 2 == 0:
                    before("q", m // 2)
                dve.wait_ge(s_("q_sg"), m + 1)
                dve.scalar_tensor_tensor(qT[:, m, :], SA[m % 4][:, :], undo_q("q", m // 2), scr[:, m % 2, :], ALU.mult,
                                         ALU.mult).then_inc(s_("q_ev"), 1)
                dve.wait_ge(s_("q_ev"), own(s_("q_ev")))
                if m % 2 == 1:
                    after("q", m // 2)
            dve.wait_ge(s_("lb_e"), 2)
            dve.tensor_tensor(mx, l0, l1, ALU.add).then_inc(dve_chain, 1)
            dve.wait_ge(dve_chain, own(dve_chain))
            dve.reciprocal(mx, mx).then_inc(dve_chain, 1)
            dve.wait_ge(dve_chain, own(dve_chain))
            dve.tensor_tensor(lbt[:, 3, :], l0, mx, ALU.mult).then_inc(dve_chain, 1)
            dve.wait_ge(dve_chain, own(dve_chain))
            dve.tensor_scalar(lbt[:, 4, :], lbt[:, 3, :], -1.0, 1.0, ALU.mult, ALU.add).then_inc(dve_chain, 1)
            dve.wait_ge(dve_chain, own(dve_chain))
            dve.tensor_scalar(lbt[:, 0, :], lbt[:, 4, :], -1.0, None, ALU.mult).then_inc(s_("lb"), 1)
            dve.wait_ge(s_("lb"), own(s_("lb")))
            dve.wait_ge(s_("lb"), 1)
            for i in range(4):
                before("v", i)
                after("v", i)
            dve.memset(mulq[:, :, :], 1.0).then_inc(dve_chain, 1)
            dve.wait_ge(dve_chain, own(dve_chain))
            dve.memset(mulk[:, :, :], 1.0).then_inc(dve_chain, 1)
            dve.wait_ge(dve_chain, own(dve_chain))
            dve.wait_ge(s_("wp_mm"), n_("wp_mm", 8))
            dve.memset(prob[:, :, :], 0.0).then_inc(dve_chain, 1)
            dve.wait_ge(dve_chain, own(dve_chain))

            def hgrn_levels(h):
                b = h % 2
                K = [side[:, 9 * b + i, :] for i in range(5)]
                Q = [qT[:, h, :]] + [side[:, 9 * b + 5 + i, :] for i in range(4)]

                def by(x, n):
                    return x.rearrange("p (s w) -> p s w", s=n)

                def wide(x, n, w):
                    return x.unsqueeze(2).to_broadcast([P, n, w])

                def joins(l):
                    n = 32 >> l
                    seg = segdec[:, l, 0:n].rearrange("p (i o) -> p i o", o=2)
                    mq = mulq[:, l, 0:n].rearrange("p (i o) -> p i o", o=2)
                    mk = mulk[:, l, 0:n].rearrange("p (i o) -> p i o", o=2)
                    dve.tensor_copy(mq[:, :, 1], seg[:, :, 0])
                    if l < 3:
                        dve.tensor_tensor(segdec[:, l + 1, 0:n // 2], seg[:, :, 0], seg[:, :, 1], ALU.mult)
                    dve.tensor_copy(mk[:, :, 0], seg[:, :, 1]).then_inc(dve_chain, 1)

                dve.wait_ge(s_("hg_e"), 2 * h + 2)
                dve.tensor_copy(segdec[:, 0, :], by(scr[:, 2, :], 32)[:, :, CH - 1]).then_inc(dve_chain, 1)
                segdec_there = own(dve_chain)
                dve.tensor_tensor(Q[0], Q[0], scr[:, 2, :], ALU.mult)
                dve.tensor_tensor(kT[:, h, :], kT[:, h, :], scr[:, 0, :], ALU.mult).then_inc(s_("hg_lv"), 1)
                dve.wait_ge(dve_chain, segdec_there)
                joins(0)
                joined = own(dve_chain)
                dve.wait_ge(s_("hg_lv"), 6 * h + 1)
                dve.sem_inc(s_("hg_k1"), 1)
                if h >= 2:
                    dve.wait_ge(s_("hg_lvl"), 6 * (h - 1))
                dve.tensor_tensor(by(K[0], 32), by(kT[:, h, :], 32), wide(segdec[:, 0, :], 32, CH), ALU.mult)\
                    .then_inc(s_("hg_lv"), 1)
                for l in range(4):
                    n, w = 32 >> l, CH << l
                    dve.wait_ge(dve_chain, joined)
                    if l < 3:
                        joins(l + 1)
                        joined = own(dve_chain)
                    dve.wait_ge(s_("hg_lv"), 6 * h + 2 + l)
                    if l < 3:
                        dve.tensor_tensor(by(Q[l + 1], n), by(Q[l], n), wide(mulq[:, l, 0:n], n, w), ALU.mult)
                        ins = dve.tensor_tensor(by(K[l + 1], n), by(K[l], n), wide(mulk[:, l, 0:n], n, w), ALU.mult)
                    else:
                        dve.tensor_tensor(by(Q[4], 4)[:, 2:4, :], by(Q[3], 4)[:, 2:4, :], wide(mulq[:, 3, 2:4], 2, w), ALU.mult)
                        ins = dve.tensor_tensor(by(K[4], 4)[:, 0:2, :], by(K[3], 4)[:, 0:2, :], wide(mulk[:, 3, 0:2], 2, w), ALU.mult)
                    ins.then_inc(s_("hg_lv"), 1)

            def hgrn_cumulate(h):
                dve.wait_ge(s_("hg_lf"), h + 1)
                if h >= 1:
                    dve.wait_ge(s_("hg_e"), 2 * h)
                dve.tensor_tensor_scan(scr[:, 1, :], segment[:, :], scr[:, 0, :], 0.0, ALU.mult, ALU.add).then_inc(s_("hg_G"), 1)
                dve.tensor_scalar(kT[:, h, :], kT[:, h, :], lbt[:, 0, h:h + 1], lbt[:, 4, h:h + 1], ALU.mult, ALU.add).then_inc(dve_chain, 1)
                dve.wait_ge(dve_chain, own(dve_chain))

            def hgrn_masks(h):
                p0 = 4 * (h % 2)
                for i in range(3):
                    r = 6 * h + i
                    dve.wait_ge(s_("hg_lvl"), r + 1)
                    if h >= 2:
                        dve.wait_ge(s_("hg_pv"), h - 1)
                    dve.copy_predicated(diag(prob[:, p0:p0 + 4, :].rearrange("p j n -> p (j n)"), 0, P),
                                        levels[:, i, :].unsqueeze(1).to_broadcast([P, 4, P]),
                                        SA[r % 4][:, :].rearrange("p (j n) -> p j n", j=4)).then_inc(s_("hg_evd"), 1)
                    dve.wait_ge(s_("hg_evd"), r - 3 * h + 1)

            def hgrn_out(h):
                dve.wait_ge(s_("hg_rs"), h + 1)
                dve.scalar_tensor_tensor(qT[:, h, :], SB[0][:, :], ng[:, h:h + 1], scr[:, 5, :], ALU.mult, ALU.mult)\
                    .then_inc(s_("hg_o"), 1)
                dve.wait_ge(s_("og_ev"), h + 1)
                dve.wait_ge(s_("hg_o"), h + 1)
                dve.tensor_tensor(qT[:, h, :], gateT[:, h, :], qT[:, h, :], ALU.mult).then_inc(s_("gate_x"), 1)

            def gate_low(h):
                dve.wait_ge(s_("gate_high"), h + 1)
                dve.scalar_tensor_tensor(ghalves[1][:, h, :], qT[:, h, :], xsc[:, 1:2], ghalves[0][:, h, :], ALU.mult,
                                         ALU.subtract).then_inc(s_("gated"), 1)

            first_og = first_slot("og")
            for h in range(HEADS_H + 2):
                if h < HEADS_H:
                    hgrn_cumulate(h)
                if 1 <= h <= HEADS_H:
                    measure(first_og + h + 1)
                if h >= 2:
                    hgrn_out(h - 2)
                if h < HEADS_H:
                    hgrn_levels(h)
                    hgrn_masks(h)
                if h >= 3:
                    gate_low(h - 3)
                if h <= HEADS_H:
                    low(first_og + h + 1)
            measure(slot_at("wa", 2))
            gate_low(HEADS_H - 1)
            low(slot_at("wa", 2))
            for m in range(8):
                if m % 2 == 0:
                    before("wa", m // 2)
                dve.wait_ge(s_("wa_mm"), n_("wa_mm", m + 1))
                dve.wait_ge(s_("ga_ev"), n_("ga_ev", m + 1))
                dve.scalar_tensor_tensor(kT[:, m, :], ps[m][:, :], undo("wa", m // 2), kT[:, m, :], ALU.mult, ALU.mult).then_inc(dve_chain, 1)
                dve.wait_ge(dve_chain, own(dve_chain))
                dve.tensor_tensor(mixT[:, m, :], mixT[:, m, :], kT[:, m, :], ALU.add).then_inc(s_("wa_ev"), 1)
                dve.wait_ge(s_("wa_ev"), own(s_("wa_ev")))
                if m % 2 == 1:
                    after("wa", m // 2)
            norm_bound("ln1")
            dve.wait_ge(s_("x_again"), 16 * TT)
            add_and_norm("o1", SA, ALPHA, "ln1", None, None, SB, "up0")
            for i, (kind, b) in enumerate(MLP):
                split_behind = {1: 0, 2: 1, 4: 2, 6: 3}.get(i)
                if kind == "up":
                    if split_behind is not None:
                        hidden_scale(split_behind)
                    for m in range(8):
                        if m % 2 == 0:
                            before(f"up{b}", m // 2)
                        dve.wait_ge(s_(f"up{b}_ev"), n_(f"up{b}_ev", m + 1))
                        if m == 0 and b >= 2:
                            dve.wait_ge(s_(f"dn{b - 2}_mm"), n_(f"dn{b - 2}_mm", 16))
                        dve.tensor_tensor(hidden(b)[0][:, m, :], scr[:, m % 2, :], scr[:, m % 2, :], ALU.mult).then_inc(s_(f"hid{b}"), 1)
                        if m in (2, 3, 4, 5) and split_behind is not None:
                            hidden_low(split_behind, m - 2)
                        dve.wait_ge(s_(f"hid{b}"), m + 1)
                        dve.tensor_reduce(hmax[:, b % 2, m:m + 1], hidden(b)[0][:, m, :], AX_X, ALU.max).then_inc(s_("hid_rows"), 1)
                        if m % 2 == 1:
                            after(f"up{b}", m // 2)
                elif b < 3:
                    if b == 0:
                        dve.wait_ge(s_("res_scaled"), TT)
                    add_into(f"dn{b}", (SA, SB)[i % 2], split_behind)
            norm_bound("rms_e")
            add_and_norm("dn3", SB, 1.0, "ln2", "rms_e", normed, SA, "qf")

            def decayed(name, banks, o):
                for m in range(4):
                    if m % 2 == 0:
                        before(name, m // 2)
                    dve.wait_ge(s_(name + "_mm"), n_(name + "_mm", m + 1))
                    dve.scalar_tensor_tensor(slab[1][:, o + m, :], banks[m][:, :], undo(name, m // 2), slab[3][:, o + m, :],
                                             ALU.mult, ALU.mult).then_inc(s_(name + "_ev"), 1)
                    if m % 2 == 1:
                        after(name, m // 2)

            for key, slots in (("qf", 2), ("kf", 2), ("vf", 2), ("fl", 1)):
                for i in range(slots):
                    before(key, i)
                    after(key, i)
            dve.wait_ge(s_("decay_in"), 32)
            decayed("qr", SB, 0)
            decayed("kr", SA, 4)
            before("vr", 0)
            dve.wait_ge(s_("fl_ln"), 1)
            dve.memset(frow[3], 1.0).then_inc(dve_chain, 1)
            dve.wait_ge(dve_chain, own(dve_chain))
            dve.scalar_tensor_tensor(frow[2], frow[0], 0.0, frow[1], ALU.min, ALU.subtract).then_inc(dve_chain, 1)
            dve.wait_ge(dve_chain, own(dve_chain))
            dve.tensor_tensor_scan(frow[4], frow[3], frow[2], 0.0, ALU.mult, ALU.add).then_inc(s_("frow"), 1)
            dve.wait_ge(s_("frow"), own(s_("frow")))

            after("vr", 0)
            before("vr", 1)
            after("vr", 1)

            def silu(name, dst):
                for m in range(8):
                    if m % 2 == 0:
                        before(name, m // 2)
                    dve.wait_ge(s_(name + "_sg"), n_(name + "_sg", m + 1))
                    dve.scalar_tensor_tensor(dst[:, m, :], SA[m % 4][:, :], undo(name, m // 2), scr[:, m % 2, :], ALU.mult,
                                             ALU.mult).then_inc(s_(name + "_ev"), 1)
                    if m % 2 == 1:
                        after(name, m // 2)

            silu("ze", slab[5])

            def attention(A):
                n, steps, N = A.name, A.steps, len(A.steps)
                for i in range(N + 1):
                    if i < N:
                        h, b, t = steps[i]
                        w = (t + 1) * P
                        if n == "nsa" and b == 0 and t == 0:
                            dve.tensor_scalar(scr[:, 4 + h % 2, :], dist, SLOPE[h], None, ALU.mult).then_inc(dve_chain, 1)
                            dve.wait_ge(dve_chain, own(dve_chain))
                        dve.wait_ge(s_(n + "_sc"), i + 1)
                        if n == "fox":
                            dve.wait_ge(s_("fox_cb"), h + 1)
                            bias = scr[:, 4 + h % 2, 0:w]
                        else:
                            bias = scr[:, 4 + h % 2, SEQ - w:]
                        if i >= SCR_S:
                            dve.wait_ge(s_(n + "_tp"), i - SCR_S + 1)
                        dve.tensor_tensor_reduce(scr[:, i % SCR_S, 0:w], ps[i % 3][:, 0:w], bias, 1.0, 3e38, ALU.add,
                                                 ALU.min, tmin[:, i % 8:i % 8 + 1]).then_inc(s_(n + "_dm"), 1)
                    if i >= 1:
                        s = i - 1
                        h, b, t = steps[s]
                        w = (t + 1) * P
                        dve.wait_ge(s_(n + "_ex"), s + 1)
                        c = slice(s % 8, s % 8 + 1)
                        dve.reciprocal(trec[:, c], tsum[:, c]).then_inc(dve_chain, 1)
                        dve.wait_ge(dve_chain, own(dve_chain))
                        pr = scr[:, s % SCR_S, 0:w]
                        if n == "fox":
                            ins = dve.tensor_scalar(pr, pr, trec[:, c], None, ALU.mult)
                        else:
                            ins = dve.tensor_scalar(pr, pr, trec[:, c], gates[:, t, 3 * h + 1 + b:3 * h + 2 + b], ALU.mult, ALU.mult)
                        ins.then_inc(s_(n + "_pn"), 1)
                    per = 8 * A.branches
                    if i >= 8 and (i - 8) % per == per - 1:
                        pair_out(A, (i - 8) // per)
                pair_out(A, A.heads // 2 - 1)

            def pair_out(A, m):
                n = A.name
                dve.wait_ge(s_(n + "_pv"), 2 * A.branches * (m + 1))
                ob = OB[0 if n == "fox" else m % 2]
                dve.tensor_tensor(A.y(m), ob[:, :], slab[5][:, m, :], ALU.mult).then_inc(s_(n + "_y"), 1)
                dve.wait_ge(s_(n + "_y"), own(s_(n + "_y")))

            def retention_out(m):
                dve.wait_ge(s_("rt_mu"), m + 1)
                dve.tensor_tensor(scr[:, 1, :], scr[:, 0, :], SB[2][:, :], ALU.subtract).then_inc(s_("rt_cen"), 1)
                dve.wait_ge(s_("rt_rs"), m + 1)
                dve.reciprocal(scr[:, 3, :], scr[:, 3, :])
                dve.scalar_tensor_tensor(scr[:, 4, :], scr[:, 1, :], gng[:, m:m + 1], slab[5][:, 4 + m, :], ALU.mult,
                                         ALU.mult).then_inc(dve_chain, 1)
                dve.wait_ge(dve_chain, own(dve_chain))
                dve.tensor_tensor(slab[2][:, 4 + m, :], scr[:, 4, :], scr[:, 3, :], ALU.mult).then_inc(s_("yr"), 1)

            attention(FOX)
            for h in range(8):
                for j in range(TT):
                    dve.wait_ge(s_("rt_ea"), 4 * h + j + 1)
                    dve.tensor_tensor(pT(h)[:, j, j * P:(j + 1) * P], pT(h)[:, j, j * P:(j + 1) * P], tril[:, :], ALU.mult)\
                        .then_inc(s_("rt_ed"), 1)
                    dve.wait_ge(s_("rt_ed"), own(s_("rt_ed")))
                if h % 2 == 1 and h >= 3:
                    retention_out((h - 3) // 2)
            norm_bound("rms_o")
            retention_out(3)
            add_and_norm("oe", SA, 1.0, None, "rms_o", normed, SB, "kc")
            for key, slots in (("kc", 1), ("vc", 1), ("ck", 2)):
                for i in range(slots):
                    before(key, i)
                    after(key, i)

            for x in range(2):
                before("cv", x)
                after("cv", x)
                for m in range(2):
                    c = 2 * x + m
                    dve.wait_ge(s_("hid_sg"), c + 1)
                    dve.scalar_tensor_tensor(hid[x][:, m, :], (SA, SB)[x][m][:, 0:NG * NC], hbias[:, c:c + 1],
                                             hsig[:, 128 * c:128 * c + NG * NC], ALU.add, ALU.mult).then_inc(s_(("hid_k", "hid_v")[x]), 1)
                    dve.wait_ge(s_(("hid_k", "hid_v")[x]), own(s_(("hid_k", "hid_v")[x])))
            for key, slots in (("ks", 1), ("kw", 1), ("vs", 1), ("vw", 1)):
                for i in range(slots):
                    before(key, i)
                    after(key, i)
            before("gl")
            for t in range(TT):
                dve.wait_ge(s_("gl_mm"), n_("gl_mm", t + 1))
                dve.scalar_tensor_tensor(gates[:, t, :], SA[t][:, 0:48], undo("gl", 0), bgate[:, :], ALU.mult, ALU.add).then_inc(s_("gl_ev"), 1)
                dve.wait_ge(s_("gl_ev"), own(s_("gl_ev")))
            after("gl")
            for i in range(4):
                before("qo", i)
                after("qo", i)
            silu("zo", slab[5])

            dve.wait_ge(s_("gate"), TT)
            for g in range(NG):
                b = g % 2
                x3 = csc[b].rearrange("p (a n) -> p a n", n=NC)
                if g >= 2:
                    dve.wait_ge(s_("ct_mm"), 4 * (g - 1))
                dve.wait_ge(s_("cs_mm"), g + 1)
                for hg in range(4):
                    c = slice(hg * TT * NC, (hg + 1) * TT * NC)
                    dve.scalar_tensor_tensor(csc[b][:, c], cdist, SLOPE[4 * g + hg],
                                             SA[2 * b + hg % 2][:, hg // 2 * TT * NC:(hg // 2 + 1) * TT * NC], ALU.mult, ALU.add)\
                        .then_inc(s_("cs_ev"), 1)
                    dve.wait_ge(s_("cs_ev"), own(s_("cs_ev")))
                dve.wait_ge(s_("cs_ev"), 4 * g + 4)
                mn, sm, rc = csmall[:, 0, :], csmall[:, 1, :], csmall[:, 2, :]
                dve.tensor_reduce(mn, x3, AX_X, ALU.min).then_inc(dve_chain, 1)
                dve.wait_ge(dve_chain, own(dve_chain))
                dve.tensor_tensor(x3, x3, mn.unsqueeze(2).to_broadcast([P, 16, NC]), ALU.subtract).then_inc(s_("cs_d"), 1)
                dve.wait_ge(s_("cs_d"), own(s_("cs_d")))
                dve.wait_ge(s_("cs_e"), g + 1)
                dve.tensor_reduce(sm, x3, AX_X, ALU.add).then_inc(dve_chain, 1)
                dve.wait_ge(dve_chain, own(dve_chain))
                dve.reciprocal(rc, sm).then_inc(dve_chain, 1)
                dve.wait_ge(dve_chain, own(dve_chain))
                gt = gates[:, :, :].rearrange("p t (h b) -> p b h t", b=3)[:, 0, 4 * g:4 * g + 4, :]
                dve.tensor_tensor(rc.rearrange("p (h t) -> p h t", h=4), rc.rearrange("p (h t) -> p h t", h=4), gt, ALU.mult).then_inc(dve_chain, 1)
                dve.wait_ge(dve_chain, own(dve_chain))
                dve.tensor_tensor(x3, x3, rc.unsqueeze(2).to_broadcast([P, 16, NC]), ALU.mult).then_inc(dve_chain, 1)
                dve.wait_ge(dve_chain, own(dve_chain))
                x4 = csc[b].rearrange("p (h n) -> p h n", h=4)
                dve.tensor_tensor(x4, x4, cmask.unsqueeze(1).to_broadcast([P, 4, TT * NC]), ALU.mult).then_inc(s_("cs_p"), 1)
                dve.wait_ge(s_("cs_p"), own(s_("cs_p")))
            attention(NSA)
            add_and_norm("oo", SA, 1.0, None, "rms_f", res, None, None)


_INS = {
    "x": None, "w_in": None, "lb_logits": None, "hgrn_norm_g": None, "w_a": None, "w_pool": None, "pool_scale": None,
    "w_out": None, "ln1_g": None, "ln1_b": None, "w_up": None, "w_down": None, "ln2_g": None, "ln2_b": None,
    "even_norm_g_2": None, "even_w_in_2": None, "even_b_f_2": None, "even_gn_g_2": None, "even_w_out_2": None,
    "odd_norm_g_2": None, "odd_w_in_2": None, "odd_b_gate_2": None, "odd_pe_k_2": None, "odd_pe_v_2": None,
    "odd_wk1_2": None, "odd_wk2_2": None, "odd_wv1_2": None, "odd_wv2_2": None, "odd_w_out_2": None, "final_g_2": None,
}


def kernel(**inputs):
    import numpy as _np
    import concourse.bacc as _bacc
    from concourse import mybir as _mybir
    from concourse.bass_utils import run_bass_kernel_spmd as _run

    nc = _bacc.Bacc("TRN2", target_bir_lowering=False, num_devices=1)
    arrays, args = {}, {}
    for name in _INS:
        a = _np.ascontiguousarray(inputs[name])
        arrays[f"in_{name}"] = a
        args[name] = nc.dram_tensor(f"in_{name}", a.shape, _mybir.dt.from_np(a.dtype), kind="ExternalInput").ap()
    out = nc.dram_tensor("result", (1, SEQ, DM), F32, kind="ExternalOutput").ap()
    build(nc, args, out)
    r = _run(nc, [arrays], core_ids=[0])
    return r.results[0]["result"]
```
